# Optimizing a Trainium2 kernel written in Bass

```python
import jax, jax.numpy as jnp
from jax import lax
import numpy as np

D_MODEL = 1024
BATCH = 1
SEQ = 1024
DEPTH = 1

CHUNK = 64
RET_HEADS = 4
RET_DK = 128
RET_DV = 256
GLA_HEADS = 4
GLA_DK = 128
GLA_DV = 256
GLA_GATE_RANK = 16
GLA_GATE_TAU = 16.0
D_FF = 2816
ROPE_BASE = 10000.0
NORM_EPS = 1e-6
RET_QK = RET_HEADS * RET_DK
RET_V = RET_HEADS * RET_DV
GLA_QK = GLA_HEADS * GLA_DK
GLA_V = GLA_HEADS * GLA_DV
IN_SPLITS = (RET_QK, RET_QK, RET_V, RET_V, GLA_QK, GLA_QK, GLA_V, GLA_V, GLA_GATE_RANK, D_MODEL, D_MODEL)
D_IN = RET_QK * 2 + RET_V * 2 + GLA_QK * 2 + GLA_V * 2 + GLA_GATE_RANK + 2 * D_MODEL

kernel_name = "hybrid_retention_gla_macaron_block"

def _rmsnorm(x, w):
    xf = x.astype(jnp.float32)
    y = xf * lax.rsqrt(jnp.mean(xf * xf, axis=-1, keepdims=True) + NORM_EPS)
    return (y * w.astype(jnp.float32)).astype(x.dtype)

def _swiglu(x, w1, w3, w2):
    return (jax.nn.silu(x @ w1) * (x @ w3)) @ w2

def _split_columns(p):
    outs = []
    off = 0
    for width in IN_SPLITS:
        outs.append(p[..., off:off + width])
        off += width
    return outs

def _rotary(x, pos):
    half = x.shape[-1] // 2
    inv_freq = ROPE_BASE ** (-jnp.arange(half, dtype=jnp.float32) / half)
    ang = pos.astype(jnp.float32)[:, None] * inv_freq[None, :]
    cos = jnp.cos(ang)[:, None, :]
    sin = jnp.sin(ang)[:, None, :]
    x = x.astype(jnp.float32)
    x1, x2 = x[..., :half], x[..., half:]
    return jnp.concatenate([x1 * cos - x2 * sin, x2 * cos + x1 * sin], axis=-1)

def _to_chunks(t):
    b, s, h, d = t.shape
    return t.reshape(b, s // CHUNK, CHUNK, h, d).transpose(1, 0, 3, 2, 4)

def _from_chunks(t):
    n, b, h, c, d = t.shape
    return t.transpose(1, 0, 3, 2, 4).reshape(b, n * c, h, d)

def _retention_chunkwise(q, k, v):
    heads = jnp.arange(RET_HEADS, dtype=jnp.float32)
    log_gamma = jnp.log1p(-jnp.exp2(-5.0 - heads))
    idx = jnp.arange(CHUNK, dtype=jnp.float32)
    intra = jnp.exp(log_gamma[:, None, None] * jnp.abs(idx[:, None] - idx[None, :]))
    q_decay = jnp.exp(log_gamma[:, None] * (idx[None, :] + 1.0))[:, :, None]
    k_decay = jnp.exp(log_gamma[:, None] * (CHUNK - 1.0 - idx[None, :]))[:, :, None]
    chunk_decay = jnp.exp(log_gamma * CHUNK)[:, None, None]

    def step(state, inp):
        qc, kc, vc = inp
        scores = jnp.einsum('bhnd,bhmd->bhnm', qc, kc) * intra
        out = (jnp.einsum('bhnm,bhmv->bhnv', scores, vc)
               + jnp.einsum('bhnd,bhdv->bhnv', qc * q_decay, state))
        state = chunk_decay * state + jnp.einsum('bhmd,bhmv->bhdv', kc * k_decay, vc)
        return state, out

    b = q.shape[1]
    state0 = jnp.zeros((b, RET_HEADS, RET_DK, RET_DV), jnp.float32)
    _, out = lax.scan(step, state0, (q, k, v))
    return out

def _gla_chunkwise(q, k, v, log_alpha):

    def step(state, inp):
        qc, kc, vc, la = inp
        cum = jnp.cumsum(la, axis=-2)
        last = cum[..., -1:, :]
        pair = jnp.exp(-jnp.abs(cum[..., :, None, :] - cum[..., None, :, :]))
        scores = jnp.einsum('bhnmd,bhmd->bhnm', qc[..., :, None, :] * pair, kc)
        out = (jnp.einsum('bhnm,bhmv->bhnv', scores, vc)
               + jnp.einsum('bhnd,bhdv->bhnv', qc * jnp.exp(cum), state))
        state = (jnp.swapaxes(jnp.exp(last), -1, -2) * state
                 + jnp.einsum('bhmd,bhmv->bhdv', kc * jnp.exp(last - cum), vc))
        return state, out

    b = q.shape[1]
    state0 = jnp.zeros((b, GLA_HEADS, GLA_DK, GLA_DV), jnp.float32)
    _, out = lax.scan(step, state0, (q, k, v, log_alpha))
    return out

def setup_inputs(seed: int = 0) -> dict:
    key = jax.random.key(seed)
    ks = jax.random.split(key, 20)
    f32 = jnp.float32

    def nrm(k, shape, fan_in):
        return jax.random.normal(k, shape, f32) * (fan_in ** -0.5)

    def gain(k, shape):
        return 1.0 + 0.02 * jax.random.normal(k, shape, f32)

    return {
        "x": jax.random.normal(ks[0], (BATCH, SEQ, D_MODEL), f32),
        "norm_ffn1": gain(ks[1], (DEPTH, D_MODEL)),
        "ffn1_w1": nrm(ks[2], (DEPTH, D_MODEL, D_FF), D_MODEL),
        "ffn1_w3": nrm(ks[3], (DEPTH, D_MODEL, D_FF), D_MODEL),
        "ffn1_w2": nrm(ks[4], (DEPTH, D_FF, D_MODEL), D_FF),
        "norm_mix": gain(ks[5], (DEPTH, D_MODEL)),
        "w_in": nrm(ks[6], (DEPTH, D_MODEL, D_IN), D_MODEL),
        "gla_gate_w2": nrm(ks[7], (DEPTH, GLA_GATE_RANK, GLA_QK), GLA_GATE_RANK),
        "gla_gate_b": 0.1 * jax.random.normal(ks[8], (DEPTH, GLA_QK), f32),
        "gla_norm_w": gain(ks[9], (DEPTH, GLA_DV)),
        "w_branch_ret": nrm(ks[10], (DEPTH, RET_V, D_MODEL), RET_V),
        "w_branch_gla": nrm(ks[11], (DEPTH, GLA_V, D_MODEL), GLA_V),
        "w_out": nrm(ks[12], (DEPTH, D_MODEL, D_MODEL), D_MODEL),
        "norm_ffn2": gain(ks[13], (DEPTH, D_MODEL)),
        "ffn2_w1": nrm(ks[14], (DEPTH, D_MODEL, D_FF), D_MODEL),
        "ffn2_w3": nrm(ks[15], (DEPTH, D_MODEL, D_FF), D_MODEL),
        "ffn2_w2": nrm(ks[16], (DEPTH, D_FF, D_MODEL), D_FF),
        "norm_final": gain(ks[17], (D_MODEL,)),
    }

def reference(x, norm_ffn1, ffn1_w1, ffn1_w3, ffn1_w2, norm_mix, w_in, gla_gate_w2, gla_gate_b,
              gla_norm_w, w_branch_ret, w_branch_gla, w_out, norm_ffn2, ffn2_w1, ffn2_w3, ffn2_w2,
              norm_final):
    b, s, _ = x.shape
    pos = jnp.arange(s, dtype=jnp.int32)
    h = x
    for l in range(DEPTH):
        h = h + 0.5 * _swiglu(_rmsnorm(h, norm_ffn1[l]), ffn1_w1[l], ffn1_w3[l], ffn1_w2[l])

        u = _rmsnorm(h, norm_mix[l])
        qa, ka, va, ra, qb, kb, vb, rb, lr, ga, gb = _split_columns(u @ w_in[l])

        qa = _rotary(qa.reshape(b, s, RET_HEADS, RET_DK), pos) * (RET_DK ** -0.5)
        ka = _rotary(ka.reshape(b, s, RET_HEADS, RET_DK), pos)
        va = va.reshape(b, s, RET_HEADS, RET_DV).astype(jnp.float32)
        oa = _from_chunks(_retention_chunkwise(_to_chunks(qa), _to_chunks(ka), _to_chunks(va)))
        mu = jnp.mean(oa, axis=-1, keepdims=True)
        var = jnp.mean(jnp.square(oa - mu), axis=-1, keepdims=True)
        oa = ((oa - mu) * lax.rsqrt(var + NORM_EPS)).reshape(b, s, RET_V)
        oa = (jax.nn.silu(ra.astype(jnp.float32)) * oa).astype(h.dtype)
        y_ret = oa @ w_branch_ret[l]

        log_alpha = jax.nn.log_sigmoid((lr @ gla_gate_w2[l] + gla_gate_b[l]).astype(jnp.float32)) / GLA_GATE_TAU
        log_alpha = log_alpha.reshape(b, s, GLA_HEADS, GLA_DK)
        qb = qb.reshape(b, s, GLA_HEADS, GLA_DK).astype(jnp.float32) * (GLA_DK ** -0.5)
        kb = kb.reshape(b, s, GLA_HEADS, GLA_DK).astype(jnp.float32)
        vb = vb.reshape(b, s, GLA_HEADS, GLA_DV).astype(jnp.float32)
        ob = _from_chunks(_gla_chunkwise(_to_chunks(qb), _to_chunks(kb), _to_chunks(vb), _to_chunks(log_alpha)))
        ob = ob * lax.rsqrt(jnp.mean(ob * ob, axis=-1, keepdims=True) + NORM_EPS) * gla_norm_w[l].astype(jnp.float32)
        ob = (jax.nn.silu(rb.astype(jnp.float32)) * ob.reshape(b, s, GLA_V)).astype(h.dtype)
        y_gla = ob @ w_branch_gla[l]

        merged = jax.nn.sigmoid(ga) * y_ret + jax.nn.sigmoid(gb) * y_gla
        h = h + merged @ w_out[l]

        h = h + 0.5 * _swiglu(_rmsnorm(h, norm_ffn2[l]), ffn2_w1[l], ffn2_w3[l], ffn2_w2[l])
    return _rmsnorm(h, norm_final)


_drawn_inputs = setup_inputs


def setup_inputs(seed=0):
    import zlib

    import numpy as np

    out = dict(_drawn_inputs(seed))
    spreads = {}
    factors = {'norm_ffn1': 5.061,
     'norm_mix': 3.096,
     'gla_gate_b': 4.885,
     'gla_norm_w': 22.609,
     'norm_ffn2': 26.998,
     'norm_final': 23.773}
    for name, (base, spread) in spreads.items():
        noise = np.random.default_rng([zlib.crc32(name.encode()), seed]).standard_normal(out[name].shape)
        drawn = base * np.exp(spread * noise) if base else spread * noise
        out[name] = __import__('jax').numpy.asarray(drawn.astype(out[name].dtype))
    for name, factor in factors.items():
        out[name] = (out[name] * factor).astype(out[name].dtype)
    return out
```

```python
from contextlib import ExitStack

import numpy as np

import concourse.bass as bass
from concourse import mybir

F32 = mybir.dt.float32
F32R = mybir.dt.float32r
U8 = mybir.dt.uint8
ALU = mybir.AluOpType
ACT = mybir.ActivationFunctionType

P = 128
T = 1024
D = 1024
KT = D // P
HF = 512
FF = 2816
FFG = FF // (2 * P)
HEADS = 4
DK = 128
DV = 256
BLK = 128
NBH = HF // BLK
CHUNK = 64
EPS = 1e-6
TAU = 16.0
QK_SCALE = DK ** -0.5
ROPE_BASE = 10000.0

RAW = 4
FFN_TILES = 6 * FFG
BRANCH_TILES = 8 * HEADS
N_F1 = 0
N_RET = N_F1 + FFN_TILES
N_GA = N_RET + BRANCH_TILES
N_LR = N_GA + KT
N_GLA = N_LR + 1
N_GB = N_GLA + BRANCH_TILES
N_OUT = N_GB + KT
N_F2 = N_OUT + KT
N_TILES = N_F2 + FFN_TILES

Q, K, V0, V1, B0, B1, R0, R1 = range(8)
STEPS = 64
LEVELS = (64, 32, 16, 8, 4, 2, 1)
NLV = len(LEVELS)
LAST, DIAG = NLV, NLV + 1


def score_step(half, item):
    return (18 if half == 0 else 36) + 2 * item


def block_step(half, b):
    return (36 if half == 0 else 54) + 2 * b


def wait(eng, sem, value):
    if isinstance(value, int) and value <= 0:
        return
    eng.wait_ge(sem, value)


def decay_tables():
    f = np.float32
    half = DK // 2
    inv = (f(ROPE_BASE) ** (-np.arange(half, dtype=f) / f(half))).astype(f)
    ang = (np.arange(T, dtype=f)[:, None] * inv[None, :]).astype(f).T.astype(np.float64)
    cos, sin = np.cos(ang), np.sin(ang)
    rope = np.stack([np.concatenate([cos, cos]), np.concatenate([sin, -sin])], 1).astype(f)
    lg = np.log1p(-np.exp2(-5.0 - np.arange(HEADS)))
    i = np.arange(BLK)
    m, n = i[:, None], i[None, :]
    seen = (m // CHUNK) <= (n // CHUNK)
    intra = np.where(seen, np.exp(lg[:, None, None] * np.abs(m - n)), 0.0) * QK_SCALE
    qdec = np.broadcast_to((np.exp(lg[:, None] * (i + 1.0)) * QK_SCALE)[:, None, :], (HEADS, P, BLK))
    kdec = np.exp(lg[:, None] * (BLK - 1.0 - i))[:, :, None]
    bdec = np.broadcast_to(np.exp(lg * BLK)[:, None, None], (HEADS, P, 1))
    ret = np.concatenate([intra, qdec, kdec, bdec], 2).transpose(1, 0, 2).astype(f)
    masks = [(m < 64) & (n >= 64)]
    for s in LEVELS[1:]:
        masks.append((m // (2 * s) == n // (2 * s)) & (m // s != n // s))
    masks.append(m == n)
    masks = np.stack(masks, 1)
    first = masks[:, 0].astype(f)
    small = np.concatenate([np.eye(P), np.full((P, P), 1.0 / D), first, np.ones((P, P)),
                            np.full((P, 1), EPS)], 1).astype(f)
    return rope, ret, np.ascontiguousarray(masks.astype(f)), small


RETC = 2 * BLK + 2
SMALLC = 4 * P + 1


class NormSignals:

    def __init__(self, sem, stage):
        self.sq_done = sem(f"{stage}_sq_done")
        self.sum_done = sem(f"{stage}_sum_done")
        self.mean_done = sem(f"{stage}_mean_done")
        self.root_done = sem(f"{stage}_root_done")
        self.inv_done = sem(f"{stage}_inv_done")
        self.u_done = sem(f"{stage}_u_done")
        self.uh_done = sem(f"{stage}_uh_done")
        self.ul_done = sem(f"{stage}_ul_done")


class FfnSignals:

    def __init__(self, sem, stage):
        self.a_done = sem(f"{stage}_a_done")
        self.b_done = sem(f"{stage}_b_done")
        self.p2_done = sem(f"{stage}_p2_done")
        self.silu_done = sem(f"{stage}_silu_done")
        self.gate_done = sem(f"{stage}_gate_done")
        self.hh_done = sem(f"{stage}_hh_done")
        self.hl_done = sem(f"{stage}_hl_done")
        self.acc_done = sem(f"{stage}_acc_done")


class BranchSignals:

    def __init__(self, sem, stage):
        self.q_half = sem(f"{stage}_q_half")
        self.k_half = sem(f"{stage}_k_half")
        self.v_half = sem(f"{stage}_v_half")
        self.r_half = sem(f"{stage}_r_half")
        self.b_part = sem(f"{stage}_b_part")
        self.q_ev = sem(f"{stage}_q_ev")
        self.k_ev = sem(f"{stage}_k_ev")
        self.v_ev = sem(f"{stage}_v_ev")
        self.vt_done = sem(f"{stage}_vt_done")
        self.vt_ev = sem(f"{stage}_vt_ev")
        self.r_ev = sem(f"{stage}_r_ev")
        self.b_ev = sem(f"{stage}_b_ev")
        self.ot_done = sem(f"{stage}_ot_done")
        self.g_done = sem(f"{stage}_g_done")
        self.oh_done = sem(f"{stage}_oh_done")
        self.ol_done = sem(f"{stage}_ol_done")
        self.sc_done = sem(f"{stage}_sc_done")
        self.sc_ev = sem(f"{stage}_sc_ev")
        self.kt_done = sem(f"{stage}_kt_done")
        self.kt_ev = sem(f"{stage}_kt_ev")
        self.qd_done = sem(f"{stage}_qd_done")
        self.o_done = sem(f"{stage}_o_done")
        self.o_ev = sem(f"{stage}_o_ev")
        self.st_done = sem(f"{stage}_st_done")
        self.st_ev = sem(f"{stage}_st_ev")
        self.var_done = sem(f"{stage}_var_done")
        self.sd_done = sem(f"{stage}_sd_done")
        self.on_done = sem(f"{stage}_on_done")
        self.chain = sem(f"{stage}_chain")
        self.headc_done = sem(f"{stage}_headc_done")
        self.y_clear = sem(f"{stage}_y_clear")


def block_kernel(nc, xT, wts, norms, gate_w2, gate_b, rope, ret, masks, small, out, h_spill, y_spill):
    ctx = ExitStack()
    with ctx:
        def sb(name, shape, dt=F32, scope=ctx):
            return scope.enter_context(nc.sbuf_tensor(name, shape, dt))

        def sem(name):
            return ctx.enter_context(nc.semaphore(name))

        uH = sb("uH", [P, KT, T], F32R)
        uL = sb("uL", [P, KT, T], F32R)
        raw = [sb(f"raw{i}", [P, D]) for i in range(RAW)]
        wH = [sb(f"wH{i}", [P, D], F32R) for i in range(2)]
        wL = [sb(f"wL{i}", [P, D], F32R) for i in range(2)]
        smallt = sb("smallt", [P, SMALLC])
        ident, mean_of, mask0 = (smallt[:, i * P:(i + 1) * P] for i in range(3))
        ones = smallt[:, 3 * P:4 * P]
        eps = smallt[:, 4 * P:4 * P + 1]
        normw = sb("normw", [P, 4 * KT + 2])
        gbt = sb("gbt", [P, HEADS])
        rett = sb("rett", [P, HEADS, RETC])
        maskt = sb("maskt", [P, NLV + 1, BLK], U8)
        w2t = sb("w2t", [16, HEADS * DK])
        w2h = sb("w2h", [16, DK])
        headc = sb("headc", [P, 4])
        carrier = sb("carrier", [P, 1])
        bst = sb("bst", [P, NBH, 6])
        mv = sb("mv", [P, NBH, 2])
        ve = sb("ve", [P, NBH])
        sd = sb("sd", [P, NBH])
        rs = sb("rs", [P, NBH])
        bdec = sb("bdec", [P, 2, NBH])

        with ExitStack() as f:
            h = sb("h", [P, KT, T], scope=f)
            hidH = sb("hidH", [P, 2, 2, T], F32R, scope=f)
            hidL = sb("hidL", [P, 2, 2, T], F32R, scope=f)
            sq = sb("sq", [P, 2, HF], scope=f)
            ssum = sb("ssum", [P, 2, HF], scope=f)
            rinv = sb("rinv", [P, 2, HF], scope=f)
            uf = sb("uf", [P, 2, HF], scope=f)
            sil = sb("sil", [P, 2, HF], scope=f)
            hidf = sb("hidf", [P, 2, HF], scope=f)
        m = ctx.enter_context(ExitStack())
        ogH = sb("ogH", [P, 2, T], F32R, scope=m)
        ogL = sb("ogL", [P, 2, T], F32R, scope=m)
        rS = sb("rS", [P, 2, T], scope=m)
        on = sb("on", [P, 2 * NBH, DV], scope=m)
        y = sb("y", [P, KT, T], scope=m)
        ogf = sb("ogf", [P, 2, HF], scope=m)
        ss = sb("ss", [P, 2, NBH, BLK], scope=m)
        qd = sb("qd", [P, NBH, BLK], scope=m)
        ktok = sb("ktok", [P, NBH, DK], scope=m)
        state = sb("state", [P, 2, DV], scope=m)
        vS = ogf
        qT = sb("qT", [P, T], scope=m)
        kT = sb("kT", [P, T], scope=m)
        vtok = sb("vtok", [P, 2 * NBH, DV], scope=m)
        with ExitStack() as r:
            ropet = sb("ropet", [P, 2, T], scope=r)
            rtmp = sb("rtmp", [P, 2, HF], scope=r)
        bc = sb("bc", [P, T], scope=m)
        lrT = sb("lrT", [16, T], scope=m)
        ee = sb("ee", [P, 2, HF], scope=m)
        qE = sb("qE", [P, 2, HF], scope=m)
        kE = sb("kE", [P, 2, HF], scope=m)

        ps = ctx.enter_context(nc.psum_tensor("ps", [P, 8, HF], F32))

        const_in = sem("const_in")
        rope_in = sem("rope_in")
        masks_done = sem("masks_done")
        raw_in = [sem(f"raw_in{i}") for i in range(RAW)]
        w_high = sem("w_high")
        w_ready = sem("w_ready")
        w_used = sem("w_used")
        h_in = [sem(f"h_in{i}") for i in range(KT)]
        h_saved = sem("h_saved")
        y_saved = sem("y_saved")
        y_back = [sem(f"y_back{i}") for i in range(2)]
        out_saved = sem("out_saved")

        norm1, norm2, norm3, norm4 = (NormSignals(sem, f"norm{i}") for i in range(1, 5))
        f1, f2 = FfnSignals(sem, "f1"), FfnSignals(sem, "f2")
        ret_s, gla_s = BranchSignals(sem, "ret"), BranchSignals(sem, "gla")
        z_done, zabs_done, zmin_done, zexp_done, zln_done, cum_done = (
            sem(x) for x in ("z_done", "zabs_done", "zmin_done", "zexp_done", "zln_done", "cum_done"))
        diff_done, exp_done, prod_done = (sem(x) for x in ("diff_done", "exp_done", "prod_done"))
        lr_half, lr_ev = sem("lr_half"), sem("lr_ev")
        ga_half, ga_sig, ga_ev = (sem(f"ga_{x}") for x in ("half", "sig", "ev"))
        gb_half, gb_sig, gb_mul, gb_ev = (sem(f"gb_{x}") for x in ("half", "sig", "mul", "ev"))
        mh_done, ml_done = sem("mh_done"), sem("ml_done")
        wo_half, wo_ev = sem("wo_half"), sem("wo_ev")

        def tok(half):
            return slice(half * HF, (half + 1) * HF)

        def carry():
            nc.vector.memset(carrier[:], 0.0)

        block = ctx.enter_context(nc.Block())

        @block.sync
        def _(sp):
            def load(n, slot, round_):
                wait(sp, w_ready, n - RAW + 1)
                sp.dma_start(raw[slot][:], wts[bass.ds(n, 1)].rearrange("a p c -> p (a c)")
                             ).then_inc(raw_in[slot], 16)

            for n in range(RAW):
                load(n, n, 0)
            with sp.Fori(1, N_TILES // RAW) as i:
                for s in range(RAW):
                    load(i * RAW + s, s, i)
            for n in range(N_TILES // RAW * RAW, N_TILES):
                load(n, n % RAW, n // RAW)

        @block.gpsimd
        def _(pool):
            def cut(n, s, round_):
                slot = s % 2
                pool.wait_ge(raw_in[s], 16 * round_ + 16)
                wait(pool, w_used, n - 1)
                nc.gpsimd.tensor_tensor(wH[slot][:], raw[s][:], ones[:, 0:1].to_broadcast([P, D]),
                                        ALU.mult).then_inc(w_high, 1)
                pool.wait_ge(w_high, n + 1)
                nc.gpsimd.tensor_tensor(wL[slot][:], raw[s][:], wH[slot][:].bitcast(F32), ALU.subtract
                                        ).then_inc(w_ready, 1)

            pool.wait_ge(const_in, 16 * 6)
            for n in range(RAW):
                cut(n, n, 0)
            with pool.Fori(1, N_TILES // RAW) as i:
                for s in range(RAW):
                    cut(i * RAW + s, s, i)
            for n in range(N_TILES // RAW * RAW, N_TILES):
                cut(n, n % RAW, n // RAW)

        @block.tensor
        def _(pe):
            mm = nc.tensor.matmul

            def triple(bank, wh, wl, xh, xl, start, stop):
                mm(bank, wh, xh, start=start, stop=False)
                mm(bank, wh, xl, start=False, stop=False)
                return mm(bank, wl, xh, start=False, stop=stop)

            def cols_part(slot, bank, half, k0, k1):
                for k in range(k0, k1):
                    last = triple(ps[:, bank, :], wH[slot][:, k * P:(k + 1) * P],
                                  wL[slot][:, k * P:(k + 1) * P], uH[:, k, tok(half)],
                                  uL[:, k, tok(half)], k == 0, k == KT - 1)
                return last

            def rows_unit(slot, bank, fl, xh, xl, half):
                for k in range(2):
                    w = slice(k * 4 * P + fl * P, k * 4 * P + (fl + 1) * P)
                    last = triple(ps[:, bank, :], wH[slot][:, w], wL[slot][:, w],
                                  xh[:, k, tok(half)], xl[:, k, tok(half)], k == 0, k == 1)
                return last

            def norm(nm):
                for t in range(2):
                    pe.wait_ge(nm.sum_done, (KT - 1) * (t + 1))
                    mm(ps[:, t, :], mean_of, ssum[:, t, :], start=True, stop=True
                       ).then_inc(nm.mean_done, 1)

            def ffn(s, n0, nm):
                def tile_no(i, j):
                    return n0 + 4 + 6 * (i - 1) + j if not isinstance(i, int) or i > 0 else n0 + j

                def p1(i, first=False, second=False):
                    for j in range(2):
                        for side in range(2):
                            n = tile_no(i, 2 * j + side)
                            slot = (n0 + side) % 2
                            pe.wait_ge(w_ready, n + 1)
                            for t in range(2):
                                u = 4 * j + 2 * side + t
                                if second:
                                    pe.wait_ge(s.gate_done if side else s.silu_done, 2 * j + t + 1)
                                elif not first:
                                    pe.wait_ge(s.acc_done, 16 * (i - 2) + 8 + u + 1)
                                if first and j == 0 and side == 0:
                                    for k in range(KT):
                                        pe.wait_ge(nm.ul_done, KT * t + k + 1)
                                        last = cols_part(slot, u, t, k, k + 1)
                                else:
                                    last = cols_part(slot, u, t, 0, KT)
                                if t == 0:
                                    last.then_inc(s.b_done if side else s.a_done, 1)
                                else:
                                    last.then_inc(w_used, 1)

                def p2(g, par, n, i=None):
                    pe.wait_ge(s.hl_done, 4 * (g + 1))
                    for v in range(16):
                        c, t, fl = v // 8, v % 8 // 4, v % 4
                        if v % 8 == 0:
                            pe.wait_ge(w_ready, n + c + 1)
                        if v < 8 and i is not None:
                            idx = 4 * i + 2 * (v // 4) + v % 2 + 1
                            pe.wait_ge(s.gate_done if v % 4 // 2 else s.silu_done, idx)
                        elif v < 8:
                            pe.wait_ge(s.acc_done, 16 * (g - 1) + 8 + v + 1)
                        else:
                            pe.wait_ge(s.acc_done, 16 * g + v - 8 + 1)
                        last = rows_unit((n0 + c) % 2, v % 8, fl, hidH[:, par], hidL[:, par], t)
                        last.then_inc(w_used if v % 8 == 7 else s.p2_done, 1)

                p1(0, first=True)
                p1(1, second=True)
                p2(0, 0, tile_no(1, 4), 1)
                with pe.Fori(1, FFG // 2) as c:
                    for par in range(2):
                        i = c * 2 + par
                        p1(i)
                        p2(i - 1, 1 - par, tile_no(i, 4), i)
                i = FFG - 1
                p1(i)
                p2(i - 1, (i - 1) % 2, tile_no(i, 4), i)
                p2(i, i % 2, tile_no(i, 4) + 2)

            def out_transposes(s, hp, half):
                pe.wait_ge(s.on_done, 2 * hp + half + 1)
                for d in range(2):
                    if half == 0:
                        pe.wait_ge(s.st_ev if d else s.o_ev, (7 if d else 8) * (hp + 1))
                    else:
                        pe.wait_ge(s.g_done, 4 * hp + d + 1)
                    for b in range(NBH):
                        last = nc.tensor.transpose(ps[:, 6 + d, b * BLK:(b + 1) * BLK],
                                                   on[:, half * NBH + b, d * P:(d + 1) * P], ident)
                    last.then_inc(s.ot_done, 1)

            def branch_unit(s, hp, n0, slot, v, n_tile, tail=False):
                c, t, fl = v // 8, v % 8 // 4, v % 4
                if v % 8 == 0:
                    pe.wait_ge(w_ready, n_tile + 1)
                if v == 0:
                    pe.wait_ge(s.ol_done, 4 * (hp + 1))
                if v < 4:
                    if tail:
                        pe.wait_ge(s.r_ev, 4 * HEADS - 3 + v)
                    else:
                        pe.wait_ge(s.v_ev, 4 * (hp + 1) + v + 1)
                else:
                    pe.wait_ge(s.b_ev, 16 * hp + v - 4 + 1)
                last = rows_unit(slot, v % 4, fl, ogH, ogL, t)
                last.then_inc(w_used if v % 8 == 7 else s.b_part, 1)

            def branch(s, n0, gla, ul):
                items = NLV + 2 if gla else 2
                n_sc = NLV + 1 if gla else 1

                def window(hd, first):
                    nw = n0 if first else n0 + 6 + 8 * (hd - 1)
                    for step in range(STEPS):
                        tile, e = step // 8, step % 8
                        if tile in (B0, B1):
                            if not first:
                                branch_unit(s, hd - 1, n0, (n0 + tile) % 2, step - 8 * B0,
                                            nw + tile)
                        else:
                            n = nw + tile - (2 if first and tile > B1 else 0)
                            slot = (n0 + tile) % 2
                            t, q4 = e // 4, e % 4
                            if e == 0:
                                pe.wait_ge(w_ready, n + 1)
                            bank = 2 * (tile % 2) + t
                            if q4 == 0:
                                if tile in (Q, K):
                                    wait(pe, s.r_ev, 4 * hd - 3 + bank if not first else 0)
                                elif tile == V0:
                                    pe.wait_ge(s.q_ev, 2 * hd + t + 1)
                                elif tile == V1:
                                    pe.wait_ge(s.k_ev, 2 * hd + t + 1)
                                elif first:
                                    pe.wait_ge(s.v_ev, bank + 1)
                                else:
                                    pe.wait_ge(s.b_ev, 16 * (hd - 1) + 12 + bank + 1)
                            if first and tile == Q and ul is not None:
                                for k in range(2 * q4, 2 * q4 + 2):
                                    pe.wait_ge(ul, KT * t + k + 1)
                                    last = cols_part(slot, bank, t, k, k + 1)
                            else:
                                last = cols_part(slot, bank, t, 2 * q4, 2 * q4 + 2)
                            if e == 3:
                                sm = {Q: s.q_half, K: s.k_half, V0: s.v_half, V1: s.v_half,
                                      R0: s.r_half, R1: s.r_half}[tile]
                                last.then_inc(sm, 1)
                            elif e == 7:
                                last.then_inc(w_used, 1)
                        if gla and step == 1:
                            pe.wait_ge(s.headc_done, hd + 1)
                            pe.wait_ge(lr_ev, 2)
                            wait(pe, s.sc_ev, 16 * hd)
                            wait(pe, s.kt_ev, 2 * hd)
                            for t in range(2):
                                mm(ps[:, 4 + t, :], w2h[:], lrT[:, tok(t)], start=True, stop=True
                                   ).then_inc(z_done, 1)
                        if step in (3, 11) and not first:
                            out_transposes(s, hd - 1, step // 8)
                        if step in (22, 26, 30, 34):
                            v = (step - 22) // 4
                            pe.wait_ge(s.v_ev, 4 * hd + v + 1)
                            if v < 2:
                                wait(pe, s.g_done, 4 * hd - 2 + v + 1 if not first else 0)
                            else:
                                pe.wait_ge(s.vt_ev, 4 * hd + v - 2 + 1)
                            for b in range(NBH):
                                last = nc.tensor.transpose(ps[:, 6 + v % 2, b * BLK:(b + 1) * BLK],
                                                           vS[:, v % 2, b * BLK:(b + 1) * BLK], ident)
                            last.then_inc(s.vt_done, 1)
                        for half in range(2):
                            for item in range(NLV + 2):
                                if step == score_step(half, item):
                                    scores(hd, half, item)
                            for b in range(NBH):
                                if step == block_step(half, b):
                                    block_out(hd, half * NBH + b)

                def scores(hd, half, item):
                    if not gla and item not in (LAST, DIAG):
                        return
                    g = half * (NLV + 2) + item
                    bank = 4 + g % 2
                    sc0 = 2 * n_sc * hd + n_sc * half
                    if gla:
                        if item == DIAG:
                            pe.wait_ge(s.sc_ev, sc0 + NLV)
                        elif g == 0:
                            pe.wait_ge(zln_done, 2 * hd + 2)
                            pe.wait_ge(zmin_done, 2 * hd + 2)
                        elif g == 1:
                            pass
                        elif item == 0:
                            pe.wait_ge(s.kt_ev, 2 * hd + half)
                        elif item == 1:
                            pe.wait_ge(s.sc_ev, sc0)
                        else:
                            pe.wait_ge(s.sc_ev, sc0 + item - 1)
                    else:
                        wait(pe, s.kt_ev, 2 * hd + half)
                        wait(pe, s.sc_ev, sc0)
                    if item < NLV or item == LAST:
                        if gla:
                            pe.wait_ge(prod_done, 2 * (NLV + 2) * hd + g + 1)
                        else:
                            pe.wait_ge(s.k_ev, 2 * hd + half + 1)
                    if item == DIAG:
                        pe.wait_ge(s.q_ev, 2 * hd + half + 1)
                        pe.wait_ge(s.k_ev, 2 * hd + half + 1)
                    for b in range(NBH):
                        blk = slice(b * BLK, (b + 1) * BLK)
                        tb = slice(half * HF + b * BLK, half * HF + (b + 1) * BLK)
                        if item == LAST:
                            src = kE[:, item % 2, blk] if gla else kT[:, tb]
                            last = nc.tensor.transpose(ps[:, bank, blk], src, ident)
                        elif item == DIAG:
                            last = mm(ps[:, bank, blk], kT[:, tb], qT[:, tb], start=True, stop=True)
                        else:
                            last = mm(ps[:, bank, blk], kE[:, item % 2, blk], qE[:, item % 2, blk],
                                      start=True, stop=True)
                    last.then_inc(s.kt_done if item == LAST else s.sc_done, 1)

                def block_out(hd, b):
                    half, bb = b // NBH, b % NBH
                    hb = slice(b % 2 * DV, (b % 2 + 1) * DV)
                    o, st = ps[:, 6, hb], ps[:, 7, hb]
                    if bb == 0:
                        pe.wait_ge(s.sc_ev, 2 * n_sc * hd + n_sc * (half + 1))
                        pe.wait_ge(s.kt_ev, 2 * hd + half + 1)
                        if gla:
                            pe.wait_ge(prod_done, (NLV + 2) * (2 * hd + half + 1))
                        else:
                            pe.wait_ge(s.qd_done, 2 * hd + half + 1)
                    if b == 0:
                        pe.wait_ge(s.vt_ev, 4 * hd + 4)
                    if b >= 1:
                        pe.wait_ge(s.o_ev, 8 * hd + b)
                    mm(o, ss[:, half, bb, :], vtok[:, b, :], start=True, stop=False)
                    if b > 0:
                        pe.wait_ge(s.st_ev, 7 * hd + b)
                    mm(o, qd[:, bb, :], state[:, b % 2, :], start=False, stop=True
                       ).then_inc(s.o_done, 1)
                    if b < 2 * NBH - 1:
                        mm(st, ktok[:, bb, :], vtok[:, b, :], start=True, stop=True
                           ).then_inc(s.st_done, 1)

                if gla:
                    pe.wait_ge(lr_ev, 2)
                window(0, True)
                with pe.Fori(1, HEADS) as hd:
                    window(hd, False)

            def branch_tail(s, n0):
                hp = HEADS - 1
                nb = n0 + 6 + 8 * hp
                out_transposes(s, hp, 0)
                out_transposes(s, hp, 1)
                for v in range(16):
                    branch_unit(s, hp, n0, (n0 + v // 8) % 2, v, nb + v // 8, tail=True)

            def cols_tile(n, half_done, free, unit0):
                pe.wait_ge(w_ready, n + 1)
                for t in range(2):
                    free(t)
                    last = cols_part(n % 2, unit0 + t, t, 0, KT)
                    last.then_inc(w_used if t else half_done, 1)

            pe.wait_ge(const_in, 16 * 6)
            norm(norm1)
            ffn(f1, N_F1, norm1)
            norm(norm2)
            branch(ret_s, N_RET, False, norm2.ul_done)
            branch_tail(ret_s, N_RET)
            for f in range(KT):
                b0 = 2 * (f % 2)
                cols_tile(N_GA + f, ga_half,
                          lambda t: pe.wait_ge(ga_sig, 2 * f - 3 + t) if f >= 2 else
                          pe.wait_ge(ret_s.b_ev, 16 * HEADS - 4 + b0 + t + 1), b0)
            cols_tile(N_LR, lr_half, lambda t: pe.wait_ge(ga_sig, 2 * KT - 3 + t), 0)
            branch(gla_s, N_GLA, True, None)
            branch_tail(gla_s, N_GLA)
            for f in range(KT):
                b0 = 2 * (f % 2)
                cols_tile(N_GB + f, gb_half,
                          lambda t: pe.wait_ge(gb_sig, 2 * f - 3 + t) if f >= 2 else
                          pe.wait_ge(gla_s.b_ev, 16 * HEADS - 4 + b0 + t + 1), b0)
            for f in range(KT):
                b0 = 2 * (f % 2)

                def free(t):
                    if f == 0:
                        pe.wait_ge(ml_done, KT * (t + 1))
                    pe.wait_ge(*((wo_ev, 2 * f - 3 + t) if f >= 2 else (gb_sig, 2 * KT - 3 + b0 + t)))
                cols_tile(N_OUT + f, wo_half, free, b0)
            norm(norm3)
            ffn(f2, N_F2, norm3)
            norm(norm4)

        @block.scalar
        def _(act):
            A = nc.scalar.activation

            def after_ffn(s):
                return lambda e, f, t: e.wait_ge(
                    s.acc_done, 16 * (FFG - 1) + 8 * (f // 4) + 4 * t + f % 4 + 1)

            def norm(nm, ready, cut):
                for t in range(2):
                    for f in range(KT):
                        idx = KT * t + f
                        ready(act, f, t)
                        wait(act, nm.sum_done, (KT - 1) * t + max(1, f - 2) if f >= 2 else
                             (KT - 1) * t)
                        A(sq[:, f % 2, :], h[:, f, tok(t)], ACT.Square).then_inc(nm.sq_done, 1)
                    act.wait_ge(nm.mean_done, t + 1)
                    A(rinv[:, t, :], ps[:, t, :], ACT.Sqrt, bias=eps).then_inc(nm.root_done, 1)
                    if cut:
                        for f in range(KT):
                            act.wait_ge(nm.u_done, KT * t + f + 1)
                            A(uH[:, f, tok(t)], uf[:, f % 2, :], ACT.Copy).then_inc(nm.uh_done, 1)

            def ffn(s, n0):
                def p1(i, par, first=False, second=False):
                    for j in range(2):
                        n = n0 + 2 * j if first else n0 + 4 + 6 * (i - 1) + 2 * j
                        for t in range(2):
                            idx = 4 * i + 2 * j + t
                            if t == 0:
                                act.wait_ge(s.a_done, 2 * i + j + 1)
                            else:
                                act.wait_ge(w_used, n + 1)
                            wait(act, s.gate_done, idx - 1 if not first else 2 * j + t - 1)
                            A(sil[:, t, :], ps[:, 4 * j + t, :], ACT.Silu).then_inc(s.silu_done, 1)
                        for t in range(2):
                            idx = 4 * i + 2 * j + t
                            act.wait_ge(s.gate_done, idx + 1)
                            if not first and not second and j == 0 and t == 0:
                                act.wait_ge(w_used, n0 + 4 + 6 * (i - 1))
                            A(hidH[:, par, j, tok(t)], hidf[:, t, :], ACT.Copy).then_inc(s.hh_done, 1)

                p1(0, 0, first=True)
                p1(1, 1, second=True)
                with act.Fori(1, FFG // 2) as c:
                    for par in range(2):
                        p1(c * 2 + par, par)
                p1(FFG - 1, (FFG - 1) % 2)

            def gate_high(s, hp, half, n_before):
                for d in range(2):
                    act.wait_ge(s.g_done, 4 * hp + 2 * half + d + 1)
                    if half == 0 and d == 0:
                        act.wait_ge(w_used, n_before)
                    A(ogH[:, d, tok(half)], ogf[:, d, :], ACT.Copy).then_inc(s.oh_done, 1)

            def branch(s, n0, gla):
                def window(hd, first):
                    nw = n0 if first else n0 + 6 + 8 * (hd - 1)

                    def ready(tile, t, half_sem, count):
                        if t == 0:
                            act.wait_ge(half_sem, count)
                        else:
                            act.wait_ge(w_used, nw + tile - (2 if first and tile > B1 else 0) + 1)

                    for step in range(STEPS + 1):
                        if gla and step in (4, 8):
                            t = step // 4 - 1
                            ready(Q, t, s.q_half, hd + 1)
                            wait(act, s.o_done, 8 * hd)
                            A(qT[:, tok(t)], ps[:, t, :], ACT.Copy, scale=QK_SCALE
                              ).then_inc(s.q_ev, 1)
                        if gla and step in (12, 16):
                            t = step // 4 - 3
                            ready(K, t, s.k_half, hd + 1)
                            A(kT[:, tok(t)], ps[:, 2 + t, :], ACT.Copy).then_inc(s.k_ev, 1)
                        if gla and step == 2:
                            act.wait_ge(s.headc_done, hd + 1)
                            for t in range(2):
                                act.wait_ge(z_done, 2 * hd + t + 1)
                                wait(act, prod_done, 2 * (NLV + 2) * hd)
                                A(ee[:, t, :], ps[:, 4 + t, :], ACT.Abs, bias=headc[:, 2:3]
                                  ).then_inc(zabs_done, 1)
                            for t in range(2):
                                act.wait_ge(zabs_done, 2 * hd + t + 1)
                                A(ee[:, t, :], ee[:, t, :], ACT.Exp, scale=-1.0).then_inc(zexp_done, 1)
                            for t in range(2):
                                act.wait_ge(zexp_done, 2 * hd + t + 1)
                                A(ee[:, t, :], ee[:, t, :], ACT.Ln, bias=ones[:, 0:1]
                                  ).then_inc(zln_done, 1)
                        if step in (3, 11) and not first:
                            gate_high(s, hd - 1, step // 8, nw)
                        if step in (20, 24, 28, 32):
                            v = (step - 20) // 4
                            ready(V0 + v // 2, v % 2, s.v_half, 2 * hd + v // 2 + 1)
                            wait(act, s.vt_done, 4 * hd + v - 1)
                            wait(act, s.ol_done, 4 * hd)
                            A(vS[:, v % 2, :], ps[:, v, :], ACT.Copy).then_inc(s.v_ev, 1)
                        if step in (22, 26, 30, 34):
                            v = (step - 22) // 4
                            act.wait_ge(s.vt_done, 4 * hd + v + 1)
                            t, d = v % 2, v // 2
                            A(vtok[:, t * NBH:(t + 1) * NBH, d * P:(d + 1) * P],
                              ps[:, 6 + v % 2, :].rearrange("p (b c) -> p b c", b=NBH), ACT.Copy
                              ).then_inc(s.vt_ev, 1)
                        for half in range(2):
                            for item in range(NLV + 2):
                                if gla and step == score_step(half, item) - 3:
                                    exps(hd, half, item)
                                if step == score_step(half, item) and item == LAST:
                                    act.wait_ge(s.kt_done, 2 * hd + half + 1)
                                    wait(act, s.o_done, 8 * hd + 4 * half)
                                    wait(act, s.st_done, 7 * hd + 4 * half)
                                    g = half * (NLV + 2) + item
                                    src = ps[:, 4 + g % 2, :].rearrange("p (b c) -> p b c", b=NBH)
                                    if not gla:
                                        act.wait_ge(s.headc_done, hd + 1)
                                    A(ktok[:], src, ACT.Copy, scale=1.0 if gla else headc[:, 0:1]
                                      ).then_inc(s.kt_ev, 1)
                            for b in range(NBH):
                                if step == block_step(half, b):
                                    bb = half * NBH + b
                                    act.wait_ge(s.o_done, 8 * hd + bb + 1)
                                    if bb == 0:
                                        wait(act, s.ot_done, 4 * hd)
                                    A(on[:, bb, :], ps[:, 6, bb % 2 * DV:(bb % 2 + 1) * DV], ACT.Copy
                                      ).then_inc(s.o_ev, 1)
                            if step == block_step(half, NBH - 1) + 2:
                                act.wait_ge(s.var_done, 2 * hd + half + 1)
                                A(sd[:], ve[:], ACT.Sqrt).then_inc(s.sd_done, 1)
                        if step in (52, 56, 60, 64):
                            v = (step - 52) // 4
                            ready(R0 + v // 2, v % 2, s.r_half, 2 * hd + v // 2 + 1)
                            wait(act, s.g_done, 4 * hd)
                            A(rS[:, v // 2, tok(v % 2)], ps[:, v, :], ACT.Silu).then_inc(s.r_ev, 1)

                def exps(hd, half, item):
                    gi = half * (NLV + 2) + item
                    e = ee[:, gi % 2, :]
                    if item <= LAST:
                        act.wait_ge(diff_done, 2 * (NLV + 1) * hd + half * (NLV + 1) + item + 1)
                    if item < NLV:
                        w = LEVELS[item]
                        v = e.rearrange("p (n s) -> p n s", s=2 * w)
                        A(v[:, :, 0:w], v[:, :, 0:w], ACT.Exp, scale=-1.0 / TAU)
                        A(v[:, :, w:], v[:, :, w:], ACT.Exp, scale=1.0 / TAU).then_inc(exp_done, 1)
                    elif item == LAST:
                        A(e, e, ACT.Exp, scale=-1.0 / TAU).then_inc(exp_done, 1)
                    else:
                        act.wait_ge(prod_done, 2 * (NLV + 2) * hd + gi - 1)
                        A(e, bc[:, tok(half)], ACT.Exp, scale=1.0 / TAU).then_inc(exp_done, 1)

                window(0, True)
                with act.Fori(1, HEADS) as hd:
                    window(hd, False)
                for half in range(2):
                    gate_high(s, HEADS - 1, half, n0 + BRANCH_TILES - 2)

            for f in range(KT):
                act.dma_start(h[:, f, :], xT[:, f, :]).then_inc(h_in[f], 16)
            act.dma_start(smallt[:], small).then_inc(const_in, 16)
            act.dma_start(normw[:], norms).then_inc(const_in, 16)
            act.dma_start(gbt[:], gate_b).then_inc(const_in, 16)
            act.dma_start(rett[:], ret).then_inc(const_in, 16)
            act.dma_start(uf[:].rearrange("p a b -> p (a b)"), masks.rearrange("p s n -> p (s n)")
                          ).then_inc(const_in, 16)
            act.dma_start(w2t[:], gate_w2).then_inc(const_in, 16)
            act.dma_start(ropet[:], rope).then_inc(rope_in, 16)
            act.wait_ge(const_in, 16 * 6)

            norm(norm1, lambda e, f, t: e.wait_ge(h_in[f], 16), True)
            ffn(f1, N_F1)
            norm(norm2, after_ffn(f1), True)
            act.dma_start(h_spill, h[:]).then_inc(h_saved, 16)
            act.wait_ge(h_saved, 16)
            branch(ret_s, N_RET, False)
            for f in range(KT):
                for t in range(2):
                    idx = 2 * f + t
                    if t == 0:
                        act.wait_ge(ga_half, f + 1)
                    else:
                        act.wait_ge(w_used, N_GA + f + 1)
                    wait(act, ga_ev, idx - 1)
                    A(vS[:, t, :], ps[:, 2 * (f % 2) + t, :], ACT.Sigmoid).then_inc(ga_sig, 1)
                if f >= 1:
                    act.wait_ge(ga_ev, 2 * f)
                    act.dma_start(y_spill[:, f - 1, :], y[:, f - 1, :]).then_inc(y_saved, 16)
            act.wait_ge(ga_ev, 2 * KT)
            act.dma_start(y_spill[:, KT - 1, :], y[:, KT - 1, :]).then_inc(y_saved, 16)
            act.wait_ge(lr_half, 1)
            A(lrT[:, tok(0)], ps[0:16, 0, :], ACT.Copy).then_inc(lr_ev, 1)
            act.wait_ge(w_used, N_LR + 1)
            A(lrT[:, tok(1)], ps[0:16, 1, :], ACT.Copy).then_inc(lr_ev, 1)
            branch(gla_s, N_GLA, True)
            yr = vtok[:].rearrange("p b c -> p (b c)").rearrange("p (s t) -> p s t", s=2)
            act.wait_ge(y_saved, 16 * KT)
            for f in range(2):
                act.dma_start(yr[:, f, :], y_spill[:, f, :]).then_inc(y_back[f], 16)
            act.wait_ge(w_used, N_GB)
            for f in range(KT):
                act.dma_start(h[:, f, :], h_spill[:, f, :]).then_inc(h_in[f], 16)
            for f in range(KT):
                for t in range(2):
                    idx = 2 * f + t
                    if t == 0:
                        act.wait_ge(gb_half, f + 1)
                    else:
                        act.wait_ge(w_used, N_GB + f + 1)
                    wait(act, gb_ev, idx - 1)
                    A(vS[:, t, :], ps[:, 2 * (f % 2) + t, :], ACT.Sigmoid).then_inc(gb_sig, 1)
                if 1 <= f < KT - 1:
                    act.wait_ge(gb_ev, 2 * f)
                    act.dma_start(yr[:, (f + 1) % 2, :], y_spill[:, f + 1, :]
                                  ).then_inc(y_back[(f + 1) % 2], 16)
            act.wait_ge(w_used, N_GB + KT)
            for t in range(2):
                for f in range(KT):
                    act.wait_ge(gb_ev, 2 * f + t + 1)
                    A(uH[:, f, tok(t)], y[:, f, tok(t)], ACT.Copy).then_inc(mh_done, 1)
            norm(norm3, lambda e, f, t: e.wait_ge(wo_ev, 2 * f + t + 1), True)
            ffn(f2, N_F2)
            norm(norm4, after_ffn(f2), False)
            for t in range(2):
                for f in range(KT):
                    act.wait_ge(norm4.u_done, KT * t + f + 1)
                    act.dma_start(out[:, f, tok(t)], h[:, f, tok(t)]).then_inc(out_saved, 16)
            act.wait_ge(out_saved, 16 * 2 * KT)

        @block.vector
        def _(dve):
            V = nc.vector

            def norm(nm, ready, cut, wcol):
                for t in range(2):
                    for f in range(1, KT):
                        dve.wait_ge(nm.sq_done, KT * t + f + 1)
                        if f > 1:
                            dve.wait_ge(nm.sum_done, (KT - 1) * t + f - 1)
                        V.tensor_tensor(ssum[:, t, :], sq[:, 0, :] if f == 1 else ssum[:, t, :],
                                        sq[:, f % 2, :], ALU.add).then_inc(nm.sum_done, 1)
                    dve.wait_ge(nm.root_done, t + 1)
                    V.reciprocal(rinv[:, t, :], rinv[:, t, :]).then_inc(nm.inv_done, 1)
                    dve.wait_ge(nm.inv_done, t + 1)

                    def scaled(f):
                        o = uf[:, f % 2, :] if cut else h[:, f, tok(t)]
                        if cut:
                            wait(dve, nm.ul_done, KT * t + f - 1)
                        V.scalar_tensor_tensor(out=o, in0=h[:, f, tok(t)],
                                               scalar=normw[:, wcol * KT + f:wcol * KT + f + 1],
                                               in1=rinv[:, t, :], op0=ALU.mult, op1=ALU.mult
                                               ).then_inc(nm.u_done, 1)

                    def low(f):
                        dve.wait_ge(nm.uh_done, KT * t + f + 1)
                        V.tensor_tensor(uL[:, f, tok(t)], uf[:, f % 2, :],
                                        uH[:, f, tok(t)].bitcast(F32), ALU.subtract
                                        ).then_inc(nm.ul_done, 1)

                    for f in range(KT):
                        scaled(f)
                        if cut and f:
                            low(f - 1)
                    if cut:
                        low(KT - 1)
                if cut:
                    dve.wait_ge(nm.ul_done, 2 * KT)

            def ffn(s, n0):
                def p1(i, par, first=False):
                    for j in range(2):
                        n = n0 + 2 * j + 1 if first else n0 + 4 + 6 * (i - 1) + 2 * j + 1
                        for t in range(2):
                            idx = 4 * i + 2 * j + t
                            if t == 0:
                                dve.wait_ge(s.b_done, 2 * i + j + 1)
                            else:
                                dve.wait_ge(w_used, n + 1)
                            dve.wait_ge(s.silu_done, idx + 1)
                            wait(dve, s.hl_done, idx - 1)
                            V.tensor_tensor(hidf[:, t, :], sil[:, t, :], ps[:, 4 * j + 2 + t, :],
                                            ALU.mult).then_inc(s.gate_done, 1)
                            dve.wait_ge(s.hh_done, idx + 1)
                            V.tensor_tensor(hidL[:, par, j, tok(t)], hidf[:, t, :],
                                            hidH[:, par, j, tok(t)].bitcast(F32), ALU.subtract
                                            ).then_inc(s.hl_done, 1)

                def p2(g, n):
                    for v in range(16):
                        c, t, fl = v // 8, v % 8 // 4, v % 4
                        f = 4 * c + fl
                        if v % 8 == 7:
                            dve.wait_ge(w_used, n + c + 1)
                        else:
                            dve.wait_ge(s.p2_done, 14 * g + 7 * c + v % 8 + 1)
                        wait(dve, s.acc_done, 16 * (g - 1) + v + 1)
                        V.scalar_tensor_tensor(out=h[:, f, tok(t)], in0=ps[:, v % 8, :], scalar=0.5,
                                               in1=h[:, f, tok(t)], op0=ALU.mult, op1=ALU.add
                                               ).then_inc(s.acc_done, 1)

                p1(0, 0, first=True)
                p1(1, 1)
                p2(0, n0 + 8)
                with dve.Fori(1, FFG // 2) as c:
                    for par in range(2):
                        i = c * 2 + par
                        p1(i, par)
                        p2(i - 1, n0 + 8 + 6 * (i - 1))
                i = FFG - 1
                p1(i, i % 2)
                p2(i - 1, n0 + 8 + 6 * (i - 1))
                p2(i, n0 + 8 + 6 * (i - 1) + 2)

            def gate(s, hp, half, gla):
                for d in range(2):
                    idx = 4 * hp + 2 * half + d
                    dve.wait_ge(s.ot_done, idx + 1)
                    dve.wait_ge(s.r_ev, 4 * hp + 4)
                    if half:
                        dve.wait_ge(s.ol_done, idx - 1)
                    o = ogf[:, d, :]
                    if gla:
                        V.scalar_tensor_tensor(out=o, in0=ps[:, 6 + d, :],
                                               scalar=normw[:, 4 * KT + d:4 * KT + d + 1],
                                               in1=rS[:, d, tok(half)], op0=ALU.mult, op1=ALU.mult
                                               ).then_inc(s.g_done, 1)
                    else:
                        V.tensor_tensor(o, ps[:, 6 + d, :], rS[:, d, tok(half)], ALU.mult
                                        ).then_inc(s.g_done, 1)
                for d in range(2):
                    idx = 4 * hp + 2 * half + d
                    dve.wait_ge(s.oh_done, idx + 1)
                    V.tensor_tensor(ogL[:, d, tok(half)], ogf[:, d, :],
                                    ogH[:, d, tok(half)].bitcast(F32), ALU.subtract
                                    ).then_inc(s.ol_done, 1)

            def branch_add(s, hp, v, n_tile, n_before):
                c, t, fl = v // 8, v % 8 // 4, v % 4
                f = 4 * c + fl
                if v % 8 == 7:
                    dve.wait_ge(w_used, n_tile + 1)
                else:
                    dve.wait_ge(s.b_part, 14 * hp + 7 * c + v % 8 + 1)
                if v == 0:
                    dve.wait_ge(w_used, n_before)
                V.tensor_tensor(y[:, f, tok(t)], ps[:, v % 4, :], y[:, f, tok(t)], ALU.add
                                ).then_inc(s.b_ev, 1)

            def branch(s, n0, gla):
                n_sc = NLV + 1 if gla else 1
                per_window = 1 + 2 * NBH + (2 * 3 + 2 if gla else 2 * 2 + 4)

                def window(hd, first):
                    nw = n0 if first else n0 + 6 + 8 * (hd - 1)
                    base = 0 if first else per_window * hd
                    count = [0]

                    def link(ins):
                        count[0] += 1
                        ins.then_inc(s.chain, 1)
                        dve.wait_ge(s.chain, base + count[0])

                    for step in range(STEPS + 1):
                        if step == 0:
                            wait(dve, s.kt_ev, 2 * hd)
                            wait(dve, s.st_ev, 7 * hd)
                            if gla:
                                wait(dve, zmin_done, 2 * hd)
                                wait(dve, z_done, 2 * hd)
                                wait(dve, zabs_done, 2 * hd)
                                V.tensor_copy(w2h[:], w2t[:, bass.ds(hd * DK, DK)])
                                V.tensor_copy(headc[:, 2:3], gbt[:, bass.ds(hd, 1)]
                                              ).then_inc(s.headc_done, 1)
                            else:
                                V.tensor_copy(headc[:, 0:2], rett[:, bass.ds(hd, 1), 2 * BLK:RETC]
                                              .rearrange("p a c -> p (a c)")).then_inc(s.headc_done, 1)
                            wait(dve, s.o_done, 8 * hd)
                            link(V.memset(state[:, 0, :], 0.0))
                            dve.wait_ge(s.headc_done, hd + 1)
                            if first:
                                V.memset(y[:], 0.0).then_inc(s.y_clear, 1)
                                dve.wait_ge(s.y_clear, 1)
                        if gla and step == 2:
                            for t in range(2):
                                dve.wait_ge(zabs_done, 2 * hd + t + 1)
                                wait(dve, exp_done, 2 * (NLV + 2) * hd)
                                wait(dve, diff_done, 2 * (NLV + 1) * hd)
                                V.tensor_scalar(bc[:, tok(t)], ps[:, 4 + t, :], headc[:, 2:3], 0.0,
                                                ALU.add, ALU.min).then_inc(zmin_done, 1)
                            for t in range(2):
                                dve.wait_ge(zln_done, 2 * hd + t + 1)
                                dve.wait_ge(zmin_done, 2 * hd + t + 1)
                                ins = V.tensor_tensor(ee[:, t, :], bc[:, tok(t)], ee[:, t, :],
                                                      ALU.subtract)
                                link(ins)
                            for b in range(2 * NBH):
                                ins = V.tensor_tensor_scan(bc[:, b * BLK:(b + 1) * BLK], ones,
                                                           ee[:, b // NBH,
                                                              b % NBH * BLK:(b % NBH + 1) * BLK],
                                                           0.0, ALU.mult, ALU.add)
                            ins.then_inc(cum_done, 1)
                            dve.wait_ge(cum_done, hd + 1)
                        if step in (3, 11) and not first:
                            gate(s, hd - 1, step // 8, gla)
                        if not gla and step in (4, 8, 12, 16):
                            t = step // 4 % 2
                            t = 0 if step in (4, 12) else 1
                            isk = step >= 12
                            if t == 0:
                                dve.wait_ge(s.k_half if isk else s.q_half, hd + 1)
                            else:
                                dve.wait_ge(w_used, nw + (K if isk else Q) + 1)
                            if first and step == 4:
                                dve.wait_ge(rope_in, 16)
                            if not isk:
                                wait(dve, s.o_done, 8 * hd)
                                wait(dve, s.qd_done, 2 * hd)
                            wait(dve, s.q_ev if step in (8, 12) else s.k_ev,
                                 2 * hd + {4: 0, 8: 1, 12: 2, 16: 1}[step])
                            x = ps[:, (2 if isk else 0) + t, :]
                            cos, sin = ropet[:, 0, tok(t)], ropet[:, 1, tok(t)]
                            V.tensor_tensor(rtmp[0:64, 0, :], x[64:128], sin[64:128], ALU.mult)
                            V.tensor_tensor(rtmp[64:128, 0, :], x[0:64], sin[0:64], ALU.mult)
                            link(V.tensor_tensor(rtmp[:, 1, :], x, cos, ALU.mult))
                            V.tensor_tensor((kT if isk else qT)[:, tok(t)], rtmp[:, 0, :],
                                            rtmp[:, 1, :], ALU.add
                                            ).then_inc(s.k_ev if isk else s.q_ev, 1)
                        for half in range(2):
                            for item in range(NLV + 2):
                                if step == score_step(half, item) - 2:
                                    if gla:
                                        gla_item(hd, half, item, link)
                                if step == score_step(half, item) + 1 and item == DIAG:
                                    if gla:
                                        score_in(hd, half, DIAG, link)
                                    else:
                                        ret_item(hd, half, link)
                            for b in range(NBH):
                                if step == block_step(half, b) + 1:
                                    block_in(hd, half * NBH + b, link)
                            if step == block_step(half, NBH - 1) + 2:
                                half_norm(hd, half, link)
                        if not first and 1 + 8 * B0 <= step < 1 + 8 * R0:
                            v = step - 1 - 8 * B0
                            branch_add(s, hd - 1, v, nw + B0 + v // 8, nw)
                    assert count[0] == per_window, (count[0], per_window)

                def ret_item(hd, half, link):
                    dve.wait_ge(s.sc_done, 2 * hd + half + 1)
                    wait(dve, s.o_done, 8 * hd)
                    pb = ps[:, 4 + (half * (NLV + 2) + DIAG) % 2, :].rearrange("p (b n) -> p b n", b=NBH)
                    for b in range(NBH):
                        last = V.tensor_tensor(ss[:, half, b, :], pb[:, b, :],
                                               rett[:, bass.ds(hd, 1), 0:BLK].rearrange("p a n -> p (a n)"),
                                               ALU.mult)
                    last.then_inc(s.sc_ev, 1)
                    wait(dve, s.o_done, 8 * hd + 4 * half)
                    dve.wait_ge(s.q_ev, 2 * hd + half + 1)
                    for b in range(NBH):
                        last = V.tensor_tensor(qd[:, b, :],
                                               qT[:, half * HF + b * BLK:half * HF + (b + 1) * BLK],
                                               rett[:, bass.ds(hd, 1), BLK:2 * BLK].rearrange("p a n -> p (a n)"),
                                               ALU.mult)
                    last.then_inc(s.qd_done, 1)

                def gla_item(hd, half, item, link):
                    if item == 0:
                        difference(hd, half, 0)
                    if item + 1 <= LAST:
                        difference(hd, half, item + 1)
                    g = half * (NLV + 2) + item
                    n = 2 * (NLV + 2) * hd + g
                    e = ee[:, g % 2, :]
                    dve.wait_ge(exp_done, n + 1)
                    dve.wait_ge(s.q_ev, 2 * hd + half + 1)
                    dve.wait_ge(s.k_ev, 2 * hd + half + 1)
                    q, k = qT[:, tok(half)], kT[:, tok(half)]
                    if item <= LAST:
                        if item == 0:
                            wait(dve, s.kt_done, 2 * hd + half)
                            wait(dve, s.sc_done, 2 * n_sc * hd + n_sc * half)
                        elif item >= 2:
                            dve.wait_ge(s.sc_done, 2 * n_sc * hd + n_sc * half + item - 1)
                    if item < NLV:
                        V.tensor_tensor(qE[:, item % 2, :], q, e, ALU.mult)
                        V.tensor_tensor(kE[:, item % 2, :], k, e, ALU.mult).then_inc(prod_done, 1)
                    elif item == LAST:
                        V.tensor_tensor(kE[:, item % 2, :], k, e, ALU.mult).then_inc(prod_done, 1)
                    else:
                        wait(dve, s.o_done, 8 * hd + 4 * half)
                        V.tensor_copy(bdec[:, half, :],
                                      e.rearrange("p (b n) -> p b n", b=NBH)[:, :, BLK - 1])
                        V.tensor_tensor(qd[:].rearrange("p b n -> p (b n)"), q, e, ALU.mult
                                        ).then_inc(prod_done, 1)
                        dve.wait_ge(prod_done, n + 1)
                    if 1 <= item <= NLV:
                        score_in(hd, half, item - 1, link)

                def difference(hd, half, item):
                    g = half * (NLV + 2) + item
                    wait(dve, prod_done, 2 * (NLV + 2) * hd + g - 1)
                    w = LEVELS[item] if item < NLV else BLK
                    n = 2 * w if item < NLV else BLK
                    b3 = bc[:, tok(half)].rearrange("p (n s) -> p n s", s=n)
                    ref = b3[:, :, w - 1:w].to_broadcast([P, HF // n, n])
                    V.tensor_tensor(ee[:, g % 2, :].rearrange("p (n s) -> p n s", s=n), b3, ref,
                                    ALU.subtract).then_inc(diff_done, 1)

                def score_in(hd, half, item, link):
                    sc = 2 * n_sc * hd + n_sc * half
                    order = item if item < NLV else NLV
                    dve.wait_ge(s.sc_done, sc + order + 1)
                    g = half * (NLV + 2) + item
                    pb = ps[:, 4 + g % 2, :].rearrange("p (b n) -> p b n", b=NBH)
                    o = ss[:, half]
                    if item == 0:
                        wait(dve, s.o_done, 8 * hd)
                        V.tensor_tensor(o, pb, mask0.unsqueeze(1).to_broadcast([P, NBH, BLK]), ALU.mult
                                        ).then_inc(s.sc_ev, 1)
                    else:
                        dve.wait_ge(s.sc_ev, sc + order)
                        mi = maskt[:, order:order + 1, :].to_broadcast([P, NBH, BLK])
                        carry()
                        V.copy_predicated(o, mi, pb).then_inc(s.sc_ev, 1)
                    if item == DIAG:
                        dve.wait_ge(prod_done, 2 * (NLV + 2) * hd + half * (NLV + 2) + NLV + 2)

                def block_in(hd, b, link):
                    half, bb = b // NBH, b % NBH
                    if gla and bb == 0:
                        dve.wait_ge(prod_done, (NLV + 2) * (2 * hd + half + 1))
                    if b < 2 * NBH - 1:
                        dve.wait_ge(s.st_done, 7 * hd + b + 1)
                        if b >= 1:
                            dve.wait_ge(s.st_ev, 7 * hd + b)
                        dve.wait_ge(s.o_done, 8 * hd + b + 1)
                        dec = bdec[:, half, bb:bb + 1] if gla else headc[:, 1:2]
                        V.scalar_tensor_tensor(out=state[:, (b + 1) % 2, :], in0=state[:, b % 2, :],
                                               scalar=dec,
                                               in1=ps[:, 7, b % 2 * DV:(b % 2 + 1) * DV],
                                               op0=ALU.mult, op1=ALU.add).then_inc(s.st_ev, 1)
                    dve.wait_ge(s.o_ev, 8 * hd + b + 1)
                    link(V.bn_stats(bst[:, bb, :], on[:, b, :]))

                def half_norm(hd, half, link):
                    wait(dve, s.on_done, 2 * hd + half)
                    carry()
                    for b in range(NBH):
                        ins = V.bn_aggr(mv[:, b, :], bst[:, b, :])
                    link(ins)
                    if gla:
                        link(V.tensor_tensor(ve[:], mv[:, :, 0], mv[:, :, 0], ALU.mult))
                        V.scalar_tensor_tensor(out=ve[:], in0=ve[:], scalar=EPS, in1=mv[:, :, 1],
                                               op0=ALU.add, op1=ALU.add).then_inc(s.var_done, 1)
                    else:
                        V.tensor_scalar(ve[:], mv[:, :, 1], EPS, None, ALU.add).then_inc(s.var_done, 1)
                    dve.wait_ge(s.sd_done, 2 * hd + half + 1)
                    link(V.reciprocal(rs[:], sd[:]))
                    for b in range(NBH):
                        o = on[:, half * NBH + b, :]
                        if gla:
                            ins = V.tensor_scalar(o, o, rs[:, b:b + 1], None, ALU.mult)
                        else:
                            ins = V.tensor_scalar(o, o, mv[:, b, 0:1], rs[:, b:b + 1], ALU.subtract,
                                                  ALU.mult)
                    ins.then_inc(s.on_done, 1)

                window(0, True)
                with dve.Fori(1, HEADS) as hd:
                    window(hd, False)
                hp = HEADS - 1
                gate(s, hp, 0, gla)
                gate(s, hp, 1, gla)
                nb = n0 + 6 + 8 * hp
                for v in range(16):
                    branch_add(s, hp, v, nb + v // 8, nb)

            dve.wait_ge(const_in, 16 * 6)
            V.tensor_copy(maskt[:].rearrange("p s n -> p (s n)"), uf[:].rearrange("p a b -> p (a b)")
                          ).then_inc(masks_done, 1)
            dve.wait_ge(masks_done, 1)
            norm(norm1, lambda e, f, t: None, True, 0)
            ffn(f1, N_F1)
            norm(norm2, lambda e, f, t: None, True, 1)
            branch(ret_s, N_RET, False)
            for f in range(KT):
                for t in range(2):
                    idx = 2 * f + t
                    dve.wait_ge(ga_sig, idx + 1)
                    if idx == 0:
                        dve.wait_ge(ret_s.b_ev, 16 * HEADS)
                    V.tensor_tensor(y[:, f, tok(t)], y[:, f, tok(t)], vS[:, t, :], ALU.mult
                                    ).then_inc(ga_ev, 1)
            dve.wait_ge(y_saved, 16 * KT)
            branch(gla_s, N_GLA, True)
            yr = vtok[:].rearrange("p b c -> p (b c)").rearrange("p (s t) -> p s t", s=2)
            for f in range(KT):
                for t in range(2):
                    idx = 2 * f + t
                    dve.wait_ge(gb_sig, idx + 1)
                    if idx == 0:
                        dve.wait_ge(gla_s.b_ev, 16 * HEADS)
                    if t == 0:
                        dve.wait_ge(y_back[f % 2], 16 * (f // 2 + 1))
                    V.tensor_tensor(vS[:, t, :], y[:, f, tok(t)], vS[:, t, :], ALU.mult
                                    ).then_inc(gb_mul, 1)
                    dve.wait_ge(gb_mul, idx + 1)
                    V.tensor_tensor(y[:, f, tok(t)], vS[:, t, :], yr[:, f % 2, tok(t)], ALU.add
                                    ).then_inc(gb_ev, 1)
            for t in range(2):
                for f in range(KT):
                    dve.wait_ge(mh_done, KT * t + f + 1)
                    V.tensor_tensor(uL[:, f, tok(t)], y[:, f, tok(t)], uH[:, f, tok(t)].bitcast(F32),
                                    ALU.subtract).then_inc(ml_done, 1)
            for f in range(KT):
                for t in range(2):
                    if t == 0:
                        dve.wait_ge(wo_half, f + 1)
                        dve.wait_ge(h_in[f], 32)
                    else:
                        dve.wait_ge(w_used, N_OUT + f + 1)
                    V.tensor_tensor(h[:, f, tok(t)], ps[:, 2 * (f % 2) + t, :], h[:, f, tok(t)],
                                    ALU.add).then_inc(wo_ev, 1)
            norm(norm3, lambda e, f, t: None, True, 2)
            ffn(f2, N_F2)
            norm(norm4, lambda e, f, t: None, False, 3)


def cols_tiles(w):
    kt, n = w.shape[0] // P, w.shape[1] // P
    return np.ascontiguousarray(w.reshape(kt, P, n, P).transpose(2, 1, 0, 3)).reshape(n, P, kt * P)


def rows_tiles(w):
    g = w.shape[0] // (2 * P)
    return np.ascontiguousarray(w.reshape(g, 2, P, 2, 4 * P).transpose(0, 3, 2, 1, 4)
                                ).reshape(2 * g, P, D)


def ffn_stream(w1, w3, w2):
    a, b, c = cols_tiles(w1), cols_tiles(w3), rows_tiles(w2)
    tiles = []
    for g in range(FFG):
        tiles += [a[2 * g], b[2 * g], a[2 * g + 1], b[2 * g + 1]]
        if g:
            tiles += [c[2 * g - 2], c[2 * g - 1]]
    return tiles + [c[2 * FFG - 2], c[2 * FFG - 1]]


def branch_stream(q, k, v, r, wb):
    b = rows_tiles(wb)
    q, k, v, r = (cols_tiles(x) for x in (q, k, v, r))
    tiles = []
    for hd in range(HEADS):
        tiles += [q[hd], k[hd], v[2 * hd], v[2 * hd + 1]]
        if hd:
            tiles += [b[2 * hd - 2], b[2 * hd - 1]]
        tiles += [r[2 * hd], r[2 * hd + 1]]
    return tiles + [b[2 * HEADS - 2], b[2 * HEADS - 1]]


def kernel(x, norm_ffn1, ffn1_w1, ffn1_w3, ffn1_w2, norm_mix, w_in, gla_gate_w2, gla_gate_b,
           gla_norm_w, w_branch_ret, w_branch_gla, w_out, norm_ffn2, ffn2_w1, ffn2_w3, ffn2_w2,
           norm_final):
    import concourse.bacc as bacc
    from concourse.bass_utils import run_bass_kernel_spmd

    A = np.asarray
    w_in = A(w_in)[0]
    widths = (512, 512, 1024, 1024, 512, 512, 1024, 1024, 16, 1024, 1024)
    at = np.cumsum((0,) + widths)
    qa, ka, va, ra, qb, kb, vb, rb, lr, ga, gb = (w_in[:, a:b] for a, b in zip(at[:-1], at[1:]))
    lr = np.concatenate([lr, np.zeros((D, P - lr.shape[1]), lr.dtype)], 1)
    tiles = ffn_stream(A(ffn1_w1)[0], A(ffn1_w3)[0], A(ffn1_w2)[0])
    tiles += branch_stream(qa, ka, va, ra, A(w_branch_ret)[0])
    tiles += list(cols_tiles(ga)) + list(cols_tiles(lr))
    tiles += branch_stream(qb, kb, vb, rb, A(w_branch_gla)[0])
    tiles += list(cols_tiles(gb)) + list(cols_tiles(A(w_out)[0]))
    tiles += ffn_stream(A(ffn2_w1)[0], A(ffn2_w3)[0], A(ffn2_w2)[0])
    assert len(tiles) == N_TILES

    def columns(v):
        return A(v).reshape(-1, P).T

    rope, ret, masks, small = decay_tables()
    arrays = {
        "xT": np.ascontiguousarray(A(x)[0].T.reshape(KT, P, T).transpose(1, 0, 2)),
        "wts": np.stack(tiles),
        "norms": np.ascontiguousarray(np.concatenate(
            [columns(v) for v in (norm_ffn1, norm_mix, norm_ffn2, norm_final, gla_norm_w)], 1)),
        "gate_w2": np.ascontiguousarray(A(gla_gate_w2)[0]),
        "gate_b": np.ascontiguousarray(columns(gla_gate_b)),
        "rope": rope,
        "ret": ret,
        "masks": masks,
        "small": small,
    }
    nc = bacc.Bacc("TRN2", target_bir_lowering=False, num_devices=1, dynamic_dma_scratch_size=1024)
    aps = [nc.dram_tensor(n, a.shape, mybir.dt.from_np(a.dtype), kind="ExternalInput").ap()
           for n, a in arrays.items()]
    out = nc.dram_tensor("yT", (P, KT, T), F32, kind="ExternalOutput").ap()
    spill = [nc.dram_tensor(n, (P, KT, T), F32, kind="Internal").ap() for n in ("h_spill", "y_spill")]
    block_kernel(nc, *aps, out, *spill)
    r = run_bass_kernel_spmd(nc, [arrays], core_ids=[0])
    got = r.results[0]["yT"]
    return np.ascontiguousarray(got.transpose(1, 0, 2)).reshape(D, T).T[None]
```

```python
from contextlib import ExitStack

import numpy as np

import concourse.bass as bass
from concourse import mybir

F32 = mybir.dt.float32
F32R = mybir.dt.float32r
U8 = mybir.dt.uint8
ALU = mybir.AluOpType
ACT = mybir.ActivationFunctionType

P = 128
T = 1024
D = 1024
KT = D // P
HF = 512
FF = 2816
FFG = FF // (2 * P)
HEADS = 4
DK = 128
DV = 256
BLK = 128
NBH = HF // BLK
CHUNK = 64
EPS = 1e-6
TAU = 16.0
QK_SCALE = DK ** -0.5
ROPE_BASE = 10000.0

RAW = 4
FFN_TILES = 6 * FFG
BRANCH_TILES = 8 * HEADS
N_F1 = 0
N_RET = N_F1 + FFN_TILES
N_GA = N_RET + BRANCH_TILES
N_LR = N_GA + KT
N_GLA = N_LR + 1
N_GB = N_GLA + BRANCH_TILES
N_OUT = N_GB + KT
N_F2 = N_OUT + KT
N_TILES = N_F2 + FFN_TILES

Q, K, V0, V1, B0, B1, R0, R1 = range(8)
STEPS = 64
LEVELS = (64, 32, 16, 8, 4, 2, 1)
NLV = len(LEVELS)
LAST, DIAG = NLV, NLV + 1


def score_step(half, item):
    return (18 if half == 0 else 36) + 2 * item


def block_step(half, b):
    return (36 if half == 0 else 54) + 2 * b


def wait(eng, sem, value):
    if isinstance(value, int) and value <= 0:
        return
    eng.wait_ge(sem, value)


def decay_tables():
    f = np.float32
    half = DK // 2
    inv = (f(ROPE_BASE) ** (-np.arange(half, dtype=f) / f(half))).astype(f)
    ang = (np.arange(T, dtype=f)[:, None] * inv[None, :]).astype(f).T.astype(np.float64)
    cos, sin = np.cos(ang), np.sin(ang)
    rope = np.stack([np.concatenate([cos, cos]), np.concatenate([sin, -sin])], 1).astype(f)
    lg = np.log1p(-np.exp2(-5.0 - np.arange(HEADS)))
    i = np.arange(BLK)
    m, n = i[:, None], i[None, :]
    seen = (m // CHUNK) <= (n // CHUNK)
    intra = np.where(seen, np.exp(lg[:, None, None] * np.abs(m - n)), 0.0) * QK_SCALE
    qdec = np.broadcast_to((np.exp(lg[:, None] * (i + 1.0)) * QK_SCALE)[:, None, :], (HEADS, P, BLK))
    kdec = np.exp(lg[:, None] * (BLK - 1.0 - i))[:, :, None]
    bdec = np.broadcast_to(np.exp(lg * BLK)[:, None, None], (HEADS, P, 1))
    ret = np.concatenate([intra, qdec, kdec, bdec], 2).transpose(1, 0, 2).astype(f)
    masks = [(m < 64) & (n >= 64)]
    for s in LEVELS[1:]:
        masks.append((m // (2 * s) == n // (2 * s)) & (m // s != n // s))
    masks.append(m == n)
    masks = np.stack(masks, 1)
    first = masks[:, 0].astype(f)
    small = np.concatenate([np.eye(P), np.full((P, P), 1.0 / D), first, np.ones((P, P)),
                            np.full((P, 1), EPS)], 1).astype(f)
    return rope, ret, np.ascontiguousarray(masks.astype(f)), small


RETC = 2 * BLK + 2
SMALLC = 4 * P + 1


class NormSignals:

    def __init__(self, sem, stage):
        self.sq_done = sem(f"{stage}_sq_done")
        self.sum_done = sem(f"{stage}_sum_done")
        self.mean_done = sem(f"{stage}_mean_done")
        self.root_done = sem(f"{stage}_root_done")
        self.inv_done = sem(f"{stage}_inv_done")
        self.uh_done = sem(f"{stage}_uh_done")
        self.ul_done = sem(f"{stage}_ul_done")


class FfnSignals:

    def __init__(self, sem, stage):
        self.a_done = sem(f"{stage}_a_done")
        self.b_done = sem(f"{stage}_b_done")
        self.p2_done = sem(f"{stage}_p2_done")
        self.as_done = sem(f"{stage}_as_done")
        self.silu_done = sem(f"{stage}_silu_done")
        self.sr_done = sem(f"{stage}_sr_done")
        self.gate_done = sem(f"{stage}_gate_done")
        self.hh_done = sem(f"{stage}_hh_done")
        self.hl_done = sem(f"{stage}_hl_done")
        self.acc_done = sem(f"{stage}_acc_done")


class BranchSignals:

    def __init__(self, sem, stage):
        self.half_done = sem(f"{stage}_half_done")
        self.b_part = sem(f"{stage}_b_part")
        self.q_ev = sem(f"{stage}_q_ev")
        self.k_ev = sem(f"{stage}_k_ev")
        self.v_ev = sem(f"{stage}_v_ev")
        self.vt_done = sem(f"{stage}_vt_done")
        self.vt_ev = sem(f"{stage}_vt_ev")
        self.r_sc = sem(f"{stage}_r_sc")
        self.r_ev = sem(f"{stage}_r_ev")
        self.b_ev = sem(f"{stage}_b_ev")
        self.ot_done = sem(f"{stage}_ot_done")
        self.g_done = sem(f"{stage}_g_done")
        self.oh_done = sem(f"{stage}_oh_done")
        self.ol_done = sem(f"{stage}_ol_done")
        self.sc_done = sem(f"{stage}_sc_done")
        self.sc_ev = sem(f"{stage}_sc_ev")
        self.kt_done = sem(f"{stage}_kt_done")
        self.kt_ev = sem(f"{stage}_kt_ev")
        self.qd_done = sem(f"{stage}_qd_done")
        self.o_done = sem(f"{stage}_o_done")
        self.o_ev = sem(f"{stage}_o_ev")
        self.st_done = sem(f"{stage}_st_done")
        self.st_ev = sem(f"{stage}_st_ev")
        self.var_done = sem(f"{stage}_var_done")
        self.sd_done = sem(f"{stage}_sd_done")
        self.on_done = sem(f"{stage}_on_done")
        self.chain = sem(f"{stage}_chain")
        self.headc_done = sem(f"{stage}_headc_done")
        self.y_clear = sem(f"{stage}_y_clear")


def block_kernel(nc, xT, wts, norms, gate_w2, gate_b, rope, ret, masks, small, out, h_spill, y_spill):
    ctx = ExitStack()
    with ctx:
        def sb(name, shape, dt=F32, scope=ctx):
            return scope.enter_context(nc.sbuf_tensor(name, shape, dt))

        def sem(name):
            return ctx.enter_context(nc.semaphore(name))

        uH = sb("uH", [P, KT, T], F32R)
        uL = sb("uL", [P, KT, T], F32R)
        raw = [sb(f"raw{i}", [P, D]) for i in range(RAW)]
        wH = [sb(f"wH{i}", [P, D], F32R) for i in range(2)]
        wL = [sb(f"wL{i}", [P, D], F32R) for i in range(2)]
        smallt = sb("smallt", [P, SMALLC])
        ident, mean_of, mask0 = (smallt[:, i * P:(i + 1) * P] for i in range(3))
        ones = smallt[:, 3 * P:4 * P]
        eps = smallt[:, 4 * P:4 * P + 1]
        normw = sb("normw", [P, 4 * KT + 2])
        gbt = sb("gbt", [P, HEADS])
        rinv = sb("rinv", [P, 2, HF])
        maskt = sb("maskt", [P, NLV + 1, BLK], U8)
        w2t = sb("w2t", [16, HEADS * DK])
        w2h = sb("w2h", [16, DK])
        headc = sb("headc", [P, 4])
        carrier = sb("carrier", [P, 1])
        bst = sb("bst", [P, NBH, 6])
        mv = sb("mv", [P, NBH, 2])
        ve = sb("ve", [P, NBH])
        sd = sb("sd", [P, NBH])
        rs = sb("rs", [P, NBH])
        bdec = sb("bdec", [P, 2, NBH])

        with ExitStack() as f:
            h = sb("h", [P, KT, T], scope=f)
            hidH = sb("hidH", [P, 2, 2, T], F32R, scope=f)
            hidL = sb("hidL", [P, 2, 2, T], F32R, scope=f)
            sq = sb("sq", [P, 2, HF], scope=f)
            ssum = sb("ssum", [P, 2, HF], scope=f)
            sil = sb("sil", [P, 2, HF], scope=f)
            hidf = sb("hidf", [P, 2, HF], scope=f)
            maskf = sb("maskf", [P, NLV + 1, BLK], scope=f)
        m = ctx.enter_context(ExitStack())
        ogH = sb("ogH", [P, 2, T], F32R, scope=m)
        ogL = sb("ogL", [P, 2, T], F32R, scope=m)
        rS = sb("rS", [P, 2, T], scope=m)
        on = sb("on", [P, 2 * NBH, DV], scope=m)
        y = sb("y", [P, KT, T], scope=m)
        ogf = sb("ogf", [P, 2, HF], scope=m)
        ss = sb("ss", [P, 2, NBH, BLK], scope=m)
        qd = sb("qd", [P, NBH, BLK], scope=m)
        ktok = sb("ktok", [P, NBH, DK], scope=m)
        state = sb("state", [P, 2, DV], scope=m)
        vS = ogf
        qT = sb("qT", [P, T], scope=m)
        kT = sb("kT", [P, T], scope=m)
        vtok = sb("vtok", [P, 2 * NBH, DV], scope=m)
        with ExitStack() as r:
            ropet = sb("ropet", [P, 2, T], scope=r)
            rtmp = sb("rtmp", [P, 2, HF], scope=r)
            rett = sb("rett", [P, HEADS, RETC], scope=r)
        bc = sb("bc", [P, T], scope=m)
        lrT = sb("lrT", [16, T], scope=m)
        ee = sb("ee", [P, 2, HF], scope=m)
        qE = sb("qE", [P, 2, HF], scope=m)
        kE = sb("kE", [P, 2, HF], scope=m)

        ps = ctx.enter_context(nc.psum_tensor("ps", [P, 8, HF], F32))

        const_in = sem("const_in")
        late_in = sem("late_in")
        rope_done = sem("rope_done")
        y_done = sem("y_done")
        masks_done = sem("masks_done")
        raw_in = [sem(f"raw_in{i}") for i in range(RAW)]
        w_high = sem("w_high")
        w_ready = sem("w_ready")
        w_used = sem("w_used")
        h_in = [sem(f"h_in{i}") for i in range(KT)]
        x_rest_in = [sem(f"x_rest_in{i}") for i in range(2)]
        cols_half = sem("cols_half")
        h_saved = sem("h_saved")
        y_saved = sem("y_saved")
        y_back = [sem(f"y_back{i}") for i in range(2)]
        out_saved = sem("out_saved")

        norm1, norm2, norm3, norm4 = (NormSignals(sem, f"norm{i}") for i in range(1, 5))
        f1, f2 = FfnSignals(sem, "f1"), FfnSignals(sem, "f2")
        ret_s, gla_s = BranchSignals(sem, "ret"), BranchSignals(sem, "gla")
        z_done, zabs_done, zmin_done, zexp_done, zln_done, cum_done = (
            sem(x) for x in ("z_done", "zabs_done", "zmin_done", "zexp_done", "zln_done", "cum_done"))
        diff_done, exp_done, prod_done = (sem(x) for x in ("diff_done", "exp_done", "prod_done"))
        lr_ev = sem("lr_ev")
        ga_sc, ga_sig, ga_ev = (sem(f"ga_{x}") for x in ("sc", "sig", "ev"))
        gb_sc, gb_sig, gb_mul, gb_ev = (sem(f"gb_{x}") for x in ("sc", "sig", "mul", "ev"))
        mh_done, ml_done = sem("mh_done"), sem("ml_done")
        wo_ev = sem("wo_ev")

        def tok(half):
            return slice(half * HF, (half + 1) * HF)

        def place(f, t):
            return 8 * (f // 4) + 4 * t + f % 4

        def carry():
            nc.vector.memset(carrier[:], 0.0)

        block = ctx.enter_context(nc.Block())

        @block.sync
        def _(sp):
            def load(n, slot, round_):
                wait(sp, w_ready, n - RAW + 1)
                sp.dma_start(raw[slot][:], wts[bass.ds(n, 1)].rearrange("a p c -> p (a c)")
                             ).then_inc(raw_in[slot], 16)

            for n in range(RAW):
                load(n, n, 0)
            with sp.Fori(1, N_TILES // RAW) as i:
                for s in range(RAW):
                    load(i * RAW + s, s, i)
            for n in range(N_TILES // RAW * RAW, N_TILES):
                load(n, n % RAW, n // RAW)

        @block.gpsimd
        def _(pool):
            def cut(n, s, round_):
                slot = s % 2
                pool.wait_ge(raw_in[s], 16 * round_ + 16)
                wait(pool, w_used, n - 1)
                nc.gpsimd.tensor_tensor(wH[slot][:], raw[s][:], ones[:, 0:1].to_broadcast([P, D]),
                                        ALU.mult).then_inc(w_high, 1)
                pool.wait_ge(w_high, n + 1)
                nc.gpsimd.tensor_tensor(wL[slot][:], raw[s][:], wH[slot][:].bitcast(F32), ALU.subtract
                                        ).then_inc(w_ready, 1)

            pool.wait_ge(const_in, 16 * 2)
            for n in range(RAW):
                cut(n, n, 0)
            with pool.Fori(1, N_TILES // RAW) as i:
                for s in range(RAW):
                    cut(i * RAW + s, s, i)
            for n in range(N_TILES // RAW * RAW, N_TILES):
                cut(n, n % RAW, n // RAW)

        @block.tensor
        def _(pe):
            mm = nc.tensor.matmul

            def triple(bank, wh, wl, xh, xl, start, stop):
                mm(bank, wh, xh, start=start, stop=False)
                mm(bank, wh, xl, start=False, stop=False)
                return mm(bank, wl, xh, start=False, stop=stop)

            def cols_part(slot, bank, half, k0, k1):
                for k in range(k0, k1):
                    last = triple(ps[:, bank, :], wH[slot][:, k * P:(k + 1) * P],
                                  wL[slot][:, k * P:(k + 1) * P], uH[:, k, tok(half)],
                                  uL[:, k, tok(half)], k == 0, k == KT - 1)
                return last

            def rows_unit(slot, bank, fl, xh, xl, half):
                for k in range(2):
                    w = slice(k * 4 * P + fl * P, k * 4 * P + (fl + 1) * P)
                    last = triple(ps[:, bank, :], wH[slot][:, w], wL[slot][:, w],
                                  xh[:, k, tok(half)], xl[:, k, tok(half)], k == 0, k == 1)
                return last

            def means(nm):
                pe.wait_ge(nm.sum_done, 2 * (KT - 1))
                for t in range(2):
                    mm(ps[:, 6 + t, :], mean_of, ssum[:, t, :], start=True, stop=True
                       ).then_inc(nm.mean_done, 1)

            def ffn(s, n0, nm, order):
                def tile_no(i, j):
                    return n0 + 4 + 6 * (i - 1) + j if not isinstance(i, int) or i > 0 else n0 + j

                def p1(i, first=False, second=False):
                    for j in range(2):
                        for side in range(2):
                            n = tile_no(i, 2 * j + side)
                            slot = (n0 + side) % 2
                            pe.wait_ge(w_ready, n + 1)
                            for t in range(2):
                                u = 4 * j + 2 * side + t
                                if second:
                                    pe.wait_ge(s.gate_done if side else s.as_done, 2 * j + t + 1)
                                elif first and u >= 6:
                                    pe.wait_ge(nm.root_done, t + 1)
                                elif not first:
                                    pe.wait_ge(s.acc_done, 16 * (i - 2) + 8 + u + 1)
                                if first and j == 0 and side == 0:
                                    for k in range(KT):
                                        pe.wait_ge(nm.ul_done, order(k, t) + 1)
                                        last = cols_part(slot, u, t, k, k + 1)
                                else:
                                    last = cols_part(slot, u, t, 0, KT)
                                if t == 0:
                                    last.then_inc(s.b_done if side else s.a_done, 1)
                                else:
                                    last.then_inc(w_used, 1)
                        if first and j == 0:
                            means(nm)

                def p2(g, par, n, i=None):
                    pe.wait_ge(s.hl_done, 4 * (g + 1))
                    for v in range(16):
                        c, t, fl = v // 8, v % 8 // 4, v % 4
                        if v % 8 == 0:
                            pe.wait_ge(w_ready, n + c + 1)
                        if v < 8 and i is not None:
                            idx = 4 * i + 2 * (v // 4) + v % 2 + 1
                            pe.wait_ge(s.gate_done if v % 4 // 2 else s.as_done, idx)
                        elif v < 8:
                            pe.wait_ge(s.acc_done, 16 * (g - 1) + 8 + v + 1)
                        else:
                            pe.wait_ge(s.acc_done, 16 * g + v - 8 + 1)
                        last = rows_unit((n0 + c) % 2, v % 8, fl, hidH[:, par], hidL[:, par], t)
                        last.then_inc(w_used if v % 8 == 7 else s.p2_done, 1)

                p1(0, first=True)
                p1(1, second=True)
                p2(0, 0, tile_no(1, 4), 1)
                with pe.Fori(1, FFG // 2) as c:
                    for par in range(2):
                        i = c * 2 + par
                        p1(i)
                        p2(i - 1, 1 - par, tile_no(i, 4), i)
                i = FFG - 1
                p1(i)
                p2(i - 1, (i - 1) % 2, tile_no(i, 4), i)
                p2(i, i % 2, tile_no(i, 4) + 2)

            def out_transposes(s, hp, half):
                pe.wait_ge(s.on_done, 2 * hp + half + 1)
                for d in range(2):
                    if half == 0:
                        pe.wait_ge(s.st_ev if d else s.o_ev, (7 if d else 8) * (hp + 1))
                    else:
                        pe.wait_ge(s.g_done, 4 * hp + d + 1)
                    for b in range(NBH):
                        last = nc.tensor.transpose(ps[:, 6 + d, b * BLK:(b + 1) * BLK],
                                                   on[:, half * NBH + b, d * P:(d + 1) * P], ident)
                    last.then_inc(s.ot_done, 1)

            def branch_unit(s, hp, n0, slot, v, n_tile, tail=False):
                c, t, fl = v // 8, v % 8 // 4, v % 4
                if v % 8 == 0:
                    pe.wait_ge(w_ready, n_tile + 1)
                if v == 0:
                    pe.wait_ge(s.ol_done, 4 * (hp + 1))
                if v < 4:
                    if tail:
                        pe.wait_ge(s.r_sc, 4 * HEADS - 3 + v)
                    else:
                        pe.wait_ge(s.v_ev, 4 * (hp + 1) + v + 1)
                else:
                    pe.wait_ge(s.b_ev, 16 * hp + v - 4 + 1)
                last = rows_unit(slot, v % 4, fl, ogH, ogL, t)
                last.then_inc(w_used if v % 8 == 7 else s.b_part, 1)

            def branch(s, n0, gla, nm):
                items = NLV + 2 if gla else 2
                n_sc = NLV + 1 if gla else 1

                def window(hd, first):
                    nw = n0 if first else n0 + 6 + 8 * (hd - 1)
                    for step in range(STEPS):
                        tile, e = step // 8, step % 8
                        if tile in (B0, B1):
                            if not first:
                                branch_unit(s, hd - 1, n0, (n0 + tile) % 2, step - 8 * B0,
                                            nw + tile)
                        else:
                            n = nw + tile - (2 if first and tile > B1 else 0)
                            slot = (n0 + tile) % 2
                            t, q4 = e // 4, e % 4
                            if e == 0:
                                pe.wait_ge(w_ready, n + 1)
                            bank = 2 * (tile % 2) + t
                            if q4 == 0:
                                if tile in (Q, K) and nm is not None and first:
                                    pe.wait_ge(f1.acc_done, 16 * (FFG - 1) + 8 + bank + 1)
                                elif tile in (Q, K):
                                    wait(pe, s.r_sc, 4 * hd - 3 + bank if not first else 0)
                                elif tile == V0:
                                    pe.wait_ge(s.q_ev, 2 * hd + t + 1)
                                elif tile == V1:
                                    pe.wait_ge(s.k_ev, 2 * hd + t + 1)
                                elif first:
                                    pe.wait_ge(s.v_ev, bank + 1)
                                else:
                                    pe.wait_ge(s.b_ev, 16 * (hd - 1) + 12 + bank + 1)
                            if first and tile == Q and nm is not None:
                                for k in range(2 * q4, 2 * q4 + 2):
                                    pe.wait_ge(nm.ul_done, place(k, t) + 1)
                                    last = cols_part(slot, bank, t, k, k + 1)
                            else:
                                last = cols_part(slot, bank, t, 2 * q4, 2 * q4 + 2)
                            if e == 3:
                                last.then_inc(s.half_done, 1)
                            elif e == 7:
                                last.then_inc(w_used, 1)
                            if first and nm is not None and step == 7:
                                means(nm)
                        if gla and step == 1:
                            pe.wait_ge(s.headc_done, hd + 1)
                            pe.wait_ge(lr_ev, 2)
                            wait(pe, s.sc_ev, 16 * hd)
                            wait(pe, s.kt_ev, 2 * hd)
                            for t in range(2):
                                mm(ps[:, 4 + t, :], w2h[:], lrT[:, tok(t)], start=True, stop=True
                                   ).then_inc(z_done, 1)
                        if step in (3, 11) and not first:
                            out_transposes(s, hd - 1, step // 8)
                        if step in (22, 26, 30, 34):
                            v = (step - 22) // 4
                            pe.wait_ge(s.v_ev, 4 * hd + v + 1)
                            if v < 2:
                                wait(pe, s.g_done, 4 * hd - 2 + v + 1 if not first else 0)
                                if first and nm is not None:
                                    pe.wait_ge(nm.root_done, 2)
                            else:
                                pe.wait_ge(s.vt_ev, 4 * hd + v - 2 + 1)
                            for b in range(NBH):
                                last = nc.tensor.transpose(ps[:, 6 + v % 2, b * BLK:(b + 1) * BLK],
                                                           vS[:, v % 2, b * BLK:(b + 1) * BLK], ident)
                            last.then_inc(s.vt_done, 1)
                        for half in range(2):
                            for item in range(NLV + 2):
                                if step == score_step(half, item):
                                    scores(hd, half, item)
                            for b in range(NBH):
                                if step == block_step(half, b):
                                    block_out(hd, half * NBH + b)

                def scores(hd, half, item):
                    if not gla and item not in (LAST, DIAG):
                        return
                    g = half * (NLV + 2) + item
                    bank = 4 + g % 2
                    sc0 = 2 * n_sc * hd + n_sc * half
                    if gla:
                        if item == DIAG:
                            pe.wait_ge(s.sc_ev, sc0 + NLV)
                        elif g == 0:
                            pe.wait_ge(zln_done, 2 * hd + 2)
                            pe.wait_ge(zmin_done, 2 * hd + 2)
                        elif g == 1:
                            pass
                        elif item == 0:
                            pe.wait_ge(s.kt_ev, 2 * hd + half)
                        elif item == 1:
                            pe.wait_ge(s.sc_ev, sc0)
                        else:
                            pe.wait_ge(s.sc_ev, sc0 + item - 1)
                    else:
                        wait(pe, s.kt_ev, 2 * hd + half)
                        wait(pe, s.sc_ev, sc0)
                    if item < NLV or item == LAST:
                        if gla:
                            pe.wait_ge(prod_done, 2 * (NLV + 2) * hd + g + 1)
                        else:
                            pe.wait_ge(s.k_ev, 2 * hd + half + 1)
                    if item == DIAG:
                        pe.wait_ge(s.q_ev, 2 * hd + half + 1)
                        pe.wait_ge(s.k_ev, 2 * hd + half + 1)
                    for b in range(NBH):
                        blk = slice(b * BLK, (b + 1) * BLK)
                        tb = slice(half * HF + b * BLK, half * HF + (b + 1) * BLK)
                        if item == LAST:
                            src = kE[:, item % 2, blk] if gla else kT[:, tb]
                            last = nc.tensor.transpose(ps[:, bank, blk], src, ident)
                        elif item == DIAG:
                            last = mm(ps[:, bank, blk], kT[:, tb], qT[:, tb], start=True, stop=True)
                        else:
                            last = mm(ps[:, bank, blk], kE[:, item % 2, blk], qE[:, item % 2, blk],
                                      start=True, stop=True)
                    last.then_inc(s.kt_done if item == LAST else s.sc_done, 1)

                def block_out(hd, b):
                    half, bb = b // NBH, b % NBH
                    hb = slice(b % 2 * DV, (b % 2 + 1) * DV)
                    o, st = ps[:, 6, hb], ps[:, 7, hb]
                    if bb == 0:
                        pe.wait_ge(s.sc_ev, 2 * n_sc * hd + n_sc * (half + 1))
                        pe.wait_ge(s.kt_ev, 2 * hd + half + 1)
                        if gla:
                            pe.wait_ge(prod_done, (NLV + 2) * (2 * hd + half + 1))
                        else:
                            pe.wait_ge(s.qd_done, 2 * hd + half + 1)
                    if b == 0:
                        pe.wait_ge(s.vt_ev, 4 * hd + 4)
                    if b >= 1:
                        pe.wait_ge(s.o_ev, 8 * hd + b)
                    mm(o, ss[:, half, bb, :], vtok[:, b, :], start=True, stop=False)
                    if b > 0:
                        pe.wait_ge(s.st_ev, 7 * hd + b)
                    mm(o, qd[:, bb, :], state[:, b % 2, :], start=False, stop=True
                       ).then_inc(s.o_done, 1)
                    if b < 2 * NBH - 1:
                        mm(st, ktok[:, bb, :], vtok[:, b, :], start=True, stop=True
                           ).then_inc(s.st_done, 1)

                if gla:
                    pe.wait_ge(lr_ev, 2)
                window(0, True)
                with pe.Fori(1, HEADS) as hd:
                    window(hd, False)

            def branch_tail(s, n0):
                hp = HEADS - 1
                nb = n0 + 6 + 8 * hp
                out_transposes(s, hp, 0)
                out_transposes(s, hp, 1)
                for v in range(16):
                    branch_unit(s, hp, n0, (n0 + v // 8) % 2, v, nb + v // 8, tail=True)

            def cols_tile(n, free, unit0):
                pe.wait_ge(w_ready, n + 1)
                for t in range(2):
                    free(t)
                    last = cols_part(n % 2, unit0 + t, t, 0, KT)
                    last.then_inc(w_used if t else cols_half, 1)

            pe.wait_ge(const_in, 16 * 2)
            ffn(f1, N_F1, norm1, lambda k, t: KT * t + k)
            branch(ret_s, N_RET, False, norm2)
            branch_tail(ret_s, N_RET)
            for f in range(KT):
                b0 = 2 * (f % 2)
                cols_tile(N_GA + f,
                          lambda t: pe.wait_ge(ga_sc, 2 * f - 3 + t) if f >= 2 else
                          pe.wait_ge(ret_s.b_ev, 16 * HEADS - 4 + b0 + t + 1), b0)
            cols_tile(N_LR, lambda t: pe.wait_ge(ga_sc, 2 * KT - 3 + t), 0)
            branch(gla_s, N_GLA, True, None)
            branch_tail(gla_s, N_GLA)
            for f in range(KT):
                b0 = 2 * (f % 2)
                cols_tile(N_GB + f,
                          lambda t: pe.wait_ge(gb_sc, 2 * f - 3 + t) if f >= 2 else
                          pe.wait_ge(gla_s.b_ev, 16 * HEADS - 4 + b0 + t + 1), b0)
            for f in range(KT):
                b0 = 2 * (f % 2)

                def free(t):
                    if f == 0:
                        pe.wait_ge(ml_done, KT * (t + 1))
                    pe.wait_ge(*((wo_ev, 2 * f - 3 + t) if f >= 2 else (gb_sc, 2 * KT - 3 + b0 + t)))
                cols_tile(N_OUT + f, free, b0)
            ffn(f2, N_F2, norm3, lambda k, t: KT * t + k)
            means(norm4)

        @block.scalar
        def _(act):
            A = nc.scalar.activation

            def high(nm, f, t, wcol):
                A(uH[:, f, tok(t)], h[:, f, tok(t)], ACT.Copy,
                  scale=normw[:, wcol * KT + f:wcol * KT + f + 1]).then_inc(nm.uh_done, 1)

            def square(nm, count, f, t):
                if f == 0:
                    A(ssum[:, t, :], h[:, f, tok(t)], ACT.Square).then_inc(nm.sq_done, 1)
                    return count
                wait(act, nm.sum_done, count - 1)
                A(sq[:, count % 2, :], h[:, f, tok(t)], ACT.Square).then_inc(nm.sq_done, 1)
                return count + 1

            def roots(nm):
                for t in range(2):
                    act.wait_ge(nm.mean_done, t + 1)
                    A(rinv[:, t, :], ps[:, 6 + t, :], ACT.Sqrt, bias=eps).then_inc(nm.root_done, 1)

            def after_ffn(s, nm, wcol):
                count = 0
                for v in range(16):
                    f, t = 4 * (v // 8) + v % 4, v % 8 // 4
                    act.wait_ge(s.acc_done, 16 * (FFG - 1) + v + 1)
                    if wcol is not None:
                        high(nm, f, t, wcol)
                    count = square(nm, count, f, t)

            def ffn(s, n0):
                def p1(i, par, first=False, second=False):
                    for j in range(2):
                        for t in range(2):
                            idx = 4 * i + 2 * j + t
                            act.wait_ge(s.as_done, idx + 1)
                            A(sil[:, t, :], sil[:, t, :], ACT.Silu).then_inc(s.silu_done, 1)
                        for t in range(2):
                            idx = 4 * i + 2 * j + t
                            act.wait_ge(s.gate_done, idx + 1)
                            if not first and not second and j == 0 and t == 0:
                                act.wait_ge(w_used, n0 + 4 + 6 * (i - 1))
                            A(hidH[:, par, j, tok(t)], hidf[:, t, :], ACT.Copy).then_inc(s.hh_done, 1)

                p1(0, 0, first=True)
                p1(1, 1, second=True)
                with act.Fori(1, FFG // 2) as c:
                    for par in range(2):
                        p1(c * 2 + par, par)
                p1(FFG - 1, (FFG - 1) % 2)

            def gate_high(s, hp, half, n_before):
                for d in range(2):
                    act.wait_ge(s.g_done, 4 * hp + 2 * half + d + 1)
                    if half == 0 and d == 0:
                        act.wait_ge(w_used, n_before)
                    A(ogH[:, d, tok(half)], ogf[:, d, :], ACT.Copy).then_inc(s.oh_done, 1)

            def branch(s, n0, gla):
                def window(hd, first):
                    nw = n0 if first else n0 + 6 + 8 * (hd - 1)

                    for step in range(STEPS + 1):
                        if gla and step == 2:
                            act.wait_ge(s.headc_done, hd + 1)
                            for t in range(2):
                                act.wait_ge(z_done, 2 * hd + t + 1)
                                wait(act, prod_done, 2 * (NLV + 2) * hd)
                                A(ee[:, t, :], ps[:, 4 + t, :], ACT.Abs, bias=headc[:, 2:3]
                                  ).then_inc(zabs_done, 1)
                            for t in range(2):
                                act.wait_ge(zabs_done, 2 * hd + t + 1)
                                A(ee[:, t, :], ee[:, t, :], ACT.Exp, scale=-1.0).then_inc(zexp_done, 1)
                            for t in range(2):
                                act.wait_ge(zexp_done, 2 * hd + t + 1)
                                A(ee[:, t, :], ee[:, t, :], ACT.Ln, bias=ones[:, 0:1]
                                  ).then_inc(zln_done, 1)
                        if step in (3, 11) and not first:
                            gate_high(s, hd - 1, step // 8, nw)
                        if step in (22, 26, 30, 34):
                            v = (step - 22) // 4
                            act.wait_ge(s.vt_done, 4 * hd + v + 1)
                            t, d = v % 2, v // 2
                            A(vtok[:, t * NBH:(t + 1) * NBH, d * P:(d + 1) * P],
                              ps[:, 6 + v % 2, :].rearrange("p (b c) -> p b c", b=NBH), ACT.Copy
                              ).then_inc(s.vt_ev, 1)
                        for half in range(2):
                            for item in range(NLV + 2):
                                if gla and step == score_step(half, item) - 3:
                                    exps(hd, half, item)
                                if step == score_step(half, item) and item == LAST:
                                    act.wait_ge(s.kt_done, 2 * hd + half + 1)
                                    wait(act, s.o_done, 8 * hd + 4 * half)
                                    wait(act, s.st_done, 7 * hd + 4 * half)
                                    g = half * (NLV + 2) + item
                                    src = ps[:, 4 + g % 2, :].rearrange("p (b c) -> p b c", b=NBH)
                                    if not gla:
                                        act.wait_ge(s.headc_done, hd + 1)
                                    A(ktok[:], src, ACT.Copy, scale=1.0 if gla else headc[:, 0:1]
                                      ).then_inc(s.kt_ev, 1)
                            for b in range(NBH):
                                if step == block_step(half, b):
                                    bb = half * NBH + b
                                    act.wait_ge(s.o_done, 8 * hd + bb + 1)
                                    if bb == 0:
                                        wait(act, s.ot_done, 4 * hd)
                                    A(on[:, bb, :], ps[:, 6, bb % 2 * DV:(bb % 2 + 1) * DV], ACT.Copy
                                      ).then_inc(s.o_ev, 1)
                            if step == block_step(half, NBH - 1) + 2:
                                act.wait_ge(s.var_done, 2 * hd + half + 1)
                                A(sd[:], ve[:], ACT.Sqrt).then_inc(s.sd_done, 1)
                        if step in (52, 56, 60, 64):
                            v = (step - 52) // 4
                            act.wait_ge(s.r_sc, 4 * hd + v + 1)
                            x = rS[:, v // 2, tok(v % 2)]
                            A(x, x, ACT.Silu).then_inc(s.r_ev, 1)

                def exps(hd, half, item):
                    gi = half * (NLV + 2) + item
                    e = ee[:, gi % 2, :]
                    if item <= LAST:
                        act.wait_ge(diff_done, 2 * (NLV + 1) * hd + half * (NLV + 1) + item + 1)
                    if item < NLV:
                        w = LEVELS[item]
                        v = e.rearrange("p (n s) -> p n s", s=2 * w)
                        A(v[:, :, 0:w], v[:, :, 0:w], ACT.Exp, scale=-1.0 / TAU)
                        A(v[:, :, w:], v[:, :, w:], ACT.Exp, scale=1.0 / TAU).then_inc(exp_done, 1)
                    elif item == LAST:
                        A(e, e, ACT.Exp, scale=-1.0 / TAU).then_inc(exp_done, 1)
                    else:
                        act.wait_ge(prod_done, 2 * (NLV + 2) * hd + gi - 1)
                        A(e, bc[:, tok(half)], ACT.Exp, scale=1.0 / TAU).then_inc(exp_done, 1)

                window(0, True)
                with act.Fori(1, HEADS) as hd:
                    window(hd, False)
                for half in range(2):
                    gate_high(s, HEADS - 1, half, n0 + BRANCH_TILES - 2)

            act.dma_start(smallt[:], small).then_inc(const_in, 16)
            act.dma_start(normw[:], norms).then_inc(const_in, 16)
            for f in range(KT):
                act.dma_start(h[:, f, tok(0)], xT[:, f, tok(0)]).then_inc(h_in[f], 16)
            for i in range(2):
                part = slice(i * KT // 2, (i + 1) * KT // 2)
                act.dma_start(h[:, part, tok(1)], xT[:, part, tok(1)]).then_inc(x_rest_in[i], 16)
            act.dma_start(gbt[:], gate_b).then_inc(late_in, 16)
            act.dma_start(rett[:], ret).then_inc(late_in, 16)
            act.dma_start(maskf[:], masks).then_inc(late_in, 16)
            act.dma_start(w2t[:], gate_w2).then_inc(late_in, 16)
            act.dma_start(ropet[:], rope).then_inc(late_in, 16)
            act.wait_ge(const_in, 16 * 2)
            for t in range(2):
                for f in range(KT):
                    act.wait_ge(x_rest_in[f // 4] if t else h_in[f], 16)
                    high(norm1, f, t, 0)
            count = 0
            for t in range(2):
                for f in range(KT):
                    count = square(norm1, count, f, t)
            roots(norm1)
            ffn(f1, N_F1)
            after_ffn(f1, norm2, 1)
            act.dma_start(h_spill, h[:]).then_inc(h_saved, 16)
            roots(norm2)
            act.wait_ge(h_saved, 16)
            branch(ret_s, N_RET, False)
            for f in range(KT):
                for t in range(2):
                    idx = 2 * f + t
                    act.wait_ge(ga_sc, idx + 1)
                    A(vS[:, t, :], vS[:, t, :], ACT.Sigmoid).then_inc(ga_sig, 1)
                if f >= 1:
                    act.wait_ge(ga_ev, 2 * f)
                    act.dma_start(y_spill[:, f - 1, :], y[:, f - 1, :]).then_inc(y_saved, 16)
            act.wait_ge(ga_ev, 2 * KT)
            act.dma_start(y_spill[:, KT - 1, :], y[:, KT - 1, :]).then_inc(y_saved, 16)
            branch(gla_s, N_GLA, True)
            yr = vtok[:].rearrange("p b c -> p (b c)").rearrange("p (s t) -> p s t", s=2)
            act.wait_ge(y_saved, 16 * KT)
            for f in range(2):
                act.dma_start(yr[:, f, :], y_spill[:, f, :]).then_inc(y_back[f], 16)
            act.wait_ge(w_used, N_GB)
            for f in range(KT):
                act.dma_start(h[:, f, :], h_spill[:, f, :]).then_inc(h_in[f], 16)
            for f in range(KT):
                for t in range(2):
                    idx = 2 * f + t
                    act.wait_ge(gb_sc, idx + 1)
                    A(vS[:, t, :], vS[:, t, :], ACT.Sigmoid).then_inc(gb_sig, 1)
                if 1 <= f < KT - 1:
                    act.wait_ge(gb_ev, 2 * f)
                    act.dma_start(yr[:, (f + 1) % 2, :], y_spill[:, f + 1, :]
                                  ).then_inc(y_back[(f + 1) % 2], 16)
            act.wait_ge(w_used, N_GB + KT)
            for t in range(2):
                for f in range(KT):
                    act.wait_ge(gb_ev, 2 * f + t + 1)
                    A(uH[:, f, tok(t)], y[:, f, tok(t)], ACT.Copy).then_inc(mh_done, 1)
            count = 0
            for f in range(KT):
                for t in range(2):
                    act.wait_ge(wo_ev, 2 * f + t + 1)
                    count = square(norm3, count, f, t)
            act.wait_ge(w_used, N_F2)
            for t in range(2):
                for f in range(KT):
                    high(norm3, f, t, 2)
            roots(norm3)
            ffn(f2, N_F2)
            after_ffn(f2, norm4, None)
            roots(norm4)
            for t in range(2):
                for f in range(KT):
                    act.wait_ge(y_done, KT * t + f + 1)
                    act.dma_start(out[:, f, tok(t)], h[:, f, tok(t)]).then_inc(out_saved, 16)
            act.wait_ge(out_saved, 16 * 2 * KT)

        @block.vector
        def _(dve):
            V = nc.vector

            def low(nm, count, f, t, wcol):
                dve.wait_ge(nm.uh_done, count + 1)
                V.scalar_tensor_tensor(out=uL[:, f, tok(t)], in0=h[:, f, tok(t)],
                                       scalar=normw[:, wcol * KT + f:wcol * KT + f + 1],
                                       in1=uH[:, f, tok(t)].bitcast(F32), op0=ALU.mult,
                                       op1=ALU.subtract).then_inc(nm.ul_done, 1)

            def add_square(nm, nth, count, f, t):
                if f == 0:
                    return count
                dve.wait_ge(nm.sq_done, nth + 1)
                wait(dve, nm.sum_done, count)
                V.tensor_tensor(ssum[:, t, :], ssum[:, t, :], sq[:, count % 2, :], ALU.add
                                ).then_inc(nm.sum_done, 1)
                return count + 1

            def inverses(nm):
                for t in range(2):
                    dve.wait_ge(nm.root_done, t + 1)
                    V.reciprocal(rinv[:, t, :], rinv[:, t, :]).then_inc(nm.inv_done, 1)
                dve.wait_ge(nm.inv_done, 2)

            def scaled(out_, bank, t, scale=None, parts=P):
                r = rinv[0:parts, t, :]
                if scale is None:
                    return V.tensor_tensor(out_, ps[0:parts, bank, :], r, ALU.mult)
                return V.scalar_tensor_tensor(out=out_, in0=ps[0:parts, bank, :], scalar=scale, in1=r,
                                              op0=ALU.mult, op1=ALU.mult)

            def ffn(s, n0, nm, wcol):
                def p1(i, par, first=False):
                    for j in range(2):
                        n = n0 + 2 * j + 1 if first else n0 + 4 + 6 * (i - 1) + 2 * j + 1
                        for t in range(2):
                            idx = 4 * i + 2 * j + t
                            if t == 0:
                                dve.wait_ge(s.a_done, 2 * i + j + 1)
                            else:
                                dve.wait_ge(w_used, n)
                            wait(dve, s.gate_done, idx - 1)
                            scaled(sil[:, t, :], 4 * j + t, t).then_inc(s.as_done, 1)
                        for t in range(2):
                            idx = 4 * i + 2 * j + t
                            dve.wait_ge(s.silu_done, idx + 1)
                            V.tensor_tensor(sil[:, t, :], sil[:, t, :], rinv[:, t, :], ALU.mult
                                            ).then_inc(s.sr_done, 1)
                        for t in range(2):
                            idx = 4 * i + 2 * j + t
                            if t == 0:
                                dve.wait_ge(s.b_done, 2 * i + j + 1)
                            else:
                                dve.wait_ge(w_used, n + 1)
                            dve.wait_ge(s.sr_done, idx + 1)
                            wait(dve, s.hl_done, idx - 1)
                            V.tensor_tensor(hidf[:, t, :], sil[:, t, :], ps[:, 4 * j + 2 + t, :],
                                            ALU.mult).then_inc(s.gate_done, 1)
                            dve.wait_ge(s.hh_done, idx + 1)
                            V.tensor_tensor(hidL[:, par, j, tok(t)], hidf[:, t, :],
                                            hidH[:, par, j, tok(t)].bitcast(F32), ALU.subtract
                                            ).then_inc(s.hl_done, 1)

                def p2(g, n, after=None):
                    for v in range(16):
                        c, t, fl = v // 8, v % 8 // 4, v % 4
                        f = 4 * c + fl
                        if v % 8 == 7:
                            dve.wait_ge(w_used, n + c + 1)
                        else:
                            dve.wait_ge(s.p2_done, 14 * g + 7 * c + v % 8 + 1)
                        wait(dve, s.acc_done, 16 * (g - 1) + v + 1)
                        V.scalar_tensor_tensor(out=h[:, f, tok(t)], in0=ps[:, v % 8, :], scalar=0.5,
                                               in1=h[:, f, tok(t)], op0=ALU.mult, op1=ALU.add
                                               ).then_inc(s.acc_done, 1)
                        if after is not None and v:
                            after(v - 1)
                    if after is not None:
                        after(15)

                p1(0, 0, first=True)
                p1(1, 1)
                p2(0, n0 + 8)
                with dve.Fori(1, FFG // 2) as c:
                    for par in range(2):
                        i = c * 2 + par
                        p1(i, par)
                        p2(i - 1, n0 + 8 + 6 * (i - 1))
                i = FFG - 1
                p1(i, i % 2)
                p2(i - 1, n0 + 8 + 6 * (i - 1))
                count = [0]

                def norm_part(v):
                    f, t = 4 * (v // 8) + v % 4, v % 8 // 4
                    if wcol is not None:
                        low(nm, v, f, t, wcol)
                    count[0] = add_square(nm, v, count[0], f, t)

                p2(i, n0 + 8 + 6 * (i - 1) + 2, norm_part)

            def gate(s, hp, half, gla):
                for d in range(2):
                    idx = 4 * hp + 2 * half + d
                    dve.wait_ge(s.ot_done, idx + 1)
                    dve.wait_ge(s.r_ev, 4 * hp + 4)
                    if half:
                        dve.wait_ge(s.ol_done, idx - 1)
                    o = ogf[:, d, :]
                    if gla:
                        V.scalar_tensor_tensor(out=o, in0=ps[:, 6 + d, :],
                                               scalar=normw[:, 4 * KT + d:4 * KT + d + 1],
                                               in1=rS[:, d, tok(half)], op0=ALU.mult, op1=ALU.mult
                                               ).then_inc(s.g_done, 1)
                    else:
                        V.tensor_tensor(o, ps[:, 6 + d, :], rS[:, d, tok(half)], ALU.mult
                                        ).then_inc(s.g_done, 1)
                for d in range(2):
                    idx = 4 * hp + 2 * half + d
                    dve.wait_ge(s.oh_done, idx + 1)
                    V.tensor_tensor(ogL[:, d, tok(half)], ogf[:, d, :],
                                    ogH[:, d, tok(half)].bitcast(F32), ALU.subtract
                                    ).then_inc(s.ol_done, 1)

            def branch_add(s, hp, v, n_tile, n_before):
                c, t, fl = v // 8, v % 8 // 4, v % 4
                f = 4 * c + fl
                if v % 8 == 7:
                    dve.wait_ge(w_used, n_tile + 1)
                else:
                    dve.wait_ge(s.b_part, 14 * hp + 7 * c + v % 8 + 1)
                if v == 0:
                    dve.wait_ge(w_used, n_before)
                V.tensor_tensor(y[:, f, tok(t)], ps[:, v % 4, :], y[:, f, tok(t)], ALU.add
                                ).then_inc(s.b_ev, 1)

            def branch(s, n0, gla):
                n_sc = NLV + 1 if gla else 1
                per_window = 1 + 2 * NBH + (2 * 3 + 2 if gla else 2 * 2 + 4)

                def window(hd, first):
                    nw = n0 if first else n0 + 6 + 8 * (hd - 1)
                    base = 0 if first else per_window * hd
                    count = [0]

                    def link(ins):
                        count[0] += 1
                        ins.then_inc(s.chain, 1)
                        dve.wait_ge(s.chain, base + count[0])

                    for step in range(STEPS + 1):
                        if step == 0:
                            wait(dve, s.kt_ev, 2 * hd)
                            wait(dve, s.st_ev, 7 * hd)
                            if gla:
                                wait(dve, zmin_done, 2 * hd)
                                wait(dve, z_done, 2 * hd)
                                wait(dve, zabs_done, 2 * hd)
                                V.tensor_copy(w2h[:], w2t[:, bass.ds(hd * DK, DK)])
                                V.tensor_copy(headc[:, 2:3], gbt[:, bass.ds(hd, 1)]
                                              ).then_inc(s.headc_done, 1)
                            else:
                                V.tensor_copy(headc[:, 0:2], rett[:, bass.ds(hd, 1), 2 * BLK:RETC]
                                              .rearrange("p a c -> p (a c)")).then_inc(s.headc_done, 1)
                            wait(dve, s.o_done, 8 * hd)
                            link(V.memset(state[:, 0, :], 0.0))
                            dve.wait_ge(s.headc_done, hd + 1)
                            if first:
                                V.memset(y[:], 0.0).then_inc(s.y_clear, 1)
                                dve.wait_ge(s.y_clear, 1)
                            if first and not gla:
                                inverses(norm2)
                                for part in range(2):
                                    for t in range(2):
                                        x = ropet[:, part, tok(t)]
                                        ins = V.tensor_tensor(x, x, rinv[:, t, :], ALU.mult)
                                ins.then_inc(rope_done, 1)
                                dve.wait_ge(rope_done, 1)
                        if gla and step == 2:
                            for t in range(2):
                                dve.wait_ge(zabs_done, 2 * hd + t + 1)
                                wait(dve, exp_done, 2 * (NLV + 2) * hd)
                                wait(dve, diff_done, 2 * (NLV + 1) * hd)
                                V.tensor_scalar(bc[:, tok(t)], ps[:, 4 + t, :], headc[:, 2:3], 0.0,
                                                ALU.add, ALU.min).then_inc(zmin_done, 1)
                            for t in range(2):
                                dve.wait_ge(zln_done, 2 * hd + t + 1)
                                dve.wait_ge(zmin_done, 2 * hd + t + 1)
                                ins = V.tensor_tensor(ee[:, t, :], bc[:, tok(t)], ee[:, t, :],
                                                      ALU.subtract)
                                link(ins)
                            for b in range(2 * NBH):
                                ins = V.tensor_tensor_scan(bc[:, b * BLK:(b + 1) * BLK], ones,
                                                           ee[:, b // NBH,
                                                              b % NBH * BLK:(b % NBH + 1) * BLK],
                                                           0.0, ALU.mult, ALU.add)
                            ins.then_inc(cum_done, 1)
                            dve.wait_ge(cum_done, hd + 1)
                        if step in (3, 11) and not first:
                            gate(s, hd - 1, step // 8, gla)
                        if gla and step in (4, 8, 12, 16):
                            t = 0 if step in (4, 12) else 1
                            isk = step >= 12
                            if t == 0:
                                dve.wait_ge(s.half_done, 6 * hd + (2 if isk else 1))
                            else:
                                dve.wait_ge(w_used, nw + (K if isk else Q) + 1)
                            if not isk:
                                wait(dve, s.o_done, 8 * hd)
                                scaled(qT[:, tok(t)], t, t, QK_SCALE).then_inc(s.q_ev, 1)
                            else:
                                scaled(kT[:, tok(t)], 2 + t, t).then_inc(s.k_ev, 1)
                        if step in (20, 24, 28, 32):
                            v = (step - 20) // 4
                            if v % 2 == 0:
                                dve.wait_ge(s.half_done, 6 * hd + 3 + v // 2)
                            else:
                                dve.wait_ge(w_used, nw + V0 + v // 2 + 1)
                            wait(dve, s.vt_done, 4 * hd + v - 1)
                            wait(dve, s.ol_done, 4 * hd)
                            scaled(vS[:, v % 2, :], v, v % 2).then_inc(s.v_ev, 1)
                        if step in (52, 56, 60, 64):
                            v = (step - 52) // 4
                            if v % 2 == 0:
                                dve.wait_ge(s.half_done, 6 * hd + 5 + v // 2)
                            else:
                                dve.wait_ge(w_used, nw + R0 + v // 2 + 1 - (2 if first else 0))
                            wait(dve, s.g_done, 4 * hd)
                            scaled(rS[:, v // 2, tok(v % 2)], v, v % 2).then_inc(s.r_sc, 1)
                        if not gla and step in (4, 8, 12, 16):
                            t = step // 4 % 2
                            t = 0 if step in (4, 12) else 1
                            isk = step >= 12
                            if t == 0:
                                dve.wait_ge(s.half_done, 6 * hd + (2 if isk else 1))
                            else:
                                dve.wait_ge(w_used, nw + (K if isk else Q) + 1)
                            if not isk:
                                wait(dve, s.o_done, 8 * hd)
                                wait(dve, s.qd_done, 2 * hd)
                            wait(dve, s.q_ev if step in (8, 12) else s.k_ev,
                                 2 * hd + {4: 0, 8: 1, 12: 2, 16: 1}[step])
                            x = ps[:, (2 if isk else 0) + t, :]
                            cos, sin = ropet[:, 0, tok(t)], ropet[:, 1, tok(t)]
                            V.tensor_tensor(rtmp[0:64, 0, :], x[64:128], sin[64:128], ALU.mult)
                            V.tensor_tensor(rtmp[64:128, 0, :], x[0:64], sin[0:64], ALU.mult)
                            link(V.tensor_tensor(rtmp[:, 1, :], x, cos, ALU.mult))
                            V.tensor_tensor((kT if isk else qT)[:, tok(t)], rtmp[:, 0, :],
                                            rtmp[:, 1, :], ALU.add
                                            ).then_inc(s.k_ev if isk else s.q_ev, 1)
                        for half in range(2):
                            for item in range(NLV + 2):
                                if step == score_step(half, item) - 2:
                                    if gla:
                                        gla_item(hd, half, item, link)
                                if step == score_step(half, item) + 1 and item == DIAG:
                                    if gla:
                                        score_in(hd, half, DIAG, link)
                                    else:
                                        ret_item(hd, half, link)
                            for b in range(NBH):
                                if step == block_step(half, b) + 1:
                                    block_in(hd, half * NBH + b, link)
                            if step == block_step(half, NBH - 1) + 2:
                                half_norm(hd, half, link)
                        if not first and 1 + 8 * B0 <= step < 1 + 8 * R0:
                            v = step - 1 - 8 * B0
                            branch_add(s, hd - 1, v, nw + B0 + v // 8, nw)
                    assert count[0] == per_window, (count[0], per_window)

                def ret_item(hd, half, link):
                    dve.wait_ge(s.sc_done, 2 * hd + half + 1)
                    wait(dve, s.o_done, 8 * hd)
                    pb = ps[:, 4 + (half * (NLV + 2) + DIAG) % 2, :].rearrange("p (b n) -> p b n", b=NBH)
                    for b in range(NBH):
                        last = V.tensor_tensor(ss[:, half, b, :], pb[:, b, :],
                                               rett[:, bass.ds(hd, 1), 0:BLK].rearrange("p a n -> p (a n)"),
                                               ALU.mult)
                    last.then_inc(s.sc_ev, 1)
                    wait(dve, s.o_done, 8 * hd + 4 * half)
                    dve.wait_ge(s.q_ev, 2 * hd + half + 1)
                    for b in range(NBH):
                        last = V.tensor_tensor(qd[:, b, :],
                                               qT[:, half * HF + b * BLK:half * HF + (b + 1) * BLK],
                                               rett[:, bass.ds(hd, 1), BLK:2 * BLK].rearrange("p a n -> p (a n)"),
                                               ALU.mult)
                    last.then_inc(s.qd_done, 1)

                def gla_item(hd, half, item, link):
                    if item == 0:
                        difference(hd, half, 0)
                    if item + 1 <= LAST:
                        difference(hd, half, item + 1)
                    g = half * (NLV + 2) + item
                    n = 2 * (NLV + 2) * hd + g
                    e = ee[:, g % 2, :]
                    dve.wait_ge(exp_done, n + 1)
                    dve.wait_ge(s.q_ev, 2 * hd + half + 1)
                    dve.wait_ge(s.k_ev, 2 * hd + half + 1)
                    q, k = qT[:, tok(half)], kT[:, tok(half)]
                    if item <= LAST:
                        if item == 0:
                            wait(dve, s.kt_done, 2 * hd + half)
                            wait(dve, s.sc_done, 2 * n_sc * hd + n_sc * half)
                        elif item >= 2:
                            dve.wait_ge(s.sc_done, 2 * n_sc * hd + n_sc * half + item - 1)
                    if item < NLV:
                        V.tensor_tensor(qE[:, item % 2, :], q, e, ALU.mult)
                        V.tensor_tensor(kE[:, item % 2, :], k, e, ALU.mult).then_inc(prod_done, 1)
                    elif item == LAST:
                        V.tensor_tensor(kE[:, item % 2, :], k, e, ALU.mult).then_inc(prod_done, 1)
                    else:
                        wait(dve, s.o_done, 8 * hd + 4 * half)
                        V.tensor_copy(bdec[:, half, :],
                                      e.rearrange("p (b n) -> p b n", b=NBH)[:, :, BLK - 1])
                        V.tensor_tensor(qd[:].rearrange("p b n -> p (b n)"), q, e, ALU.mult
                                        ).then_inc(prod_done, 1)
                        dve.wait_ge(prod_done, n + 1)
                    if 1 <= item <= NLV:
                        score_in(hd, half, item - 1, link)

                def difference(hd, half, item):
                    g = half * (NLV + 2) + item
                    wait(dve, prod_done, 2 * (NLV + 2) * hd + g - 1)
                    w = LEVELS[item] if item < NLV else BLK
                    n = 2 * w if item < NLV else BLK
                    b3 = bc[:, tok(half)].rearrange("p (n s) -> p n s", s=n)
                    ref = b3[:, :, w - 1:w].to_broadcast([P, HF // n, n])
                    V.tensor_tensor(ee[:, g % 2, :].rearrange("p (n s) -> p n s", s=n), b3, ref,
                                    ALU.subtract).then_inc(diff_done, 1)

                def score_in(hd, half, item, link):
                    sc = 2 * n_sc * hd + n_sc * half
                    order = item if item < NLV else NLV
                    dve.wait_ge(s.sc_done, sc + order + 1)
                    g = half * (NLV + 2) + item
                    pb = ps[:, 4 + g % 2, :].rearrange("p (b n) -> p b n", b=NBH)
                    o = ss[:, half]
                    if item == 0:
                        wait(dve, s.o_done, 8 * hd)
                        V.tensor_tensor(o, pb, mask0.unsqueeze(1).to_broadcast([P, NBH, BLK]), ALU.mult
                                        ).then_inc(s.sc_ev, 1)
                    else:
                        dve.wait_ge(s.sc_ev, sc + order)
                        mi = maskt[:, order:order + 1, :].to_broadcast([P, NBH, BLK])
                        carry()
                        V.copy_predicated(o, mi, pb).then_inc(s.sc_ev, 1)
                    if item == DIAG:
                        dve.wait_ge(prod_done, 2 * (NLV + 2) * hd + half * (NLV + 2) + NLV + 2)

                def block_in(hd, b, link):
                    half, bb = b // NBH, b % NBH
                    if gla and bb == 0:
                        dve.wait_ge(prod_done, (NLV + 2) * (2 * hd + half + 1))
                    if b < 2 * NBH - 1:
                        dve.wait_ge(s.st_done, 7 * hd + b + 1)
                        if b >= 1:
                            dve.wait_ge(s.st_ev, 7 * hd + b)
                        dve.wait_ge(s.o_done, 8 * hd + b + 1)
                        dec = bdec[:, half, bb:bb + 1] if gla else headc[:, 1:2]
                        V.scalar_tensor_tensor(out=state[:, (b + 1) % 2, :], in0=state[:, b % 2, :],
                                               scalar=dec,
                                               in1=ps[:, 7, b % 2 * DV:(b % 2 + 1) * DV],
                                               op0=ALU.mult, op1=ALU.add).then_inc(s.st_ev, 1)
                    dve.wait_ge(s.o_ev, 8 * hd + b + 1)
                    link(V.bn_stats(bst[:, bb, :], on[:, b, :]))

                def half_norm(hd, half, link):
                    wait(dve, s.on_done, 2 * hd + half)
                    carry()
                    for b in range(NBH):
                        ins = V.bn_aggr(mv[:, b, :], bst[:, b, :])
                    link(ins)
                    if gla:
                        link(V.tensor_tensor(ve[:], mv[:, :, 0], mv[:, :, 0], ALU.mult))
                        V.scalar_tensor_tensor(out=ve[:], in0=ve[:], scalar=EPS, in1=mv[:, :, 1],
                                               op0=ALU.add, op1=ALU.add).then_inc(s.var_done, 1)
                    else:
                        V.tensor_scalar(ve[:], mv[:, :, 1], EPS, None, ALU.add).then_inc(s.var_done, 1)
                    dve.wait_ge(s.sd_done, 2 * hd + half + 1)
                    link(V.reciprocal(rs[:], sd[:]))
                    for b in range(NBH):
                        o = on[:, half * NBH + b, :]
                        if gla:
                            ins = V.tensor_scalar(o, o, rs[:, b:b + 1], None, ALU.mult)
                        else:
                            ins = V.tensor_scalar(o, o, mv[:, b, 0:1], rs[:, b:b + 1], ALU.subtract,
                                                  ALU.mult)
                    ins.then_inc(s.on_done, 1)

                window(0, True)
                with dve.Fori(1, HEADS) as hd:
                    window(hd, False)
                hp = HEADS - 1
                gate(s, hp, 0, gla)
                gate(s, hp, 1, gla)
                nb = n0 + 6 + 8 * hp
                for v in range(16):
                    branch_add(s, hp, v, nb + v // 8, nb)

            dve.wait_ge(const_in, 16 * 2)
            for t in range(2):
                for f in range(KT):
                    low(norm1, KT * t + f, f, t, 0)
            count = 0
            for t in range(2):
                for f in range(KT):
                    count = add_square(norm1, KT * t + f, count, f, t)
            dve.wait_ge(late_in, 16 * 5)
            V.tensor_copy(maskt[:].rearrange("p s n -> p (s n)"), maskf[:].rearrange("p s n -> p (s n)")
                          ).then_inc(masks_done, 1)
            inverses(norm1)
            dve.wait_ge(masks_done, 1)
            ffn(f1, N_F1, norm2, 1)
            branch(ret_s, N_RET, False)

            def gate_scaled(n, f, t, halves, ev, sc_done):
                if t == 0:
                    dve.wait_ge(cols_half, halves + f + 1)
                else:
                    dve.wait_ge(w_used, n + f + 1)
                wait(dve, ev, 2 * f + t - 1)
                scaled(vS[:, t, :], 2 * (f % 2) + t, t).then_inc(sc_done, 1)

            for f in range(KT):
                for t in range(2):
                    gate_scaled(N_GA, f, t, 0, ga_ev, ga_sc)
                    idx = 2 * f + t
                    dve.wait_ge(ga_sig, idx + 1)
                    if idx == 0:
                        dve.wait_ge(ret_s.b_ev, 16 * HEADS)
                    V.tensor_tensor(y[:, f, tok(t)], y[:, f, tok(t)], vS[:, t, :], ALU.mult
                                    ).then_inc(ga_ev, 1)
            for t in range(2):
                if t == 0:
                    dve.wait_ge(cols_half, KT + 1)
                else:
                    dve.wait_ge(w_used, N_LR + 1)
                scaled(lrT[:, tok(t)], t, t, parts=16).then_inc(lr_ev, 1)
            dve.wait_ge(y_saved, 16 * KT)
            branch(gla_s, N_GLA, True)
            yr = vtok[:].rearrange("p b c -> p (b c)").rearrange("p (s t) -> p s t", s=2)
            for f in range(KT):
                for t in range(2):
                    gate_scaled(N_GB, f, t, KT + 1, gb_ev, gb_sc)
                    idx = 2 * f + t
                    dve.wait_ge(gb_sig, idx + 1)
                    if idx == 0:
                        dve.wait_ge(gla_s.b_ev, 16 * HEADS)
                    if t == 0:
                        dve.wait_ge(y_back[f % 2], 16 * (f // 2 + 1))
                    V.tensor_tensor(vS[:, t, :], y[:, f, tok(t)], vS[:, t, :], ALU.mult
                                    ).then_inc(gb_mul, 1)
                    dve.wait_ge(gb_mul, idx + 1)
                    V.tensor_tensor(y[:, f, tok(t)], vS[:, t, :], yr[:, f % 2, tok(t)], ALU.add
                                    ).then_inc(gb_ev, 1)
            for t in range(2):
                for f in range(KT):
                    dve.wait_ge(mh_done, KT * t + f + 1)
                    V.tensor_tensor(uL[:, f, tok(t)], y[:, f, tok(t)], uH[:, f, tok(t)].bitcast(F32),
                                    ALU.subtract).then_inc(ml_done, 1)
            count = 0
            for f in range(KT):
                for t in range(2):
                    if t == 0:
                        dve.wait_ge(cols_half, 2 * KT + 1 + f + 1)
                        dve.wait_ge(h_in[f], 32)
                    else:
                        dve.wait_ge(w_used, N_OUT + f + 1)
                    V.tensor_tensor(h[:, f, tok(t)], ps[:, 2 * (f % 2) + t, :], h[:, f, tok(t)],
                                    ALU.add).then_inc(wo_ev, 1)
                    count = add_square(norm3, 2 * f + t, count, f, t)
            for t in range(2):
                for f in range(KT):
                    low(norm3, KT * t + f, f, t, 2)
            inverses(norm3)
            ffn(f2, N_F2, norm4, None)
            inverses(norm4)
            for t in range(2):
                for f in range(KT):
                    V.scalar_tensor_tensor(out=h[:, f, tok(t)], in0=h[:, f, tok(t)],
                                           scalar=normw[:, 3 * KT + f:3 * KT + f + 1],
                                           in1=rinv[:, t, :], op0=ALU.mult, op1=ALU.mult
                                           ).then_inc(y_done, 1)


def cols_tiles(w):
    kt, n = w.shape[0] // P, w.shape[1] // P
    return np.ascontiguousarray(w.reshape(kt, P, n, P).transpose(2, 1, 0, 3)).reshape(n, P, kt * P)


def rows_tiles(w):
    g = w.shape[0] // (2 * P)
    return np.ascontiguousarray(w.reshape(g, 2, P, 2, 4 * P).transpose(0, 3, 2, 1, 4)
                                ).reshape(2 * g, P, D)


def ffn_stream(w1, w3, w2):
    a, b, c = cols_tiles(w1), cols_tiles(w3), rows_tiles(w2)
    tiles = []
    for g in range(FFG):
        tiles += [a[2 * g], b[2 * g], a[2 * g + 1], b[2 * g + 1]]
        if g:
            tiles += [c[2 * g - 2], c[2 * g - 1]]
    return tiles + [c[2 * FFG - 2], c[2 * FFG - 1]]


def branch_stream(q, k, v, r, wb):
    b = rows_tiles(wb)
    q, k, v, r = (cols_tiles(x) for x in (q, k, v, r))
    tiles = []
    for hd in range(HEADS):
        tiles += [q[hd], k[hd], v[2 * hd], v[2 * hd + 1]]
        if hd:
            tiles += [b[2 * hd - 2], b[2 * hd - 1]]
        tiles += [r[2 * hd], r[2 * hd + 1]]
    return tiles + [b[2 * HEADS - 2], b[2 * HEADS - 1]]


def kernel(x, norm_ffn1, ffn1_w1, ffn1_w3, ffn1_w2, norm_mix, w_in, gla_gate_w2, gla_gate_b,
           gla_norm_w, w_branch_ret, w_branch_gla, w_out, norm_ffn2, ffn2_w1, ffn2_w3, ffn2_w2,
           norm_final):
    import concourse.bacc as bacc
    from concourse.bass_utils import run_bass_kernel_spmd

    A = np.asarray
    w_in = A(w_in)[0]
    widths = (512, 512, 1024, 1024, 512, 512, 1024, 1024, 16, 1024, 1024)
    at = np.cumsum((0,) + widths)
    qa, ka, va, ra, qb, kb, vb, rb, lr, ga, gb = (w_in[:, a:b] for a, b in zip(at[:-1], at[1:]))
    lr = np.concatenate([lr, np.zeros((D, P - lr.shape[1]), lr.dtype)], 1)
    tiles = ffn_stream(A(ffn1_w1)[0], A(ffn1_w3)[0], A(ffn1_w2)[0])
    tiles += branch_stream(qa, ka, va, ra, A(w_branch_ret)[0])
    tiles += list(cols_tiles(ga)) + list(cols_tiles(lr))
    tiles += branch_stream(qb, kb, vb, rb, A(w_branch_gla)[0])
    tiles += list(cols_tiles(gb)) + list(cols_tiles(A(w_out)[0]))
    tiles += ffn_stream(A(ffn2_w1)[0], A(ffn2_w3)[0], A(ffn2_w2)[0])
    assert len(tiles) == N_TILES

    def columns(v):
        return A(v).reshape(-1, P).T

    rope, ret, masks, small = decay_tables()
    arrays = {
        "xT": np.ascontiguousarray(A(x)[0].T.reshape(KT, P, T).transpose(1, 0, 2)),
        "wts": np.stack(tiles),
        "norms": np.ascontiguousarray(np.concatenate(
            [columns(v) for v in (norm_ffn1, norm_mix, norm_ffn2, norm_final, gla_norm_w)], 1)),
        "gate_w2": np.ascontiguousarray(A(gla_gate_w2)[0]),
        "gate_b": np.ascontiguousarray(columns(gla_gate_b)),
        "rope": rope,
        "ret": ret,
        "masks": masks,
        "small": small,
    }
    nc = bacc.Bacc("TRN2", target_bir_lowering=False, num_devices=1, dynamic_dma_scratch_size=1024)
    aps = [nc.dram_tensor(n, a.shape, mybir.dt.from_np(a.dtype), kind="ExternalInput").ap()
           for n, a in arrays.items()]
    out = nc.dram_tensor("yT", (P, KT, T), F32, kind="ExternalOutput").ap()
    spill = [nc.dram_tensor(n, (P, KT, T), F32, kind="Internal").ap() for n in ("h_spill", "y_spill")]
    block_kernel(nc, *aps, out, *spill)
    r = run_bass_kernel_spmd(nc, [arrays], core_ids=[0])
    got = r.results[0]["yT"]
    return np.ascontiguousarray(got.transpose(1, 0, 2)).reshape(D, T).T[None]
```

```python
from contextlib import ExitStack

import numpy as np

import concourse.bass as bass
from concourse import mybir

F32 = mybir.dt.float32
F32R = mybir.dt.float32r
U8 = mybir.dt.uint8
ALU = mybir.AluOpType
ACT = mybir.ActivationFunctionType

P = 128
T = 1024
D = 1024
KT = D // P
HF = 512
FF = 2816
FFG = FF // (2 * P)
HEADS = 4
DK = 128
DV = 256
BLK = 128
NBH = HF // BLK
CHUNK = 64
EPS = 1e-6
TAU = 16.0
QK_SCALE = DK ** -0.5
ROPE_BASE = 10000.0

RAW = 4
FFN_TILES = 6 * FFG
BRANCH_TILES = 8 * HEADS
N_F1 = 0
N_RET = N_F1 + FFN_TILES
N_GA0 = N_RET + BRANCH_TILES - 2
N_LR = N_RET + BRANCH_TILES + 1
N_GA = N_LR
N_GLA = N_GA + KT
N_GB0 = N_GLA + BRANCH_TILES - 2
N_GB = N_GLA + BRANCH_TILES
N_OUT = N_GB + KT
N_F2 = N_OUT + KT
N_TILES = N_F2 + FFN_TILES

Q, K, V0, V1, B0, B1, R0, R1 = range(8)
STEPS = 64
NORM_STEPS = (50, 62)
LEVELS = (64, 32, 16, 8, 4, 2, 1)
NLV = len(LEVELS)
LAST, DIAG = NLV, NLV + 1


def score_step(half, item):
    return (18 if half == 0 else 36) + 2 * item


def block_step(half, b):
    return (36 if half == 0 else 54) + 2 * b


POOL_LAST = range(5, KT)
DVE_ADD = 5
POOL_ADDS = 4
INV_AT = 15
RANK = 16
CH_GA, CH_LR, CH_GB, CH_OUT = 1, 2, 1 + KT, 1 + 2 * KT
PAIRED = [(f, t) for f in range(KT - 2) for t in range(2)] + [(f, t) for t in range(2)
                                                             for f in (KT - 2, KT - 1)]
PLACE = {ft: i for i, ft in enumerate(PAIRED)}


def last_unit(v):
    t, f = divmod(v, KT)
    return f // 4, t, f, v % 6, int(v > 11)


def wait(eng, sem, value):
    if isinstance(value, int) and value <= 0:
        return
    eng.wait_ge(sem, value)


def decay_tables():
    f = np.float32
    half = DK // 2
    inv = (f(ROPE_BASE) ** (-np.arange(half, dtype=f) / f(half))).astype(f)
    ang = (np.arange(T, dtype=f)[:, None] * inv[None, :]).astype(f).T.astype(np.float64)
    cos, sin = np.cos(ang), np.sin(ang)
    rope = np.stack([np.concatenate([cos, cos]), np.concatenate([sin, -sin])], 1).astype(f)
    lg = np.log1p(-np.exp2(-5.0 - np.arange(HEADS)))
    i = np.arange(BLK)
    m, n = i[:, None], i[None, :]
    seen = (m // CHUNK) <= (n // CHUNK)
    intra = np.where(seen, np.exp(lg[:, None, None] * np.abs(m - n)), 0.0) * QK_SCALE
    qdec = np.broadcast_to((np.exp(lg[:, None] * (i + 1.0)) * QK_SCALE)[:, None, :], (HEADS, P, BLK))
    kdec = np.exp(lg[:, None] * (BLK - 1.0 - i))[:, :, None]
    bdec = np.broadcast_to(np.exp(lg * BLK)[:, None, None], (HEADS, P, 1))
    ret = np.concatenate([intra, qdec, kdec, bdec], 2).transpose(1, 0, 2).astype(f)
    masks = []
    for s in LEVELS[1:]:
        masks.append((m // (2 * s) == n // (2 * s)) & (m // s != n // s))
    masks.append(m == n)
    masks = np.stack(masks, 1)
    small = np.concatenate([np.eye(P), np.full((P, P), 1.0 / D), np.ones((P, P)),
                            np.full((P, 1), EPS)], 1).astype(f)
    return rope, ret, np.ascontiguousarray(masks.astype(f)), small


RETC = 2 * BLK + 2
SMALLC = 3 * P + 1


class NormSignals:

    def __init__(self, sem, stage, feeds_product=True):
        self.sq_done = sem(f"{stage}_sq_done")
        self.sum_done = sem(f"{stage}_sum_done")
        self.mean_done = sem(f"{stage}_mean_done")
        self.root_done = sem(f"{stage}_root_done")
        self.inv_done = sem(f"{stage}_inv_done")
        if feeds_product:
            self.uh_done = sem(f"{stage}_uh_done")
            self.ul_done = sem(f"{stage}_ul_done")


class FfnSignals:

    def __init__(self, sem, stage):
        self.a_done = sem(f"{stage}_a_done")
        self.b_done = sem(f"{stage}_b_done")
        self.p2_done = sem(f"{stage}_p2_done")
        self.as_done = sem(f"{stage}_as_done")
        self.silu_done = sem(f"{stage}_silu_done")
        self.sr_done = sem(f"{stage}_sr_done")
        self.gate_done = sem(f"{stage}_gate_done")
        self.hh_done = sem(f"{stage}_hh_done")
        self.hl_done = sem(f"{stage}_hl_done")
        self.acc_done = sem(f"{stage}_acc_done")


class BranchSignals:

    def __init__(self, sem, stage, gla):
        self.half_done = sem(f"{stage}_half_done")
        self.b_part = sem(f"{stage}_b_part")
        self.q_ev = sem(f"{stage}_q_ev")
        self.k_ev = sem(f"{stage}_k_ev")
        self.v_ev = sem(f"{stage}_v_ev")
        self.vt_done = sem(f"{stage}_vt_done")
        self.vt_ev = sem(f"{stage}_vt_ev")
        self.r_sc = sem(f"{stage}_r_sc")
        self.r_ev = sem(f"{stage}_r_ev")
        self.b_ev = sem(f"{stage}_b_ev")
        self.ot_done = sem(f"{stage}_ot_done")
        self.g_done = sem(f"{stage}_g_done")
        self.oh_done = sem(f"{stage}_oh_done")
        self.ol_done = sem(f"{stage}_ol_done")
        self.sc_done = sem(f"{stage}_sc_done")
        self.sc_ev = sem(f"{stage}_sc_ev")
        self.kt_done = sem(f"{stage}_kt_done")
        self.kt_ev = sem(f"{stage}_kt_ev")
        if not gla:
            self.qd_done = sem(f"{stage}_qd_done")
        self.o_done = sem(f"{stage}_o_done")
        self.o_ev = sem(f"{stage}_o_ev")
        self.st_done = sem(f"{stage}_st_done")
        self.st_ev = sem(f"{stage}_st_ev")
        self.var_done = sem(f"{stage}_var_done")
        self.sd_done = sem(f"{stage}_sd_done")
        self.on_done = sem(f"{stage}_on_done")
        self.chain = sem(f"{stage}_chain")
        self.headc_done = sem(f"{stage}_headc_done")


def block_kernel(nc, xT, wts, norms, gate_w2, gate_b, rope, ret, masks, small, out, h_spill, y_spill):
    ctx = ExitStack()
    with ctx:
        def sb(name, shape, dt=F32, scope=ctx):
            return scope.enter_context(nc.sbuf_tensor(name, shape, dt))

        def sem(name):
            return ctx.enter_context(nc.semaphore(name))

        uH = sb("uH", [P, KT, T], F32R)
        uL = sb("uL", [P, KT, T], F32R)
        raw = [sb(f"raw{i}", [P, D]) for i in range(RAW)]
        wH = [sb(f"wH{i}", [P, D], F32R) for i in range(2)]
        wL = [sb(f"wL{i}", [P, D], F32R) for i in range(2)]
        smallt = sb("smallt", [P, SMALLC])
        ident, mean_of, ones = (smallt[:, i * P:(i + 1) * P] for i in range(3))
        eps = smallt[:, 3 * P:3 * P + 1]
        normw = sb("normw", [P, 4 * KT + 2])
        gbt = sb("gbt", [P, HEADS])
        rinv = sb("rinv", [P, 2, HF])
        one = sb("one", [P, 1])
        warm = sb("warm", [P, 3])
        maskt = sb("maskt", [P, NLV, BLK], U8)
        w2t = sb("w2t", [6 * RANK, HEADS * DK])
        w2s = sb("w2s", [6 * RANK, DK], F32R)
        lrw = sb("lrw", [P, KT, 2 * RANK], F32R)
        headc = sb("headc", [P, 4])
        carrier = sb("carrier", [P, 2])
        bst = sb("bst", [P, NBH, 6])
        mv = sb("mv", [P, NBH, 2])
        ve = sb("ve", [P, NBH])
        sd = sb("sd", [P, NBH])
        rs = sb("rs", [P, NBH])
        bdec = sb("bdec", [P, 2, NBH])

        with ExitStack() as f:
            h = sb("h", [P, KT, T], scope=f)
            hidH = sb("hidH", [P, 2, 2, T], F32R, scope=f)
            hidL = sb("hidL", [P, 2, 2, T], F32R, scope=f)
            sq = sb("sq", [P, 2, HF], scope=f)
            ssum = sb("ssum", [P, 2, HF], scope=f)
            sil = sb("sil", [P, 2, HF], scope=f)
            hidf = sb("hidf", [P, 2, HF], scope=f)
            maskf = sb("maskf", [P, NLV, BLK], scope=f)
        m = ctx.enter_context(ExitStack())
        ogH = sb("ogH", [P, 2, T], F32R, scope=m)
        ogL = sb("ogL", [P, 2, T], F32R, scope=m)
        rS = sb("rS", [P, 2, T], scope=m)
        on = sb("on", [P, 2 * NBH, DV], scope=m)
        y = sb("y", [P, KT, T], scope=m)
        ogf = sb("ogf", [P, 2, HF], scope=m)
        ss = sb("ss", [P, 2, NBH, BLK], scope=m)
        qd = sb("qd", [P, NBH, BLK], scope=m)
        ktok = sb("ktok", [P, NBH, DK], scope=m)
        state = sb("state", [P, 2, DV], scope=m)
        vS = ogf
        qT = sb("qT", [P, T], scope=m)
        kT = sb("kT", [P, T], scope=m)
        vtok = sb("vtok", [P, 2 * NBH, DV], scope=m)
        with ExitStack() as r:
            ropet = sb("ropet", [P, 2, T], scope=r)
            rtmp = sb("rtmp", [P, 2, HF], scope=r)
            rett = sb("rett", [P, HEADS, RETC], scope=r)
        bc = sb("bc", [P, T], scope=m)
        lrT = sb("lrT", [6 * RANK, T], F32R, scope=m)
        ee = sb("ee", [P, 2, HF], scope=m)
        qE = sb("qE", [P, 2, HF], scope=m)
        kE = sb("kE", [P, 2, HF], scope=m)

        ps = ctx.enter_context(nc.psum_tensor("ps", [P, 8, HF], F32))

        const_in = sem("const_in")
        normw_in = sem("normw_in")
        one_set = sem("one_set")
        late_in = sem("late_in")
        once_done = sem("once_done")
        y_over_rms = sem("y_over_rms")
        y_act_done = sem("y_act_done")
        y_dve_done = sem("y_dve_done")
        raw_in = [sem(f"raw_in{i}") for i in range(RAW)]
        w_high = sem("w_high")
        w_ready = sem("w_ready")
        w_used = sem("w_used")
        h_in = [sem(f"h_in{i}") for i in range(KT)]
        x_rest_in = [sem(f"x_rest_in{i}") for i in range(2)]
        cols_half = sem("cols_half")
        h_saved = sem("h_saved")
        y_saved = sem("y_saved")
        y_back = [sem(f"y_back{i}") for i in range(2)]
        out_saved = sem("out_saved")

        norm1, norm2, norm3, norm4 = (NormSignals(sem, f"norm{i}", i < 4) for i in range(1, 5))
        f1, f2 = FfnSignals(sem, "f1"), FfnSignals(sem, "f2")
        ret_s, gla_s = BranchSignals(sem, "ret", False), BranchSignals(sem, "gla", True)
        z_done, zabs_done, zmin_done, zexp_done, zln_done, cum_done = (
            sem(x) for x in ("z_done", "zabs_done", "zmin_done", "zexp_done", "zln_done", "cum_done"))
        diff_done, exp_done, prod_done = (sem(x) for x in ("diff_done", "exp_done", "prod_done"))
        lr_ev = sem("lr_ev")
        lr_part = sem("lr_part")
        lrw_done = sem("lrw_done")
        ga_sc, ga_sig, ga_ev = (sem(f"ga_{x}") for x in ("sc", "sig", "ev"))
        gb_sc, gb_sig, gb_mul, gb_ev = (sem(f"gb_{x}") for x in ("sc", "sig", "mul", "ev"))
        mh_done, ml_done = sem("mh_done"), sem("ml_done")
        wo_ev = sem("wo_ev")

        def tok(half):
            return slice(half * HF, (half + 1) * HF)

        def carry(place=0):
            nc.vector.memset(carrier[:, place:place + 1], 0.0)

        def last_square(f):
            return (None, sq[:, 1, :], sq[:, 0, :], sil[:, 0, :], sil[:, 1, :], hidf[:, 0, :],
                    hidf[:, 1, :], sq[:, 1, :])[f]

        def load_x(eng, f):
            eng.dma_start(h[:, f, tok(0)], xT[:, f, tok(0)]).then_inc(h_in[f], 16)

        block = ctx.enter_context(nc.Block())

        @block.sync
        def _(sp):
            def load(n, slot):
                wait(sp, w_ready, n - RAW + 1)
                sp.dma_start(raw[slot][:], wts[bass.ds(n, 1)].rearrange("a p c -> p (a c)")
                             ).then_inc(raw_in[slot], 16)

            load(0, 0)
            for f in range(1, KT):
                if f == 4:
                    load(1, 1)
                load_x(sp, f)
            for i in range(2):
                part = slice(i * KT // 2, (i + 1) * KT // 2)
                sp.dma_start(h[:, part, tok(1)], xT[:, part, tok(1)]).then_inc(x_rest_in[i], 16)
            sp.dma_start(smallt[:], small).then_inc(const_in, 16)
            load(2, 2)
            load(3, 3)
            for to, source in ((gbt, gate_b), (rett, ret), (maskf, masks), (w2t, gate_w2), (ropet, rope)):
                sp.dma_start(to[:], source).then_inc(late_in, 16)
            with sp.Fori(1, N_TILES // RAW) as i:
                for s in range(RAW):
                    load(i * RAW + s, s)
            for n in range(N_TILES // RAW * RAW, N_TILES):
                load(n, n % RAW)
            for i in range(2 * POOL_LAST[0]):
                t, f = divmod(i, POOL_LAST[0])
                sp.wait_ge(y_dve_done, i + 1)
                sp.dma_start(out[:, f, tok(t)], h[:, f, tok(t)]).then_inc(out_saved, 16)

        @block.gpsimd
        def _(pool):
            def cut(n, s, round_):
                slot = s % 2
                pool.wait_ge(raw_in[s], 16 * round_ + 16)
                wait(pool, w_used, n - 1)
                nc.gpsimd.tensor_tensor(wH[slot][:], raw[s][:], one[:].to_broadcast([P, D]),
                                        ALU.mult).then_inc(w_high, 1)
                pool.wait_ge(w_high, n + 1)
                nc.gpsimd.tensor_tensor(wL[slot][:], raw[s][:], wH[slot][:].bitcast(F32), ALU.subtract
                                        ).then_inc(w_ready, 1)

            nc.gpsimd.memset(one[:], 1.0).then_inc(one_set, 1)
            pool.wait_ge(one_set, 1)
            pool.wait_ge(w_ready, 1)
            for n in range(1, RAW):
                cut(n, n, 0)
            with pool.Fori(1, N_TILES // RAW) as i:
                for s in range(RAW):
                    cut(i * RAW + s, s, i)
            for n in range(N_TILES // RAW * RAW, N_TILES):
                cut(n, n % RAW, n // RAW)

            for f in range(1, POOL_ADDS + 1):
                pool.wait_ge(norm4.sq_done, KT + f + 1)
                pool.wait_ge(norm4.sum_done, KT - 1 + f - 1)
                nc.gpsimd.tensor_tensor(ssum[:, 1, :], ssum[:, 1, :], last_square(f), ALU.add
                                        ).then_inc(norm4.sum_done, 1)
            for t in range(2):
                pool.wait_ge(norm4.inv_done, t + 1)
                for f in POOL_LAST:
                    nc.gpsimd.tensor_tensor(h[:, f, tok(t)], h[:, f, tok(t)], rinv[:, t, :], ALU.mult
                                            ).then_inc(y_over_rms, 1)

        @block.tensor
        def _(pe):
            mm = nc.tensor.matmul

            def triple(bank, wh, wl, xh, xl, start, stop):
                mm(bank, wh, xh, start=start, stop=False)
                mm(bank, wh, xl, start=False, stop=False)
                return mm(bank, wl, xh, start=False, stop=stop)

            def cols_part(slot, bank, half, k0, k1):
                for k in range(k0, k1):
                    last = triple(ps[:, bank, :], wH[slot][:, k * P:(k + 1) * P],
                                  wL[slot][:, k * P:(k + 1) * P], uH[:, k, tok(half)],
                                  uL[:, k, tok(half)], k == 0, k == KT - 1)
                return last

            def rows_unit(slot, bank, fl, xh, xl, half):
                for k in range(2):
                    w = slice(k * 4 * P + fl * P, k * 4 * P + (fl + 1) * P)
                    last = triple(ps[:, bank, :], wH[slot][:, w], wL[slot][:, w],
                                  xh[:, k, tok(half)], xl[:, k, tok(half)], k == 0, k == 1)
                return last

            def mean(nm, t, sums):
                pe.wait_ge(nm.sum_done, sums)
                mm(ps[:, 6 + t, :], mean_of, ssum[:, t, :], start=True, stop=True
                   ).then_inc(nm.mean_done, 1)

            def ffn(s, n0, nm, next_nm, mean_at):
                def tile_no(i, j):
                    return n0 + 4 + 6 * (i - 1) + j if not isinstance(i, int) or i > 0 else n0 + j

                def p1(i, first=False, second=False):
                    for j in range(2):
                        order = [(0, 0), (1, 0), (0, 1), (1, 1)] if first and j == 0 else \
                                [(0, 0), (0, 1), (1, 0), (1, 1)]
                        for side, t in order:
                            n = tile_no(i, 2 * j + side)
                            slot = (n0 + side) % 2
                            if t == 0:
                                pe.wait_ge(w_ready, n + 1)
                            u = 4 * j + 2 * side + t
                            if second:
                                pe.wait_ge(s.gate_done if side else s.as_done, 2 * j + t + 1)
                            elif first and u >= 6:
                                pe.wait_ge(nm.root_done, t + 1)
                            elif not first:
                                pe.wait_ge(s.acc_done, 16 * (i - 2) + 8 + u + 1)
                            if first and j == 0 and side == 0:
                                for k in range(KT):
                                    pe.wait_ge(nm.ul_done, KT * t + k + 1)
                                    last = cols_part(slot, u, t, k, k + 1)
                            else:
                                last = cols_part(slot, u, t, 0, KT)
                            if t == 0:
                                last.then_inc(s.b_done if side else s.a_done, 1)
                            else:
                                last.then_inc(w_used, 1)
                            if first and u == 4:
                                pe.wait_ge(const_in, 16)
                                for half in range(2):
                                    mean(nm, half, 2 * (KT - 1))

                def p2(g, par, n, i=None):
                    pe.wait_ge(s.hl_done, 4 * (g + 1))
                    for v in range(16):
                        c, t, fl = v // 8, v % 8 // 4, v % 4
                        if v % 8 == 0:
                            pe.wait_ge(w_ready, n + c + 1)
                        if v < 8 and i is not None:
                            idx = 4 * i + 2 * (v // 4) + v % 2 + 1
                            pe.wait_ge(s.gate_done if v % 4 // 2 else s.as_done, idx)
                        elif v < 8:
                            pe.wait_ge(s.acc_done, 16 * (g - 1) + 8 + v + 1)
                        else:
                            pe.wait_ge(s.acc_done, 16 * g + v - 8 + 1)
                        last = rows_unit((n0 + c) % 2, v % 8, fl, hidH[:, par], hidL[:, par], t)
                        last.then_inc(w_used if v % 8 == 7 else s.p2_done, 1)

                p1(0, first=True)
                p1(1, second=True)
                p2(0, 0, tile_no(1, 4), 1)
                with pe.Fori(1, FFG // 2) as c:
                    for par in range(2):
                        i = c * 2 + par
                        p1(i)
                        p2(i - 1, 1 - par, tile_no(i, 4), i)
                i = FFG - 1
                p1(i)
                p2(i - 1, (i - 1) % 2, tile_no(i, 4), i)
                n = tile_no(i, 4) + 2
                pe.wait_ge(s.hl_done, 4 * FFG)
                for v in range(16):
                    c, t, f, bank, through = last_unit(v)
                    if v % 4 == 0 and v < 8:
                        pe.wait_ge(w_ready, n + c + 1)
                    pe.wait_ge(s.acc_done, 16 * (i - 1) + 8 + v + 1 if v < 6 else 16 * i + v - 6 + 1)
                    last = rows_unit((n0 + c) % 2, bank, f % 4, hidH[:, i % 2], hidL[:, i % 2], t)
                    last.then_inc(w_used if v in (11, 15) else s.p2_done, 1)
                    if v == mean_at:
                        mean(next_nm, 0, KT - 1)

            def out_transposes(s, hp, half):
                pe.wait_ge(s.on_done, 2 * hp + half + 1)
                for d in range(2):
                    if half == 0:
                        pe.wait_ge(s.st_ev if d else s.o_ev, (7 if d else 8) * (hp + 1))
                    else:
                        pe.wait_ge(s.g_done, 4 * hp + d + 1)
                    for b in range(NBH):
                        last = nc.tensor.transpose(ps[:, 6 + d, b * BLK:(b + 1) * BLK],
                                                   on[:, half * NBH + b, d * P:(d + 1) * P], ident)
                    last.then_inc(s.ot_done, 1)

            def branch_unit(s, hp, n0, slot, v, n_tile, tail=False):
                c, t, fl = v // 8, v % 8 // 4, v % 4
                if v % 8 == 0:
                    pe.wait_ge(w_ready, n_tile + 1)
                if v == 0:
                    pe.wait_ge(s.ol_done, 4 * (hp + 1))
                if v < 4:
                    if tail:
                        pe.wait_ge(s.r_sc, 4 * HEADS - 3 + v)
                    else:
                        pe.wait_ge(s.v_ev, 4 * (hp + 1) + v + 1)
                else:
                    pe.wait_ge(s.b_ev, 16 * hp + v - 4 + 1)
                last = rows_unit(slot, v % 4, fl, ogH, ogL, t)
                last.then_inc(w_used if v % 8 == 7 else s.b_part, 1)

            def gate_logits(hd):
                pe.wait_ge(gla_s.headc_done, hd + 1)
                pe.wait_ge(lr_ev, 2)
                wait(pe, gla_s.sc_ev, 16 * hd)
                wait(pe, gla_s.kt_ev, 2 * hd)
                for t in range(2):
                    mm(ps[:, 4 + t, :], w2s[:], lrT[:, tok(t)], start=True, stop=True
                       ).then_inc(z_done, 1)

            def branch(s, n0, gla, nm):
                n_sc = NLV + 1 if gla else 1

                def window(hd, first):
                    nw = n0 if first else n0 + 6 + 8 * (hd - 1)
                    for step in range(STEPS):
                        tile, e = step // 8, step % 8
                        if first and step >= 32:
                            tile, e = R0 + (step - 32) // 16, (step - 32) % 16 // 2
                        if first and step >= 32 and step % 2:
                            pass
                        elif tile in (B0, B1):
                            branch_unit(s, hd - 1, n0, (n0 + tile) % 2, step - 8 * B0, nw + tile)
                        else:
                            n = nw + tile - (2 if first and tile > B1 else 0)
                            slot = (n0 + tile) % 2
                            t, q4 = e // 4, e % 4
                            if e == 0:
                                pe.wait_ge(w_ready, n + 1)
                            bank = 2 * (tile % 2) + t
                            if q4 == 0:
                                if tile in (Q, K) and nm is not None and first:
                                    pe.wait_ge(f1.acc_done, 16 * (FFG - 1) + 12 + bank + 1)
                                elif tile in (Q, K) and first:
                                    pe.wait_ge(ga_sc, 2 * KT - 4 + bank + 1)
                                elif tile in (Q, K):
                                    wait(pe, s.r_sc, 4 * hd - 3 + bank)
                                elif tile == V0:
                                    pe.wait_ge(s.q_ev, 2 * hd + t + 1)
                                elif tile == V1:
                                    pe.wait_ge(s.k_ev, 2 * hd + t + 1)
                                elif first:
                                    pe.wait_ge(s.v_ev, bank + 1)
                                else:
                                    pe.wait_ge(s.b_ev, 16 * (hd - 1) + 12 + bank + 1)
                            if first and tile == Q and nm is not None:
                                for k in range(2 * q4, 2 * q4 + 2):
                                    pe.wait_ge(nm.ul_done, KT * t + k + 1)
                                    last = cols_part(slot, bank, t, k, k + 1)
                            else:
                                last = cols_part(slot, bank, t, 2 * q4, 2 * q4 + 2)
                            if e == 3:
                                last.then_inc(s.half_done, 1)
                            elif e == 7:
                                last.then_inc(w_used, 1)
                            if first and nm is not None and step == 12:
                                mean(nm, 1, 2 * (KT - 1))
                        if gla and step == 1 and not first:
                            gate_logits(hd)
                        if step in (3, 11) and not first:
                            out_transposes(s, hd - 1, step // 8)
                        if step in (22, 26, 30, 34):
                            v = (step - 22) // 4
                            pe.wait_ge(s.v_ev, 4 * hd + v + 1)
                            if v < 2:
                                wait(pe, s.g_done, 4 * hd - 2 + v + 1 if not first else 0)
                                if first and nm is not None:
                                    pe.wait_ge(nm.root_done, 2)
                            else:
                                pe.wait_ge(s.vt_ev, 4 * hd + v - 2 + 1)
                            for b in range(NBH):
                                last = nc.tensor.transpose(ps[:, 6 + v % 2, b * BLK:(b + 1) * BLK],
                                                           vS[:, v % 2, b * BLK:(b + 1) * BLK], ident)
                            last.then_inc(s.vt_done, 1)
                        for half in range(2):
                            for item in range(NLV + 2):
                                if step == score_step(half, item):
                                    scores(hd, half, item)
                            for b in range(NBH):
                                if step == block_step(half, b):
                                    block_out(hd, half * NBH + b)

                def scores(hd, half, item):
                    if not gla and item not in (LAST, DIAG):
                        return
                    g = half * (NLV + 2) + item
                    bank = 4 + g % 2
                    sc0 = 2 * n_sc * hd + n_sc * half
                    if gla:
                        if item == DIAG:
                            pe.wait_ge(s.sc_ev, sc0 + NLV)
                        elif g == 0:
                            pe.wait_ge(zln_done, 2 * hd + 2)
                            pe.wait_ge(zmin_done, 2 * hd + 2)
                        elif g == 1:
                            pass
                        elif item == 0:
                            pe.wait_ge(s.kt_ev, 2 * hd + half)
                        elif item == 1:
                            pe.wait_ge(s.sc_ev, sc0)
                        else:
                            pe.wait_ge(s.sc_ev, sc0 + item - 1)
                    else:
                        wait(pe, s.kt_ev, 2 * hd + half)
                        wait(pe, s.sc_ev, sc0)
                    if item < NLV or item == LAST:
                        if gla:
                            pe.wait_ge(prod_done, 2 * (NLV + 2) * hd + g + 1)
                        else:
                            pe.wait_ge(s.k_ev, 2 * hd + half + 1)
                    if item == DIAG:
                        pe.wait_ge(s.q_ev, 2 * hd + half + 1)
                        pe.wait_ge(s.k_ev, 2 * hd + half + 1)
                    for b in range(NBH):
                        blk = slice(b * BLK, (b + 1) * BLK)
                        tb = slice(half * HF + b * BLK, half * HF + (b + 1) * BLK)
                        if item == LAST:
                            src = kE[:, item % 2, blk] if gla else kT[:, tb]
                            last = nc.tensor.transpose(ps[:, bank, blk], src, ident)
                        elif item == DIAG:
                            last = mm(ps[:, bank, blk], kT[:, tb], qT[:, tb], start=True, stop=True)
                        elif item == 0:
                            last = mm(ps[0:CHUNK, bank, b * BLK + CHUNK:(b + 1) * BLK],
                                      kE[:, 0, b * BLK:b * BLK + CHUNK],
                                      qE[:, 0, b * BLK + CHUNK:(b + 1) * BLK], start=True, stop=True)
                        else:
                            last = mm(ps[:, bank, blk], kE[:, item % 2, blk], qE[:, item % 2, blk],
                                      start=True, stop=True)
                    last.then_inc(s.kt_done if item == LAST else s.sc_done, 1)

                def block_out(hd, b):
                    half, bb = b // NBH, b % NBH
                    hb = slice(b % 2 * DV, (b % 2 + 1) * DV)
                    o, st = ps[:, 6, hb], ps[:, 7, hb]
                    if bb == 0:
                        pe.wait_ge(s.sc_ev, 2 * n_sc * hd + n_sc * (half + 1))
                        pe.wait_ge(s.kt_ev, 2 * hd + half + 1)
                        if gla:
                            pe.wait_ge(prod_done, (NLV + 2) * (2 * hd + half + 1))
                        else:
                            pe.wait_ge(s.qd_done, 2 * hd + half + 1)
                    if b == 0:
                        pe.wait_ge(s.vt_ev, 4 * hd + 4)
                    if b >= 1:
                        pe.wait_ge(s.o_ev, 8 * hd + b)
                    last = mm(o, ss[:, half, bb, :], vtok[:, b, :], start=True, stop=b == 0)
                    if b > 0:
                        pe.wait_ge(s.st_ev, 7 * hd + b)
                        last = mm(o, qd[:, bb, :], state[:, b % 2, :], start=False, stop=True)
                    last.then_inc(s.o_done, 1)
                    if b < 2 * NBH - 1:
                        mm(st, ktok[:, bb, :], vtok[:, b, :], start=True, stop=True
                           ).then_inc(s.st_done, 1)

                window(0, True)
                with pe.Fori(1, HEADS) as hd:
                    window(hd, False)

            def cols_half_tile(n, bank, t, fresh=None):
                if t == 0:
                    pe.wait_ge(w_ready, n + 1)
                for k in range(KT):
                    if fresh is not None:
                        fresh(k)
                    last = cols_part(n % 2, bank, t, k, k + 1)
                last.then_inc(w_used if t else cols_half, 1)

            def branch_tail(s, n0, n_mid, n_sc):
                hp = HEADS - 1
                nb = n0 + BRANCH_TILES - 1
                for t in range(2):
                    out_transposes(s, hp, t)
                    pe.wait_ge(s.sc_ev, 2 * n_sc * HEADS)
                    pe.wait_ge(s.kt_ev, 2 * HEADS)
                    cols_half_tile(n_mid, 4 + t, t)
                for v in range(16):
                    branch_unit(s, hp, n0, (nb + v // 8) % 2, v, nb + v // 8, tail=True)

            ffn(f1, N_F1, norm1, norm2, 14)
            branch(ret_s, N_RET, False, norm2)
            branch_tail(ret_s, N_RET, N_GA0, 1)
            pe.wait_ge(lrw_done, 1)
            for t in range(2):
                pe.wait_ge(ret_s.b_ev, 16 * HEADS - 4 + t + 1)
                for k in range(KT):
                    mm(ps[0:2 * RANK, t, :], lrw[:, k, :], uH[:, k, tok(t)], start=k == 0, stop=False)
                    last = mm(ps[0:2 * RANK, t, :], lrw[:, k, :], uL[:, k, tok(t)], start=False,
                              stop=k == KT - 1)
                last.then_inc(w_used if t else cols_half, 1)
            for f in range(1, KT):
                for t in range(2):
                    bank = 2 * (f % 2) + t
                    if f == 1:
                        pe.wait_ge(ret_s.b_ev, 16 * HEADS - 4 + bank + 1)
                    elif f == 2:
                        pe.wait_ge(lr_ev, t + 1)
                    else:
                        pe.wait_ge(ga_sc, 2 * f - 3 + t)
                    cols_half_tile(N_GA + f, bank, t)
                if f == 3:
                    gate_logits(0)
            branch(gla_s, N_GLA, True, None)
            branch_tail(gla_s, N_GLA, N_GB0, NLV + 1)
            for f, t in PAIRED[2:]:
                bank = 2 * (f % 2) + t
                if f < 3:
                    pe.wait_ge(gla_s.b_ev, 16 * HEADS - 4 + bank + 1)
                else:
                    pe.wait_ge(gb_sc, PLACE[f - 2, t] + 1)
                cols_half_tile(N_GB + f, bank, t)
            for f, t in PAIRED:
                pe.wait_ge(*((wo_ev, PLACE[f - 2, t] + 1) if f >= 2 else
                             (gb_sc, PLACE[f + KT - 2, t] + 1)))
                cols_half_tile(N_OUT + f, 2 * (f % 2) + t, t,
                               (lambda k: pe.wait_ge(ml_done, KT * t + k + 1)) if f == 0 else None)
            ffn(f2, N_F2, norm3, norm4, 9)
            pe.wait_ge(norm4.sum_done, KT - 1 + DVE_ADD)
            mm(ps[:, 7, :], mean_of, ssum[:, 1, :], start=True, stop=False)
            for f in range(DVE_ADD + 1, KT):
                pe.wait_ge(norm4.sq_done, KT + f + 1)
                last = mm(ps[:, 7, :], mean_of, last_square(f), start=False, stop=f == KT - 1)
            last.then_inc(norm4.mean_done, 1)

        @block.scalar
        def _(act):
            A = nc.scalar.activation

            def high(nm, f, t, wcol):
                A(uH[:, f, tok(t)], h[:, f, tok(t)], ACT.Copy,
                  scale=normw[:, wcol * KT + f:wcol * KT + f + 1]).then_inc(nm.uh_done, 1)

            def square(nm, count, f, t):
                if f == 0:
                    A(ssum[:, t, :], h[:, f, tok(t)], ACT.Square).then_inc(nm.sq_done, 1)
                    return count
                wait(act, nm.sum_done, count - 1)
                A(sq[:, count % 2, :], h[:, f, tok(t)], ACT.Square).then_inc(nm.sq_done, 1)
                return count + 1

            def root(nm, t):
                act.wait_ge(nm.mean_done, t + 1)
                A(rinv[:, t, :], ps[:, 6 + t, :], ACT.Sqrt, bias=eps).then_inc(nm.root_done, 1)

            def roots(nm):
                for t in range(2):
                    root(nm, t)

            def ffn(s, n0):
                def p1(i, par, first=False, second=False):
                    for j in range(2):
                        for t in range(2):
                            idx = 4 * i + 2 * j + t
                            act.wait_ge(s.as_done, idx + 1)
                            A(sil[:, t, :], sil[:, t, :], ACT.Silu).then_inc(s.silu_done, 1)
                        for t in range(2):
                            idx = 4 * i + 2 * j + t
                            act.wait_ge(s.gate_done, idx + 1)
                            if not first and not second and j == 0 and t == 0:
                                act.wait_ge(w_used, n0 + 4 + 6 * (i - 1))
                            A(hidH[:, par, j, tok(t)], hidf[:, t, :], ACT.Copy).then_inc(s.hh_done, 1)

                p1(0, 0, first=True)
                p1(1, 1, second=True)
                with act.Fori(1, FFG // 2) as c:
                    for par in range(2):
                        p1(c * 2 + par, par)
                p1(FFG - 1, (FFG - 1) % 2)

            def gate_high(s, hp, half, n_before):
                for d in range(2):
                    act.wait_ge(s.g_done, 4 * hp + 2 * half + d + 1)
                    if half == 0 and d == 0:
                        act.wait_ge(w_used, n_before)
                    A(ogH[:, d, tok(half)], ogf[:, d, :], ACT.Copy).then_inc(s.oh_done, 1)

            def soft_part(hd):
                act.wait_ge(gla_s.headc_done, hd + 1)
                for t in range(2):
                    act.wait_ge(z_done, 2 * hd + t + 1)
                    wait(act, prod_done, 2 * (NLV + 2) * hd)
                    A(ee[:, t, :], ps[:, 4 + t, :], ACT.Abs, bias=headc[:, 2:3]
                      ).then_inc(zabs_done, 1)
                for t in range(2):
                    act.wait_ge(zabs_done, 2 * hd + t + 1)
                    A(ee[:, t, :], ee[:, t, :], ACT.Exp, scale=-1.0).then_inc(zexp_done, 1)
                for t in range(2):
                    act.wait_ge(zexp_done, 2 * hd + t + 1)
                    A(ee[:, t, :], ee[:, t, :], ACT.Ln, bias=ones[:, 0:1]).then_inc(zln_done, 1)

            def branch(s, n0, gla):
                def window(hd, first):
                    nw = n0 if first else n0 + 6 + 8 * (hd - 1)

                    for step in range(STEPS + 1):
                        if gla and step == 2 and not first:
                            soft_part(hd)
                        if step in (3, 11) and not first:
                            gate_high(s, hd - 1, step // 8, nw)
                        if step in (22, 26, 30, 34):
                            v = (step - 22) // 4
                            act.wait_ge(s.vt_done, 4 * hd + v + 1)
                            t, d = v % 2, v // 2
                            A(vtok[:, t * NBH:(t + 1) * NBH, d * P:(d + 1) * P],
                              ps[:, 6 + v % 2, :].rearrange("p (b c) -> p b c", b=NBH), ACT.Copy
                              ).then_inc(s.vt_ev, 1)
                        for half in range(2):
                            for item in range(NLV + 2):
                                if gla and step == score_step(half, item) - 3:
                                    exps(hd, half, item)
                                if step == score_step(half, item) and item == LAST:
                                    act.wait_ge(s.kt_done, 2 * hd + half + 1)
                                    wait(act, s.o_done, 8 * hd + 4 * half)
                                    wait(act, s.st_done, 7 * hd + 4 * half)
                                    g = half * (NLV + 2) + item
                                    src = ps[:, 4 + g % 2, :].rearrange("p (b c) -> p b c", b=NBH)
                                    if not gla:
                                        act.wait_ge(s.headc_done, hd + 1)
                                    A(ktok[:], src, ACT.Copy, scale=1.0 if gla else headc[:, 0:1]
                                      ).then_inc(s.kt_ev, 1)
                            for b in range(NBH):
                                if step == block_step(half, b):
                                    bb = half * NBH + b
                                    act.wait_ge(s.o_done, 8 * hd + bb + 1)
                                    if bb == 0:
                                        wait(act, s.ot_done, 4 * hd)
                                    A(on[:, bb, :], ps[:, 6, bb % 2 * DV:(bb % 2 + 1) * DV], ACT.Copy
                                      ).then_inc(s.o_ev, 1)
                            if step == NORM_STEPS[half]:
                                act.wait_ge(s.var_done, 2 * hd + half + 1)
                                A(sd[:], ve[:], ACT.Sqrt).then_inc(s.sd_done, 1)
                        if step in (52, 56, 60, 64):
                            v = (step - 52) // 4
                            act.wait_ge(s.r_sc, 4 * hd + v + 1)
                            x = rS[:, v // 2, tok(v % 2)]
                            A(x, x, ACT.Silu).then_inc(s.r_ev, 1)

                def exps(hd, half, item):
                    gi = half * (NLV + 2) + item
                    e = ee[:, gi % 2, :]
                    if item <= LAST:
                        act.wait_ge(diff_done, 2 * (NLV + 1) * hd + half * (NLV + 1) + item + 1)
                    if item < NLV:
                        w = LEVELS[item]
                        v = e.rearrange("p (n s) -> p n s", s=2 * w)
                        A(v[:, :, 0:w], v[:, :, 0:w], ACT.Exp, scale=-1.0 / TAU)
                        A(v[:, :, w:], v[:, :, w:], ACT.Exp, scale=1.0 / TAU).then_inc(exp_done, 1)
                    elif item == LAST:
                        A(e, e, ACT.Exp, scale=-1.0 / TAU).then_inc(exp_done, 1)
                    else:
                        act.wait_ge(prod_done, 2 * (NLV + 2) * hd + gi - 1)
                        A(e, bc[:, tok(half)], ACT.Exp, scale=1.0 / TAU).then_inc(exp_done, 1)

                window(0, True)
                with act.Fori(1, HEADS) as hd:
                    window(hd, False)
                for half in range(2):
                    gate_high(s, HEADS - 1, half, n0 + BRANCH_TILES - 2)

            act.dma_start(normw[:], norms).then_inc(normw_in, 16)
            load_x(act, 0)
            act.wait_ge(one_set, 1)
            A(warm[:, 0:1], one[:], ACT.Copy)
            act.wait_ge(normw_in, 16)
            for t in range(2):
                for f in range(KT):
                    act.wait_ge(x_rest_in[f // 4] if t else h_in[f], 16)
                    high(norm1, f, t, 0)
            count = 0
            for t in range(2):
                for f in range(KT):
                    count = square(norm1, count, f, t)
            act.wait_ge(const_in, 16)
            roots(norm1)
            ffn(f1, N_F1)
            A(warm[:, 1:2], one[:], ACT.Sqrt)
            count = 0
            for v in range(16):
                c, t, f, _, _ = last_unit(v)
                act.wait_ge(f1.acc_done, 16 * (FFG - 1) + v + 1)
                high(norm2, f, t, 1)
                if t == 0:
                    count = square(norm2, count, f, t)
                if f == KT - 1:
                    act.dma_start(h_spill[:, :, tok(t)], h[:, :, tok(t)]).then_inc(h_saved, 16)
            root(norm2, 0)
            for f in range(KT):
                count = square(norm2, count, f, 1)
            root(norm2, 1)
            act.wait_ge(h_saved, 32)
            branch(ret_s, N_RET, False)
            for f in range(KT):
                for t in range(2):
                    act.wait_ge(ga_sc, 2 * f + t + 1)
                    A(vS[:, t, :], vS[:, t, :], ACT.Sigmoid).then_inc(ga_sig, 1)
                if f >= 1:
                    act.wait_ge(ga_ev, 2 * f)
                    act.dma_start(y_spill[:, f - 1, :], y[:, f - 1, :]).then_inc(y_saved, 16)
                if f == 3:
                    soft_part(0)
            act.wait_ge(ga_ev, 2 * KT)
            act.dma_start(y_spill[:, KT - 1, :], y[:, KT - 1, :]).then_inc(y_saved, 16)
            branch(gla_s, N_GLA, True)
            yr = vtok[:].rearrange("p b c -> p (b c)").rearrange("p (s t) -> p s t", s=2)
            act.wait_ge(y_saved, 16 * KT)
            for f in range(2):
                act.dma_start(yr[:, f, :], y_spill[:, f, :]).then_inc(y_back[f], 16)
            act.wait_ge(w_used, N_GB + 1)
            for f in range(KT):
                act.dma_start(h[:, f, :], h_spill[:, f, :]).then_inc(h_in[f], 16)

            def merged_high(t):
                for f in range(KT):
                    act.wait_ge(gb_ev, PLACE[f, t] + 1)
                    A(uH[:, f, tok(t)], y[:, f, tok(t)], ACT.Copy).then_inc(mh_done, 1)

            for idx, (f, t) in enumerate(PAIRED):
                act.wait_ge(gb_sc, idx + 1)
                A(vS[:, idx % 2, :], vS[:, idx % 2, :], ACT.Sigmoid).then_inc(gb_sig, 1)
                if idx % 2 == 0 and 1 <= idx // 2 < KT - 1:
                    i = idx // 2
                    act.wait_ge(gb_ev, 2 * i)
                    act.dma_start(yr[:, (i + 1) % 2, :], y_spill[:, i + 1, :]
                                  ).then_inc(y_back[(i + 1) % 2], 16)
                if (f, t) == (KT - 1, 0):
                    act.wait_ge(cols_half, CH_GB + KT)
                    merged_high(0)
            act.wait_ge(w_used, N_GB + KT)
            merged_high(1)
            count = 0
            for idx, (f, t) in enumerate(PAIRED):
                act.wait_ge(wo_ev, idx + 1)
                count = square(norm3, count, f, t)
                if (f, t) == (KT - 1, 0):
                    act.wait_ge(cols_half, CH_OUT + KT)
                    for g in range(KT):
                        high(norm3, g, 0, 2)
            act.wait_ge(w_used, N_F2)
            for f in range(KT):
                high(norm3, f, 1, 2)
            roots(norm3)
            ffn(f2, N_F2)
            A(warm[:, 2:3], one[:], ACT.Sqrt)
            count = 0
            for v in range(16):
                _, t, f, _, _ = last_unit(v)
                act.wait_ge(f2.acc_done, 16 * (FFG - 1) + v + 1)
                if t == 0 or f == 0:
                    count = square(norm4, count, f, t)
                else:
                    if f in (1, 2):
                        act.wait_ge(norm4.sum_done, KT - 2 + f - 1)
                    elif f == KT - 1:
                        act.wait_ge(norm4.sum_done, KT)
                    else:
                        act.wait_ge(f2.hl_done, 4 * FFG)
                    A(last_square(f), h[:, f, tok(t)], ACT.Square).then_inc(norm4.sq_done, 1)
                if v == 9:
                    root(norm4, 0)
            root(norm4, 1)
            for i in range(2 * len(POOL_LAST)):
                t, f = i // len(POOL_LAST), POOL_LAST[i % len(POOL_LAST)]
                act.wait_ge(y_over_rms, i + 1)
                A(h[:, f, tok(t)], h[:, f, tok(t)], ACT.Copy,
                  scale=normw[:, 3 * KT + f:3 * KT + f + 1]).then_inc(y_act_done, 1)
                act.wait_ge(y_act_done, i + 1)
                act.dma_start(out[:, f, tok(t)], h[:, f, tok(t)]).then_inc(out_saved, 16)
            act.wait_ge(out_saved, 16 * 2 * KT)

        @block.vector
        def _(dve):
            V = nc.vector

            def low(nm, count, f, t, wcol):
                dve.wait_ge(nm.uh_done, count + 1)
                V.scalar_tensor_tensor(out=uL[:, f, tok(t)], in0=h[:, f, tok(t)],
                                       scalar=normw[:, wcol * KT + f:wcol * KT + f + 1],
                                       in1=uH[:, f, tok(t)].bitcast(F32), op0=ALU.mult,
                                       op1=ALU.subtract).then_inc(nm.ul_done, 1)

            def add_square(nm, nth, count, f, t):
                if f == 0:
                    return count
                dve.wait_ge(nm.sq_done, nth + 1)
                wait(dve, nm.sum_done, count)
                V.tensor_tensor(ssum[:, t, :], ssum[:, t, :], sq[:, count % 2, :], ALU.add
                                ).then_inc(nm.sum_done, 1)
                return count + 1

            def inverse(nm, t):
                dve.wait_ge(nm.root_done, t + 1)
                V.reciprocal(rinv[:, t, :], rinv[:, t, :]).then_inc(nm.inv_done, 1)
                dve.wait_ge(nm.inv_done, t + 1)

            def inverses(nm):
                for t in range(2):
                    inverse(nm, t)

            def scaled(out_, bank, t, scale=None, parts=P):
                r = rinv[0:parts, t, :]
                if scale is None:
                    return V.tensor_tensor(out_, ps[0:parts, bank, :], r, ALU.mult)
                return V.scalar_tensor_tensor(out=out_, in0=ps[0:parts, bank, :], scalar=scale, in1=r,
                                              op0=ALU.mult, op1=ALU.mult)

            def ffn(s, n0, nm, wcol):
                def p1(i, par, first=False):
                    for j in range(2):
                        n = n0 + 2 * j + 1 if first else n0 + 4 + 6 * (i - 1) + 2 * j + 1
                        for t in range(2):
                            idx = 4 * i + 2 * j + t
                            if t == 0:
                                dve.wait_ge(s.a_done, 2 * i + j + 1)
                            else:
                                dve.wait_ge(w_used, n)
                            wait(dve, s.gate_done, idx - 1)
                            scaled(sil[:, t, :], 4 * j + t, t).then_inc(s.as_done, 1)
                        for t in range(2):
                            idx = 4 * i + 2 * j + t
                            dve.wait_ge(s.silu_done, idx + 1)
                            V.tensor_tensor(sil[:, t, :], sil[:, t, :], rinv[:, t, :], ALU.mult
                                            ).then_inc(s.sr_done, 1)
                        for t in range(2):
                            idx = 4 * i + 2 * j + t
                            if t == 0:
                                dve.wait_ge(s.b_done, 2 * i + j + 1)
                            else:
                                dve.wait_ge(w_used, n + 1)
                            dve.wait_ge(s.sr_done, idx + 1)
                            wait(dve, s.hl_done, idx - 1)
                            V.tensor_tensor(hidf[:, t, :], sil[:, t, :], ps[:, 4 * j + 2 + t, :],
                                            ALU.mult).then_inc(s.gate_done, 1)
                            dve.wait_ge(s.hh_done, idx + 1)
                            V.tensor_tensor(hidL[:, par, j, tok(t)], hidf[:, t, :],
                                            hidH[:, par, j, tok(t)].bitcast(F32), ALU.subtract
                                            ).then_inc(s.hl_done, 1)

                def p2(g, n):
                    for v in range(16):
                        c, t, fl = v // 8, v % 8 // 4, v % 4
                        f = 4 * c + fl
                        if v % 8 == 7:
                            dve.wait_ge(w_used, n + c + 1)
                        else:
                            dve.wait_ge(s.p2_done, 14 * g + 7 * c + v % 8 + 1)
                        wait(dve, s.acc_done, 16 * (g - 1) + v + 1)
                        V.scalar_tensor_tensor(out=h[:, f, tok(t)], in0=ps[:, v % 8, :], scalar=0.5,
                                               in1=h[:, f, tok(t)], op0=ALU.mult, op1=ALU.add
                                               ).then_inc(s.acc_done, 1)

                p1(0, 0, first=True)
                p1(1, 1)
                p2(0, n0 + 8)
                with dve.Fori(1, FFG // 2) as c:
                    for par in range(2):
                        i = c * 2 + par
                        p1(i, par)
                        p2(i - 1, n0 + 8 + 6 * (i - 1))
                i = FFG - 1
                p1(i, i % 2)
                p2(i - 1, n0 + 8 + 6 * (i - 1))
                n = n0 + 8 + 6 * (i - 1) + 2
                count = 0
                for v in range(16 + 1):
                    if v < 16:
                        c, t, f, bank, through = last_unit(v)
                        if v in (11, 15):
                            dve.wait_ge(w_used, n + c + 1)
                        else:
                            dve.wait_ge(s.p2_done, 14 * i + v + 1 - through)
                        dve.wait_ge(s.acc_done, 16 * (i - 1) + 16)
                        V.scalar_tensor_tensor(out=h[:, f, tok(t)], in0=ps[:, bank, :], scalar=0.5,
                                               in1=h[:, f, tok(t)], op0=ALU.mult, op1=ALU.add
                                               ).then_inc(s.acc_done, 1)
                    if v > 0:
                        _, t, f, _, _ = last_unit(v - 1)
                        if wcol is not None:
                            low(nm, v - 1, f, t, wcol)
                        if t == 0:
                            count = add_square(nm, v - 1, count, f, t)
                        elif wcol is None and f == DVE_ADD:
                            dve.wait_ge(nm.sq_done, v)
                            dve.wait_ge(nm.sum_done, KT - 1 + f - 1)
                            V.tensor_tensor(ssum[:, 1, :], ssum[:, 1, :], last_square(f), ALU.add
                                            ).then_inc(nm.sum_done, 1)
                    if wcol is None and v == INV_AT:
                        inverse(nm, 0)
                if wcol is not None:
                    inverse(nm, 0)
                    for f in range(KT):
                        count = add_square(nm, KT + f, count, f, 1)

            def gate(s, hp, half, gla):
                for d in range(2):
                    idx = 4 * hp + 2 * half + d
                    dve.wait_ge(s.ot_done, idx + 1)
                    dve.wait_ge(s.r_ev, 4 * hp + 4)
                    if half:
                        dve.wait_ge(s.ol_done, idx - 1)
                    o = ogf[:, d, :]
                    if gla:
                        V.scalar_tensor_tensor(out=o, in0=ps[:, 6 + d, :],
                                               scalar=normw[:, 4 * KT + d:4 * KT + d + 1],
                                               in1=rS[:, d, tok(half)], op0=ALU.mult, op1=ALU.mult
                                               ).then_inc(s.g_done, 1)
                    else:
                        V.tensor_tensor(o, ps[:, 6 + d, :], rS[:, d, tok(half)], ALU.mult
                                        ).then_inc(s.g_done, 1)
                for d in range(2):
                    idx = 4 * hp + 2 * half + d
                    dve.wait_ge(s.oh_done, idx + 1)
                    V.tensor_tensor(ogL[:, d, tok(half)], ogf[:, d, :],
                                    ogH[:, d, tok(half)].bitcast(F32), ALU.subtract
                                    ).then_inc(s.ol_done, 1)

            def branch_add(s, hp, v, n_tile, n_before):
                c, t, fl = v // 8, v % 8 // 4, v % 4
                f = 4 * c + fl
                if v % 8 == 7:
                    dve.wait_ge(w_used, n_tile + 1)
                else:
                    dve.wait_ge(s.b_part, 14 * hp + 7 * c + v % 8 + 1)
                if v == 0:
                    dve.wait_ge(w_used, n_before)
                V.tensor_tensor(y[:, f, tok(t)], ps[:, v % 4, :], y[:, f, tok(t)], ALU.add
                                ).then_inc(s.b_ev, 1)

            def start_head(s, hd, gla, link):
                wait(dve, s.kt_ev, 2 * hd)
                wait(dve, s.st_ev, 7 * hd)
                if gla:
                    wait(dve, zmin_done, 2 * hd)
                    wait(dve, z_done, 2 * hd)
                    wait(dve, zabs_done, 2 * hd)
                    link(V.tensor_copy(w2s[:], w2t[:, bass.ds(hd * DK, DK)]))
                    low_rows = slice(4 * RANK, 6 * RANK)
                    V.tensor_tensor(w2s[low_rows, :], w2t[low_rows, bass.ds(hd * DK, DK)],
                                    w2s[low_rows, :].bitcast(F32), ALU.subtract)
                    V.tensor_copy(headc[:, 2:3], gbt[:, bass.ds(hd, 1)]).then_inc(s.headc_done, 1)
                else:
                    V.tensor_copy(headc[:, 0:2], rett[:, bass.ds(hd, 1), 2 * BLK:RETC]
                                  .rearrange("p a c -> p (a c)")).then_inc(s.headc_done, 1)
                wait(dve, s.o_done, 8 * hd)
                link(V.memset(state[:, 0, :], 0.0))
                dve.wait_ge(s.headc_done, hd + 1)

            def log_decays(hd, link):
                for t in range(2):
                    dve.wait_ge(zabs_done, 2 * hd + t + 1)
                    wait(dve, exp_done, 2 * (NLV + 2) * hd)
                    wait(dve, diff_done, 2 * (NLV + 1) * hd)
                    V.tensor_scalar(bc[:, tok(t)], ps[:, 4 + t, :], headc[:, 2:3], 0.0,
                                    ALU.add, ALU.min).then_inc(zmin_done, 1)
                for t in range(2):
                    dve.wait_ge(zln_done, 2 * hd + t + 1)
                    dve.wait_ge(zmin_done, 2 * hd + t + 1)
                    link(V.tensor_tensor(ee[:, t, :], bc[:, tok(t)], ee[:, t, :], ALU.subtract))
                for b in range(2 * NBH):
                    ins = V.tensor_tensor_scan(bc[:, b * BLK:(b + 1) * BLK], ones,
                                               ee[:, b // NBH, b % NBH * BLK:(b % NBH + 1) * BLK],
                                               0.0, ALU.mult, ALU.add)
                ins.then_inc(cum_done, 1)
                dve.wait_ge(cum_done, hd + 1)

            ONCE_MASKS, ONCE_ROPE, ONCE_CLEAR = 1, (2, 3), (4, 5)
            EARLY_LINKS = 4

            def early_link(count):
                def link(ins):
                    count[0] += 1
                    ins.then_inc(gla_s.chain, 1)
                    dve.wait_ge(gla_s.chain, count[0])
                return link

            def branch(s, n0, gla):
                n_sc = NLV + 1 if gla else 1
                per_window = 1 + 2 * NBH + (2 * 3 + 3 if gla else 2 * 2 + 4)

                def window(hd, first):
                    nw = n0 if first else n0 + 6 + 8 * (hd - 1)
                    base = 0 if first else per_window * hd
                    count = [0]

                    def link(ins):
                        count[0] += 1
                        ins.then_inc(s.chain, 1)
                        dve.wait_ge(s.chain, base + count[0])

                    if first and gla:
                        count[0] = EARLY_LINKS
                    for step in range(STEPS + 1):
                        if step == 0 and not (gla and first):
                            start_head(s, hd, gla, link)
                        clear_steps = (5, 6, 7, 9, 10, 11, 13, 14) if gla else \
                            (25, 27, 29, 30, 31, 33, 34, 35)
                        if first and step in clear_steps:
                            f = clear_steps.index(step)
                            if gla and f == 0:
                                dve.wait_ge(y_saved, 16 * KT)
                            ins = V.memset(y[:, f, :], 0.0)
                            if f == KT - 1:
                                ins.then_inc(once_done, 1)
                                dve.wait_ge(once_done, ONCE_CLEAR[gla])
                        if first and not gla and step in (0, 5):
                            t = int(step > 0)
                            if t:
                                inverse(norm2, 1)
                            for part in range(2):
                                x = ropet[:, part, tok(t)]
                                ins = V.tensor_tensor(x, x, rinv[:, t, :], ALU.mult)
                            ins.then_inc(once_done, 1)
                            dve.wait_ge(once_done, ONCE_ROPE[t])
                        if gla and step == 2 and not first:
                            log_decays(hd, link)
                        if step in (3, 11) and not first:
                            gate(s, hd - 1, step // 8, gla)
                        if gla and step in (4, 8, 12, 16):
                            t = 0 if step in (4, 12) else 1
                            isk = step >= 12
                            if t == 0:
                                dve.wait_ge(s.half_done, 6 * hd + (2 if isk else 1))
                            else:
                                dve.wait_ge(w_used, nw + (K if isk else Q) + 1)
                            if not isk:
                                wait(dve, s.o_done, 8 * hd)
                                scaled(qT[:, tok(t)], t, t, QK_SCALE).then_inc(s.q_ev, 1)
                            else:
                                scaled(kT[:, tok(t)], 2 + t, t).then_inc(s.k_ev, 1)
                        if step in (20, 24, 28, 32):
                            v = (step - 20) // 4
                            if v % 2 == 0:
                                dve.wait_ge(s.half_done, 6 * hd + 3 + v // 2)
                            else:
                                dve.wait_ge(w_used, nw + V0 + v // 2 + 1)
                            wait(dve, s.vt_done, 4 * hd + v - 1)
                            wait(dve, s.ol_done, 4 * hd)
                            scaled(vS[:, v % 2, :], v, v % 2).then_inc(s.v_ev, 1)
                        if step in (52, 56, 60, 64):
                            v = (step - 52) // 4
                            if v % 2 == 0:
                                dve.wait_ge(s.half_done, 6 * hd + 5 + v // 2)
                            else:
                                dve.wait_ge(w_used, nw + R0 + v // 2 + 1 - (2 if first else 0))
                            wait(dve, s.g_done, 4 * hd)
                            scaled(rS[:, v // 2, tok(v % 2)], v, v % 2).then_inc(s.r_sc, 1)
                        if not gla and step in (4, 8, 12, 16):
                            t = step // 4 % 2
                            t = 0 if step in (4, 12) else 1
                            isk = step >= 12
                            if t == 0:
                                dve.wait_ge(s.half_done, 6 * hd + (2 if isk else 1))
                            else:
                                dve.wait_ge(w_used, nw + (K if isk else Q) + 1)
                            if not isk:
                                wait(dve, s.o_done, 8 * hd)
                                wait(dve, s.qd_done, 2 * hd)
                            wait(dve, s.q_ev if step in (8, 12) else s.k_ev,
                                 2 * hd + {4: 0, 8: 1, 12: 2, 16: 1}[step])
                            x = ps[:, (2 if isk else 0) + t, :]
                            cos, sin = ropet[:, 0, tok(t)], ropet[:, 1, tok(t)]
                            V.tensor_tensor(rtmp[0:64, 0, :], x[64:128], sin[64:128], ALU.mult)
                            V.tensor_tensor(rtmp[64:128, 0, :], x[0:64], sin[0:64], ALU.mult)
                            link(V.tensor_tensor(rtmp[:, 1, :], x, cos, ALU.mult))
                            V.tensor_tensor((kT if isk else qT)[:, tok(t)], rtmp[:, 0, :],
                                            rtmp[:, 1, :], ALU.add
                                            ).then_inc(s.k_ev if isk else s.q_ev, 1)
                        for half in range(2):
                            for item in range(NLV + 2):
                                if step == score_step(half, item) - 2:
                                    if gla:
                                        gla_item(hd, half, item, link)
                                if step == score_step(half, item) + 1 and item == DIAG:
                                    if gla:
                                        score_in(hd, half, DIAG, link)
                                    else:
                                        ret_item(hd, half, link)
                            for b in range(NBH):
                                if step == block_step(half, b) + 1:
                                    block_in(hd, half * NBH + b, link)
                            if step == NORM_STEPS[half]:
                                half_variance(hd, half, link)
                            if step == NORM_STEPS[half] + 2:
                                half_norm(hd, half, link)
                        if not first and 1 + 8 * B0 <= step < 1 + 8 * R0:
                            v = step - 1 - 8 * B0
                            branch_add(s, hd - 1, v, nw + B0 + v // 8, nw)
                    assert count[0] == per_window, (count[0], per_window)

                def ret_item(hd, half, link):
                    dve.wait_ge(s.sc_done, 2 * hd + half + 1)
                    wait(dve, s.o_done, 8 * hd)
                    pb = ps[:, 4 + (half * (NLV + 2) + DIAG) % 2, :].rearrange("p (b n) -> p b n", b=NBH)
                    for b in range(NBH):
                        last = V.tensor_tensor(ss[:, half, b, :], pb[:, b, :],
                                               rett[:, bass.ds(hd, 1), 0:BLK].rearrange("p a n -> p (a n)"),
                                               ALU.mult)
                    last.then_inc(s.sc_ev, 1)
                    wait(dve, s.o_done, 8 * hd + 4 * half)
                    dve.wait_ge(s.q_ev, 2 * hd + half + 1)
                    for b in range(NBH):
                        last = V.tensor_tensor(qd[:, b, :],
                                               qT[:, half * HF + b * BLK:half * HF + (b + 1) * BLK],
                                               rett[:, bass.ds(hd, 1), BLK:2 * BLK].rearrange("p a n -> p (a n)"),
                                               ALU.mult)
                    last.then_inc(s.qd_done, 1)

                def gla_item(hd, half, item, link):
                    if item == 0:
                        difference(hd, half, 0)
                    if item + 1 <= LAST:
                        difference(hd, half, item + 1)
                    g = half * (NLV + 2) + item
                    n = 2 * (NLV + 2) * hd + g
                    e = ee[:, g % 2, :]
                    dve.wait_ge(exp_done, n + 1)
                    dve.wait_ge(s.q_ev, 2 * hd + half + 1)
                    dve.wait_ge(s.k_ev, 2 * hd + half + 1)
                    q, k = qT[:, tok(half)], kT[:, tok(half)]
                    if item <= LAST:
                        if item == 0:
                            wait(dve, s.kt_done, 2 * hd + half)
                            wait(dve, s.sc_done, 2 * n_sc * hd + n_sc * half)
                        elif item >= 2:
                            dve.wait_ge(s.sc_done, 2 * n_sc * hd + n_sc * half + item - 1)
                    if item == 0:
                        qe, ke, q3, k3, e3 = (x.rearrange("p (b n) -> p b n", b=NBH) for x in
                                              (qE[:, 0, :], kE[:, 0, :], q, k, e))
                        V.tensor_tensor(qe[:, :, CHUNK:], q3[:, :, CHUNK:], e3[:, :, CHUNK:], ALU.mult)
                        V.tensor_tensor(ke[:, :, :CHUNK], k3[:, :, :CHUNK], e3[:, :, :CHUNK],
                                        ALU.mult).then_inc(prod_done, 1)
                    elif item < NLV:
                        V.tensor_tensor(qE[:, item % 2, :], q, e, ALU.mult)
                        V.tensor_tensor(kE[:, item % 2, :], k, e, ALU.mult).then_inc(prod_done, 1)
                    elif item == LAST:
                        V.tensor_tensor(kE[:, item % 2, :], k, e, ALU.mult).then_inc(prod_done, 1)
                    else:
                        wait(dve, s.o_done, 8 * hd + 4 * half)
                        V.tensor_copy(bdec[:, half, :],
                                      e.rearrange("p (b n) -> p b n", b=NBH)[:, :, BLK - 1])
                        V.tensor_tensor(qd[:].rearrange("p b n -> p (b n)"), q, e, ALU.mult
                                        ).then_inc(prod_done, 1)
                        dve.wait_ge(prod_done, n + 1)
                    if 1 <= item <= NLV:
                        score_in(hd, half, item - 1, link)

                def difference(hd, half, item):
                    g = half * (NLV + 2) + item
                    wait(dve, prod_done, 2 * (NLV + 2) * hd + g - 1)
                    w = LEVELS[item] if item < NLV else BLK
                    n = 2 * w if item < NLV else BLK
                    b3 = bc[:, tok(half)].rearrange("p (n s) -> p n s", s=n)
                    ref = b3[:, :, w - 1:w].to_broadcast([P, HF // n, n])
                    V.tensor_tensor(ee[:, g % 2, :].rearrange("p (n s) -> p n s", s=n), b3, ref,
                                    ALU.subtract).then_inc(diff_done, 1)

                def score_in(hd, half, item, link):
                    sc = 2 * n_sc * hd + n_sc * half
                    order = item if item < NLV else NLV
                    dve.wait_ge(s.sc_done, sc + order + 1)
                    g = half * (NLV + 2) + item
                    pb = ps[:, 4 + g % 2, :].rearrange("p (b n) -> p b n", b=NBH)
                    o = ss[:, half]
                    if item == 0:
                        wait(dve, s.o_done, 8 * hd)
                        V.memset(o[0:CHUNK, :, :CHUNK], 0.0)
                        V.memset(o[CHUNK:, :, :], 0.0)
                        V.tensor_copy(o[0:CHUNK, :, CHUNK:], pb[0:CHUNK, :, CHUNK:]
                                      ).then_inc(s.sc_ev, 1)
                    else:
                        dve.wait_ge(s.sc_ev, sc + order)
                        mi = maskt[:, order - 1:order, :].to_broadcast([P, NBH, BLK])
                        carry()
                        V.copy_predicated(o, mi, pb).then_inc(s.sc_ev, 1)
                    if item == DIAG:
                        dve.wait_ge(prod_done, 2 * (NLV + 2) * hd + half * (NLV + 2) + NLV + 2)

                def block_in(hd, b, link):
                    half, bb = b // NBH, b % NBH
                    if gla and bb == 0:
                        dve.wait_ge(prod_done, (NLV + 2) * (2 * hd + half + 1))
                    if b < 2 * NBH - 1:
                        dve.wait_ge(s.st_done, 7 * hd + b + 1)
                        if b >= 1:
                            dve.wait_ge(s.st_ev, 7 * hd + b)
                        dve.wait_ge(s.o_done, 8 * hd + b + 1)
                        dec = bdec[:, half, bb:bb + 1] if gla else headc[:, 1:2]
                        V.scalar_tensor_tensor(out=state[:, (b + 1) % 2, :], in0=state[:, b % 2, :],
                                               scalar=dec,
                                               in1=ps[:, 7, b % 2 * DV:(b % 2 + 1) * DV],
                                               op0=ALU.mult, op1=ALU.add).then_inc(s.st_ev, 1)
                    dve.wait_ge(s.o_ev, 8 * hd + b + 1)
                    link(V.bn_stats(bst[:, bb, :], on[:, b, :]))

                def half_variance(hd, half, link):
                    wait(dve, s.on_done, 2 * hd + half)
                    carry(1)
                    for b in range(NBH):
                        ins = V.bn_aggr(mv[:, b, :], bst[:, b, :])
                    link(ins)
                    if gla:
                        link(V.tensor_tensor(ve[:], mv[:, :, 0], mv[:, :, 0], ALU.mult))
                        V.scalar_tensor_tensor(out=ve[:], in0=ve[:], scalar=EPS, in1=mv[:, :, 1],
                                               op0=ALU.add, op1=ALU.add).then_inc(s.var_done, 1)
                    else:
                        V.tensor_scalar(ve[:], mv[:, :, 1], EPS, None, ALU.add).then_inc(s.var_done, 1)

                def half_norm(hd, half, link):
                    dve.wait_ge(s.sd_done, 2 * hd + half + 1)
                    link(V.reciprocal(rs[:], sd[:]))
                    for b in range(NBH):
                        o = on[:, half * NBH + b, :]
                        if gla:
                            ins = V.tensor_scalar(o, o, rs[:, b:b + 1], None, ALU.mult)
                        else:
                            ins = V.tensor_scalar(o, o, mv[:, b, 0:1], rs[:, b:b + 1], ALU.subtract,
                                                  ALU.mult)
                    ins.then_inc(s.on_done, 1)

                window(0, True)
                with dve.Fori(1, HEADS) as hd:
                    window(hd, False)
                hp = HEADS - 1
                for half in range(2):
                    gate(s, hp, half, gla)
                nb = n0 + BRANCH_TILES - 1
                for v in range(16):
                    branch_add(s, hp, v, nb + v // 8, nb)

            dve.wait_ge(raw_in[0], 16)
            V.tensor_copy(wH[0][:], raw[0][:]).then_inc(w_high, 1)
            dve.wait_ge(w_high, 1)
            V.tensor_tensor(wL[0][:], raw[0][:], wH[0][:].bitcast(F32), ALU.subtract
                            ).then_inc(w_ready, 1)
            dve.wait_ge(normw_in, 16)
            for t in range(2):
                for f in range(KT):
                    low(norm1, KT * t + f, f, t, 0)
            count = 0
            for t in range(2):
                for f in range(KT):
                    count = add_square(norm1, KT * t + f, count, f, t)
            dve.wait_ge(const_in, 16)
            dve.wait_ge(late_in, 16 * 5)
            V.tensor_copy(maskt[:].rearrange("p s n -> p (s n)"), maskf[:].rearrange("p s n -> p (s n)")
                          ).then_inc(once_done, 1)
            inverses(norm1)
            dve.wait_ge(once_done, ONCE_MASKS)
            ffn(f1, N_F1, norm2, 1)

            branch(ret_s, N_RET, False)
            dve.wait_ge(w_ready, N_LR + 1)
            for i, part in enumerate((wH[N_LR % 2], wL[N_LR % 2])):
                ins = V.tensor_copy(lrw[:, :, i * RANK:(i + 1) * RANK],
                                    part[:].rearrange("p (k c) -> p k c", k=KT)[:, :, 0:RANK])
            ins.then_inc(lrw_done, 1)
            for t in range(2):
                if t == 0:
                    dve.wait_ge(cols_half, CH_LR)
                else:
                    dve.wait_ge(w_used, N_LR + 1)
                whole = qE[0:2 * RANK, t, :]
                scaled(whole, t, t, parts=2 * RANK).then_inc(lr_part, 1)
                dve.wait_ge(lr_part, 2 * t + 1)
                V.tensor_copy(lrT[0:2 * RANK, tok(t)], whole)
                V.tensor_copy(lrT[4 * RANK:6 * RANK, tok(t)], whole).then_inc(lr_part, 1)
                dve.wait_ge(lr_part, 2 * t + 2)
                V.tensor_tensor(lrT[2 * RANK:4 * RANK, tok(t)], whole,
                                lrT[0:2 * RANK, tok(t)].bitcast(F32), ALU.subtract).then_inc(lr_ev, 1)

            def gate_scaled(n, idx, bank, t, halves, ev, sc_done):
                if t == 0:
                    dve.wait_ge(cols_half, halves)
                else:
                    dve.wait_ge(w_used, n + 1)
                wait(dve, ev, idx - 1)
                scaled(vS[:, idx % 2, :], bank, t).then_inc(sc_done, 1)

            for f in range(KT):
                for t in range(2):
                    idx = 2 * f + t
                    gate_scaled(N_GA + f if f else N_GA0, idx, 2 * (f % 2) + t if f else 4 + t, t,
                                CH_LR + f if f else CH_GA, ga_ev, ga_sc)
                    dve.wait_ge(ga_sig, idx + 1)
                    if idx == 0:
                        dve.wait_ge(ret_s.b_ev, 16 * HEADS)
                    V.tensor_tensor(y[:, f, tok(t)], y[:, f, tok(t)], vS[:, t, :], ALU.mult
                                    ).then_inc(ga_ev, 1)
                if f in (2, 3):
                    link = early_link([0 if f == 2 else 2])
                    if f == 2:
                        start_head(gla_s, 0, True, link)
                    else:
                        log_decays(0, link)
            branch(gla_s, N_GLA, True)
            yr = vtok[:].rearrange("p b c -> p (b c)").rearrange("p (s t) -> p s t", s=2)

            def merged_low(t):
                for f in range(KT):
                    dve.wait_ge(mh_done, KT * t + f + 1)
                    V.tensor_tensor(uL[:, f, tok(t)], y[:, f, tok(t)], uH[:, f, tok(t)].bitcast(F32),
                                    ALU.subtract).then_inc(ml_done, 1)

            for idx, (f, t) in enumerate(PAIRED):
                gate_scaled(N_GB + f if f else N_GB0, idx, 2 * (f % 2) + t if f else 4 + t, t,
                            CH_GB + f + 1, gb_ev, gb_sc)
                dve.wait_ge(gb_sig, idx + 1)
                if idx == 0:
                    dve.wait_ge(gla_s.b_ev, 16 * HEADS)
                if t == 0:
                    dve.wait_ge(y_back[f % 2], 16 * (f // 2 + 1))
                V.tensor_tensor(vS[:, idx % 2, :], y[:, f, tok(t)], vS[:, idx % 2, :], ALU.mult
                                ).then_inc(gb_mul, 1)
                dve.wait_ge(gb_mul, idx + 1)
                V.tensor_tensor(y[:, f, tok(t)], vS[:, idx % 2, :], yr[:, f % 2, tok(t)], ALU.add
                                ).then_inc(gb_ev, 1)
                if (f, t) == (KT - 1, 0):
                    merged_low(0)
            merged_low(1)
            count = 0
            for idx, (f, t) in enumerate(PAIRED):
                if t == 0:
                    dve.wait_ge(cols_half, CH_OUT + f + 1)
                    dve.wait_ge(h_in[f], 32)
                else:
                    dve.wait_ge(w_used, N_OUT + f + 1)
                V.tensor_tensor(h[:, f, tok(t)], ps[:, 2 * (f % 2) + t, :], h[:, f, tok(t)],
                                ALU.add).then_inc(wo_ev, 1)
                count = add_square(norm3, idx, count, f, t)
                if (f, t) == (KT - 1, 0):
                    for g in range(KT):
                        low(norm3, g, g, 0, 2)
            for f in range(KT):
                low(norm3, KT + f, f, 1, 2)
            inverses(norm3)
            ffn(f2, N_F2, norm4, None)
            for t in range(2):
                for f in range(POOL_LAST[0]):
                    if (t, f) == (0, 3):
                        inverse(norm4, 1)
                    V.scalar_tensor_tensor(out=h[:, f, tok(t)], in0=h[:, f, tok(t)],
                                           scalar=normw[:, 3 * KT + f:3 * KT + f + 1],
                                           in1=rinv[:, t, :], op0=ALU.mult, op1=ALU.mult
                                           ).then_inc(y_dve_done, 1)


def cols_tiles(w):
    kt, n = w.shape[0] // P, w.shape[1] // P
    return np.ascontiguousarray(w.reshape(kt, P, n, P).transpose(2, 1, 0, 3)).reshape(n, P, kt * P)


def rows_tiles(w):
    g = w.shape[0] // (2 * P)
    return np.ascontiguousarray(w.reshape(g, 2, P, 2, 4 * P).transpose(0, 3, 2, 1, 4)
                                ).reshape(2 * g, P, D)


def ffn_stream(w1, w3, w2):
    a, b, c = cols_tiles(w1), cols_tiles(w3), rows_tiles(w2)
    tiles = []
    for g in range(FFG):
        tiles += [a[2 * g], b[2 * g], a[2 * g + 1], b[2 * g + 1]]
        if g:
            tiles += [c[2 * g - 2], c[2 * g - 1]]
    return tiles + [c[2 * FFG - 2], c[2 * FFG - 1]]


def branch_stream(q, k, v, r, wb, mid):
    b = rows_tiles(wb)
    q, k, v, r = (cols_tiles(x) for x in (q, k, v, r))
    tiles = []
    for hd in range(HEADS):
        tiles += [q[hd], k[hd], v[2 * hd], v[2 * hd + 1]]
        if hd:
            tiles += [b[2 * hd - 2], b[2 * hd - 1]]
        tiles += [r[2 * hd], r[2 * hd + 1]]
    return tiles + [mid, b[2 * HEADS - 2], b[2 * HEADS - 1]]


def kernel(x, norm_ffn1, ffn1_w1, ffn1_w3, ffn1_w2, norm_mix, w_in, gla_gate_w2, gla_gate_b,
           gla_norm_w, w_branch_ret, w_branch_gla, w_out, norm_ffn2, ffn2_w1, ffn2_w3, ffn2_w2,
           norm_final):
    import concourse.bacc as bacc
    from concourse.bass_utils import run_bass_kernel_spmd

    A = np.asarray
    w_in = A(w_in)[0]
    widths = (512, 512, 1024, 1024, 512, 512, 1024, 1024, 16, 1024, 1024)
    at = np.cumsum((0,) + widths)
    qa, ka, va, ra, qb, kb, vb, rb, lr, ga, gb = (w_in[:, a:b] for a, b in zip(at[:-1], at[1:]))
    lr = np.concatenate([lr, np.zeros((D, P - lr.shape[1]), lr.dtype)], 1)
    tiles = ffn_stream(A(ffn1_w1)[0], A(ffn1_w3)[0], A(ffn1_w2)[0])
    ga = cols_tiles(ga)
    tiles += branch_stream(qa, ka, va, ra, A(w_branch_ret)[0], ga[0])
    tiles += list(cols_tiles(lr)) + list(ga[1:])
    gb = cols_tiles(gb)
    tiles += branch_stream(qb, kb, vb, rb, A(w_branch_gla)[0], gb[0])
    tiles += list(gb[1:]) + list(cols_tiles(A(w_out)[0]))
    tiles += ffn_stream(A(ffn2_w1)[0], A(ffn2_w3)[0], A(ffn2_w2)[0])
    assert len(tiles) == N_TILES

    def columns(v):
        return A(v).reshape(-1, P).T

    rope, ret, masks, small = decay_tables()
    arrays = {
        "xT": np.ascontiguousarray(A(x)[0].T.reshape(KT, P, T).transpose(1, 0, 2)),
        "wts": np.stack(tiles),
        "norms": np.ascontiguousarray(np.concatenate(
            [columns(v) for v in (norm_ffn1, norm_mix, norm_ffn2, norm_final, gla_norm_w)], 1)),
        "gate_w2": np.concatenate([A(gla_gate_w2)[0]] * 6),
        "gate_b": np.ascontiguousarray(columns(gla_gate_b)),
        "rope": rope,
        "ret": ret,
        "masks": masks,
        "small": small,
    }
    nc = bacc.Bacc("TRN2", target_bir_lowering=False, num_devices=1, dynamic_dma_scratch_size=1024)
    aps = [nc.dram_tensor(n, a.shape, mybir.dt.from_np(a.dtype), kind="ExternalInput").ap()
           for n, a in arrays.items()]
    out = nc.dram_tensor("yT", (P, KT, T), F32, kind="ExternalOutput").ap()
    spill = [nc.dram_tensor(n, (P, KT, T), F32, kind="Internal").ap() for n in ("h_spill", "y_spill")]
    block_kernel(nc, *aps, out, *spill)
    r = run_bass_kernel_spmd(nc, [arrays], core_ids=[0])
    got = r.results[0]["yT"]
    return np.ascontiguousarray(got.transpose(1, 0, 2)).reshape(D, T).T[None]
```
